# Optimizing a Trainium2 kernel written in Bass

```python
import jax, jax.numpy as jnp
from jax import lax
import numpy as np

D_MODEL = 1024
BATCH = 1
SEQ = 512
DEPTH = 1
DEC_BATCH = 8
DEC_SEQ = 4
PAST_LEN = 2048
PAGE_SIZE = 128

NSA_HEADS = 8
NSA_KV_HEADS = 2
NSA_GROUP = NSA_HEADS // NSA_KV_HEADS
NSA_HD = 64
NSA_QW = NSA_HEADS * NSA_HD
NSA_KVW = NSA_KV_HEADS * NSA_HD
CMP_BLOCK = 32
CMP_STRIDE = 16
SEL_BLOCK = 64
SEL_TOP = 16
WINDOW = 512
PHI_HIDDEN = 256
Q_BLOCK = 64
ATTN_SCALE = NSA_HD ** -0.5
ROPE_THETA = 10000.0
M_HEADS = 4
M_HD = 128
M_W = M_HEADS * M_HD
M_CHUNK = 64
CONV_W = 4
PEER_HEADS = 8
N_KEYS = 128
N_EXPERTS = N_KEYS * N_KEYS
PEER_TOPK = 16
PEER_QDIM = 256
PEER_BLOCK = 128
MIX_W = NSA_QW + M_W
IN_SPLITS = (NSA_QW, 6 * NSA_KVW, 3 * NSA_HEADS, 2 * M_W, M_W, M_W, 2 * M_HEADS)
IN_W = sum(IN_SPLITS)
LN_EPS = 1e-5
ALPHA = (2 * DEPTH) ** 0.25
BETA = (8 * DEPTH) ** -0.25

kernel_name = 'nsa_mlstm_peer_hybrid_step'

def layer_norm(x, g, b):
    xf = x.astype(jnp.float32)
    mu = xf.mean(-1, keepdims=True)
    var = jnp.square(xf - mu).mean(-1, keepdims=True)
    return ((xf - mu) * lax.rsqrt(var + LN_EPS) * g + b).astype(x.dtype)

def rope(x, pos):
    half = x.shape[-1] // 2
    inv = ROPE_THETA ** (-jnp.arange(half, dtype=jnp.float32) / half)
    ang = pos.astype(jnp.float32)[:, None] * inv[None, :]
    cos = jnp.cos(ang)[:, None, :]
    sin = jnp.sin(ang)[:, None, :]
    xf = x.astype(jnp.float32)
    x1, x2 = xf[..., :half], xf[..., half:]
    return jnp.concatenate([x1 * cos - x2 * sin, x2 * cos + x1 * sin], axis=-1).astype(x.dtype)

def split_in_proj(x, w_in):
    z = x @ w_in
    cuts = [int(c) for c in np.cumsum(IN_SPLITS)[:-1]]
    return jnp.split(z, cuts, axis=-1)

def nsa_project(zq, zkv, zg, pos):
    B, T, _ = zq.shape
    q = rope(zq.reshape(B, T, NSA_HEADS, NSA_HD), pos)
    kv = zkv.reshape(B, T, 6, NSA_KV_HEADS, NSA_HD)
    rows = (rope(kv[:, :, 0], pos), kv[:, :, 1], rope(kv[:, :, 2], pos), kv[:, :, 3],
            rope(kv[:, :, 4], pos), kv[:, :, 5])
    gates = jax.nn.sigmoid(zg.astype(jnp.float32)).reshape(B, T, NSA_HEADS, 3)
    return q, rows, gates

def compress(rows, pe, w1, b1, w2):
    B, L, KV, hd = rows.shape
    r = CMP_BLOCK // CMP_STRIDE
    nch = L // CMP_STRIDE
    ch = rows[:, :nch * CMP_STRIDE].reshape(B, nch, CMP_STRIDE, KV, hd)
    nblk = nch - r + 1
    blocks = jnp.concatenate([ch[:, j:j + nblk] for j in range(r)], axis=2)
    blocks = blocks + pe[None, None, :, None, :]
    flat = blocks.transpose(0, 1, 3, 2, 4).reshape(B, nblk, KV, CMP_BLOCK * hd)
    hid = jax.nn.gelu(flat @ w1 + b1, approximate=False)
    return hid @ w2

def cmp_attend(q, qpos, kc, vc):
    B, T = q.shape[:2]
    qg = q.reshape(B, T, NSA_KV_HEADS, NSA_GROUP, NSA_HD)
    s = jnp.einsum('btngd,bcnd->btngc', qg, kc).astype(jnp.float32) * ATTN_SCALE
    nblk = kc.shape[1]
    blk_end = jnp.arange(nblk) * CMP_STRIDE + CMP_BLOCK - 1
    valid = (blk_end[None, :] <= qpos[:, None])[None, :, None, None, :]
    p = jax.nn.softmax(jnp.where(valid, s, -1e30), axis=-1) * valid
    o = jnp.einsum('btngc,bcnd->btngd', p.astype(vc.dtype), vc)
    return o.reshape(B, T, NSA_HEADS, NSA_HD), p

def select_blocks(p, qpos, n_sel):
    imp = p.sum(axis=3)
    R = SEL_BLOCK // CMP_STRIDE
    r = CMP_BLOCK // CMP_STRIDE
    nb = imp.shape[-1]
    right = n_sel * R + R - 1 - nb
    padded = jnp.pad(imp, ((0, 0), (0, 0), (0, 0), (r - 1, right)))
    score = padded[..., 0:(n_sel - 1) * R + 1:R]
    for o in range(1, R + r - 1):
        score = score + padded[..., o:o + (n_sel - 1) * R + 1:R]
    j = jnp.arange(n_sel)[None, :]
    cur = (qpos // SEL_BLOCK)[:, None]
    valid = (j * SEL_BLOCK <= qpos[:, None])[None, :, None, :]
    forced = ((j == 0) | (j == cur) | (j == cur - 1))[None, :, None, :]
    score = jnp.where(forced, jnp.inf, jnp.where(valid, score, -jnp.inf))
    _, sel = lax.top_k(score, min(SEL_TOP, n_sel))
    return sel

def to_blocks(rows, n_sel):
    B, L, KV, hd = rows.shape
    rows = jnp.pad(rows, ((0, 0), (0, n_sel * SEL_BLOCK - L), (0, 0), (0, 0)))
    return rows.reshape(B, n_sel, SEL_BLOCK, KV, hd).transpose(0, 3, 1, 2, 4)

def take_rows(table, idx):
    return table[idx]

def sel_attend(q, qpos, sel, kb, vb):
    B, Tq = q.shape[:2]
    k = sel.shape[-1]
    sel_t = sel.transpose(0, 2, 1, 3)
    gather = jax.vmap(jax.vmap(take_rows))
    kg = gather(kb, sel_t).reshape(B, NSA_KV_HEADS, Tq, k * SEL_BLOCK, NSA_HD)
    vg = gather(vb, sel_t).reshape(B, NSA_KV_HEADS, Tq, k * SEL_BLOCK, NSA_HD)
    kpos = (sel_t[..., None] * SEL_BLOCK + jnp.arange(SEL_BLOCK)).reshape(B, NSA_KV_HEADS, Tq, k * SEL_BLOCK)
    qg = q.reshape(B, Tq, NSA_KV_HEADS, NSA_GROUP, NSA_HD).transpose(0, 2, 1, 3, 4)
    s = jnp.einsum('bntgd,bntsd->bntgs', qg, kg).astype(jnp.float32) * ATTN_SCALE
    mask = kpos[:, :, :, None, :] <= qpos[None, None, :, None, None]
    pr = jax.nn.softmax(jnp.where(mask, s, -jnp.inf), axis=-1)
    o = jnp.einsum('bntgs,bntsd->bntgd', pr.astype(vg.dtype), vg)
    return o.transpose(0, 2, 1, 3, 4).reshape(B, Tq, NSA_HEADS, NSA_HD)

def win_attend(q, qpos, k, v, kpos):
    B, Tq = q.shape[:2]
    qg = q.reshape(B, Tq, NSA_KV_HEADS, NSA_GROUP, NSA_HD)
    s = jnp.einsum('btngd,bsnd->btngs', qg, k).astype(jnp.float32) * ATTN_SCALE
    diff = qpos[:, None] - kpos[None, :]
    mask = ((diff >= 0) & (diff < WINDOW) & (kpos[None, :] >= 0))[None, :, None, None, :]
    pr = jax.nn.softmax(jnp.where(mask, s, -jnp.inf), axis=-1)
    o = jnp.einsum('btngs,bsnd->btngd', pr.astype(v.dtype), v)
    return o.reshape(B, Tq, NSA_HEADS, NSA_HD)

def nsa_global(q, qpos, k_cmp, v_cmp, k_slc, v_slc, pe, w1, b1, w2):
    kc = compress(k_cmp, pe[0], w1[0], b1[0], w2[0])
    vc = compress(v_cmp, pe[1], w1[1], b1[1], w2[1])
    o_cmp, p = cmp_attend(q, qpos, kc, vc)
    n_sel = -(-k_slc.shape[1] // SEL_BLOCK)
    sel = select_blocks(p, qpos, n_sel)
    return o_cmp, sel, to_blocks(k_slc, n_sel), to_blocks(v_slc, n_sel)

def nsa_combine(gates, o_cmp, o_sel, o_win):
    B, T = gates.shape[:2]
    o = gates[..., 0:1] * o_cmp + gates[..., 1:2] * o_sel + gates[..., 2:3] * o_win
    return o.reshape(B, T, NSA_QW).astype(o_cmp.dtype)

def mlstm_chunk(carry, inp):
    C, n, m = carry
    q, k, v, ig, lf = inp
    L = q.shape[2]
    b = jnp.cumsum(lf, axis=-1)
    causal = jnp.tril(jnp.ones((L, L), dtype=bool))
    dmat = jnp.where(causal, b[..., :, None] - b[..., None, :] + ig[..., None, :], -jnp.inf)
    inter = b + m[..., None]
    m_t = jnp.maximum(inter, dmat.max(axis=-1))
    w_intra = jnp.exp(dmat - m_t[..., None])
    w_inter = jnp.exp(inter - m_t)
    s = jnp.einsum('bhtd,bhsd->bhts', q, k) * w_intra
    num = jnp.einsum('bhts,bhsv->bhtv', s, v) + w_inter[..., None] * jnp.einsum('bhtd,bhdv->bhtv', q, C)
    den = s.sum(-1) + w_inter * jnp.einsum('bhtd,bhd->bht', q, n)
    h = num / jnp.maximum(jnp.abs(den), jnp.exp(-m_t))[..., None]
    m_new = m_t[..., -1]
    w_s = jnp.exp(b[..., -1:] - b + ig - m_new[..., None])
    w_p = jnp.exp(b[..., -1] + m - m_new)
    C_new = w_p[..., None, None] * C + jnp.einsum('bhs,bhsd,bhsv->bhdv', w_s, k, v)
    n_new = w_p[..., None] * n + jnp.einsum('bhs,bhsd->bhd', w_s, k)
    return (C_new, n_new, m_new), h

def mlstm_mix(zqk, zv, zo, zif, buf0, C0, n0, m0, conv_w, conv_b, b_if, chunk):
    B, T, _ = zqk.shape
    f32 = jnp.float32
    full = jnp.concatenate([buf0.astype(zqk.dtype), zqk], axis=1)
    conv = conv_b
    for j in range(CONV_W):
        conv = conv + full[:, j:j + T] * conv_w[j]
    qk = jax.nn.silu(conv.astype(f32))

    def heads(a):
        return a.reshape(B, T, M_HEADS, M_HD).transpose(0, 2, 1, 3)

    q = heads(qk[..., :M_W])
    k = heads(qk[..., M_W:]) * (M_HD ** -0.5)
    v = heads(zv.astype(f32))
    gif = zif.astype(f32) + b_if.astype(f32)
    ig = gif[..., :M_HEADS].transpose(0, 2, 1)
    lf = jax.nn.log_sigmoid(gif[..., M_HEADS:]).transpose(0, 2, 1)
    nc = T // chunk

    def to_chunks(a):
        return jnp.moveaxis(a.reshape(B, M_HEADS, nc, chunk, *a.shape[3:]), 2, 0)

    carry0 = (C0.astype(f32), n0.astype(f32), m0.astype(f32))
    (C, n, m), h = lax.scan(mlstm_chunk, carry0,
                            (to_chunks(q), to_chunks(k), to_chunks(v), to_chunks(ig), to_chunks(lf)))
    h = jnp.moveaxis(h, 0, 2).reshape(B, M_HEADS, T, M_HD).transpose(0, 2, 1, 3).reshape(B, T, M_W)
    out = (jax.nn.sigmoid(zo.astype(f32)) * h).astype(zqk.dtype)
    return out, (C.astype(C0.dtype), n.astype(n0.dtype), m.astype(m0.dtype), full[:, T:])

def peer_ffn(x, w_pq, sub_keys, u_tab, v_tab):
    B, T, D = x.shape
    nt = B * T
    nb = -(-nt // PEER_BLOCK)
    xf = jnp.pad(x.reshape(nt, D), ((0, nb * PEER_BLOCK - nt), (0, 0))).reshape(nb, PEER_BLOCK, D)

    def one(xb):
        q = (xb @ w_pq).reshape(PEER_BLOCK, PEER_HEADS, 2, PEER_QDIM // 2)
        s = jnp.einsum('phcd,hckd->phck', q, sub_keys).astype(jnp.float32)
        ts, ti = lax.top_k(s, PEER_TOPK)
        cand = ts[:, :, 0, :, None] + ts[:, :, 1, None, :]
        cidx = ti[:, :, 0, :, None] * N_KEYS + ti[:, :, 1, None, :]
        fs, fpos = lax.top_k(cand.reshape(PEER_BLOCK, PEER_HEADS, -1), PEER_TOPK)
        eidx = jnp.take_along_axis(cidx.reshape(PEER_BLOCK, PEER_HEADS, -1), fpos, axis=-1)
        g = jax.nn.softmax(fs, axis=-1)
        u = u_tab[eidx]
        v = v_tab[eidx]
        a = jax.nn.gelu(jnp.einsum('pd,phkd->phk', xb, u).astype(jnp.float32), approximate=False)
        return jnp.einsum('phk,phkd->pd', (g * a).astype(v.dtype), v)

    y = lax.map(one, xf)
    return y.reshape(nb * PEER_BLOCK, D)[:nt].reshape(B, T, D)

def block_tail(x, mix, w_out, ln_g, ln_b, w_pq, sub_keys, u_tab, v_tab):
    h = layer_norm(ALPHA * x + mix @ w_out, ln_g[0], ln_b[0])
    return layer_norm(ALPHA * h + peer_ffn(h, w_pq, sub_keys, u_tab, v_tab), ln_g[1], ln_b[1])

def prompt_mix(x, w_in, pe, w1, b1, w2, conv_w, conv_b, b_if):
    B, S, _ = x.shape
    pos = jnp.arange(S)
    zq, zkv, zg, zqk, zv, zo, zif = split_in_proj(x, w_in)
    q, (k_cmp, v_cmp, k_slc, v_slc, k_win, v_win), gates = nsa_project(zq, zkv, zg, pos)
    o_cmp, sel, kb, vb = nsa_global(q, pos, k_cmp, v_cmp, k_slc, v_slc, pe, w1, b1, w2)
    pad = ((0, 0), (WINDOW, 0), (0, 0), (0, 0))
    kwp = jnp.pad(k_win, pad)
    vwp = jnp.pad(v_win, pad)

    def local(i):
        s0 = i * Q_BLOCK
        qb = lax.dynamic_slice_in_dim(q, s0, Q_BLOCK, axis=1)
        pb = lax.dynamic_slice_in_dim(pos, s0, Q_BLOCK, axis=0)
        sb = lax.dynamic_slice_in_dim(sel, s0, Q_BLOCK, axis=1)
        kw = lax.dynamic_slice_in_dim(kwp, s0, WINDOW + Q_BLOCK, axis=1)
        vw = lax.dynamic_slice_in_dim(vwp, s0, WINDOW + Q_BLOCK, axis=1)
        kpos = s0 - WINDOW + jnp.arange(WINDOW + Q_BLOCK)
        return sel_attend(qb, pb, sb, kb, vb), win_attend(qb, pb, kw, vw, kpos)

    o_sel, o_win = lax.map(local, jnp.arange(S // Q_BLOCK))
    o_sel = jnp.moveaxis(o_sel, 0, 1).reshape(B, S, NSA_HEADS, NSA_HD)
    o_win = jnp.moveaxis(o_win, 0, 1).reshape(B, S, NSA_HEADS, NSA_HD)
    o_nsa = nsa_combine(gates, o_cmp, o_sel, o_win)
    C0 = jnp.zeros((B, M_HEADS, M_HD, M_HD), jnp.float32)
    n0 = jnp.zeros((B, M_HEADS, M_HD), jnp.float32)
    m0 = jnp.zeros((B, M_HEADS), jnp.float32)
    buf0 = jnp.zeros((B, CONV_W - 1, 2 * M_W), x.dtype)
    o_m, (C, n, m, buf) = mlstm_mix(zqk, zv, zo, zif, buf0, C0, n0, m0, conv_w, conv_b, b_if, M_CHUNK)
    wl = min(WINDOW, S)
    mix = jnp.concatenate([o_nsa, o_m], axis=-1)
    return mix, (k_cmp, v_cmp, k_slc, v_slc, k_win[:, S - wl:], v_win[:, S - wl:], C, n, m, buf)

def sample_mix(x, kc_pool, vc_pool, ks_pool, vs_pool, kw_buf, vw_buf, C0, n0, m0, buf0, page_table,
               w_in, pe, w1, b1, w2, conv_w, conv_b, b_if):
    B, T, _ = x.shape
    past = page_table.shape[1] * PAGE_SIZE
    pos = past + jnp.arange(T)
    zq, zkv, zg, zqk, zv, zo, zif = split_in_proj(x, w_in)
    q, (k_cmp, v_cmp, k_slc, v_slc, k_win, v_win), gates = nsa_project(zq, zkv, zg, pos)

    def with_past(pool, new):
        old = pool[page_table].reshape(B, past, NSA_KV_HEADS, NSA_HD)
        return jnp.concatenate([old, new.astype(old.dtype)], axis=1)

    o_cmp, sel, kb, vb = nsa_global(q, pos, with_past(kc_pool, k_cmp), with_past(vc_pool, v_cmp),
                                    with_past(ks_pool, k_slc), with_past(vs_pool, v_slc), pe, w1, b1, w2)
    wb = kw_buf.shape[1]
    kw = jnp.concatenate([kw_buf, k_win.astype(kw_buf.dtype)], axis=1)
    vw = jnp.concatenate([vw_buf, v_win.astype(vw_buf.dtype)], axis=1)
    kpos = past - wb + jnp.arange(wb + T)
    o_sel = sel_attend(q, pos, sel, kb, vb)
    o_win = win_attend(q, pos, kw, vw, kpos)
    o_nsa = nsa_combine(gates, o_cmp, o_sel, o_win)
    o_m, (C, n, m, buf) = mlstm_mix(zqk, zv, zo, zif, buf0, C0, n0, m0, conv_w, conv_b, b_if, T)
    mix = jnp.concatenate([o_nsa, o_m], axis=-1)
    return mix, (k_cmp, v_cmp, k_slc, v_slc, kw[:, T:], vw[:, T:], C, n, m, buf)

def setup_inputs(seed: int = 0) -> dict:
    key = jax.random.key(seed)
    ks = jax.random.split(key, 32)
    f32 = jnp.float32
    n_pages = PAST_LEN // PAGE_SIZE
    n_used = DEC_BATCH * n_pages
    n_pool = n_used + max(1, n_used // 4)
    wb = min(WINDOW, PAST_LEN)

    def nrm(k, shape, scale=1.0):
        return jax.random.normal(k, shape, f32) * scale

    pool_shape = (DEPTH, n_pool, PAGE_SIZE, NSA_KV_HEADS, NSA_HD)
    win_shape = (DEPTH, DEC_BATCH, wb, NSA_KV_HEADS, NSA_HD)
    page_table = jax.random.permutation(ks[12], n_pool)[:n_used].reshape(DEC_BATCH, n_pages).astype(jnp.int32)
    b_i = nrm(ks[21], (DEPTH, M_HEADS), 0.1)
    b_f = jnp.linspace(3.0, 6.0, M_HEADS, dtype=f32)[None, :] + nrm(ks[22], (DEPTH, M_HEADS), 0.1)
    return {
        'x_prompt': nrm(ks[0], (BATCH, SEQ, D_MODEL)),
        'x_sample': nrm(ks[1], (DEC_BATCH, DEC_SEQ, D_MODEL)),
        'cache_k_cmp': nrm(ks[2], pool_shape),
        'cache_v_cmp': nrm(ks[3], pool_shape),
        'cache_k_slc': nrm(ks[4], pool_shape),
        'cache_v_slc': nrm(ks[5], pool_shape),
        'cache_k_win': nrm(ks[6], win_shape),
        'cache_v_win': nrm(ks[7], win_shape),
        'state_C': nrm(ks[8], (DEPTH, DEC_BATCH, M_HEADS, M_HD, M_HD), 0.1),
        'state_n': nrm(ks[9], (DEPTH, DEC_BATCH, M_HEADS, M_HD), 0.1),
        'state_m': nrm(ks[10], (DEPTH, DEC_BATCH, M_HEADS)),
        'state_conv': nrm(ks[11], (DEPTH, DEC_BATCH, CONV_W - 1, 2 * M_W)),
        'page_table': page_table,
        'w_in': nrm(ks[13], (DEPTH, D_MODEL, IN_W), D_MODEL ** -0.5),
        'w_out': nrm(ks[14], (DEPTH, MIX_W, D_MODEL), MIX_W ** -0.5 * BETA),
        'w_phi1': nrm(ks[15], (DEPTH, 2, CMP_BLOCK * NSA_HD, PHI_HIDDEN), (CMP_BLOCK * NSA_HD) ** -0.5),
        'b_phi1': nrm(ks[16], (DEPTH, 2, PHI_HIDDEN), 0.02),
        'w_phi2': nrm(ks[17], (DEPTH, 2, PHI_HIDDEN, NSA_HD), PHI_HIDDEN ** -0.5),
        'pe_cmp': nrm(ks[18], (DEPTH, 2, CMP_BLOCK, NSA_HD), 0.02),
        'conv_w': nrm(ks[19], (DEPTH, CONV_W, 2 * M_W), CONV_W ** -0.5),
        'conv_b': nrm(ks[20], (DEPTH, 2 * M_W), 0.02),
        'b_if': jnp.concatenate([b_i, b_f], axis=-1),
        'ln_g': 1.0 + nrm(ks[23], (DEPTH, 2, D_MODEL), 0.02),
        'ln_b': nrm(ks[24], (DEPTH, 2, D_MODEL), 0.02),
        'w_pq': nrm(ks[25], (DEPTH, D_MODEL, PEER_HEADS * PEER_QDIM), D_MODEL ** -0.5),
        'sub_keys': nrm(ks[26], (DEPTH, PEER_HEADS, 2, N_KEYS, PEER_QDIM // 2), (PEER_QDIM // 2) ** -0.5),
        'u_tab': nrm(ks[27], (DEPTH, N_EXPERTS, D_MODEL), D_MODEL ** -0.5),
        'v_tab': nrm(ks[28], (DEPTH, N_EXPERTS, D_MODEL), BETA),
    }

def reference(x_prompt, x_sample, cache_k_cmp, cache_v_cmp, cache_k_slc, cache_v_slc, cache_k_win, cache_v_win,
              state_C, state_n, state_m, state_conv, page_table, w_in, w_out, w_phi1, b_phi1, w_phi2, pe_cmp,
              conv_w, conv_b, b_if, ln_g, ln_b, w_pq, sub_keys, u_tab, v_tab):
    xp, xs = x_prompt, x_sample
    p_states, s_states = [], []
    for l in range(DEPTH):
        mix_p, st_p = prompt_mix(xp, w_in[l], pe_cmp[l], w_phi1[l], b_phi1[l], w_phi2[l],
                                 conv_w[l], conv_b[l], b_if[l])
        mix_s, st_s = sample_mix(xs, cache_k_cmp[l], cache_v_cmp[l], cache_k_slc[l], cache_v_slc[l],
                                 cache_k_win[l], cache_v_win[l], state_C[l], state_n[l], state_m[l],
                                 state_conv[l], page_table, w_in[l], pe_cmp[l], w_phi1[l], b_phi1[l],
                                 w_phi2[l], conv_w[l], conv_b[l], b_if[l])
        xp = block_tail(xp, mix_p, w_out[l], ln_g[l], ln_b[l], w_pq[l], sub_keys[l], u_tab[l], v_tab[l])
        xs = block_tail(xs, mix_s, w_out[l], ln_g[l], ln_b[l], w_pq[l], sub_keys[l], u_tab[l], v_tab[l])
        p_states.append(st_p)
        s_states.append(st_s)
    p_kc, p_vc, p_ks, p_vs, p_kw, p_vw, p_C, p_n, p_m, p_conv = [jnp.stack(a) for a in zip(*p_states)]
    s_kc, s_vc, s_ks, s_vs, s_kw, s_vw, s_C, s_n, s_m, s_conv = [jnp.stack(a) for a in zip(*s_states)]
    return (xp, xs, p_kc, p_vc, p_ks, p_vs, p_kw, p_vw, p_C, p_n, p_m, p_conv,
            s_kc, s_vc, s_ks, s_vs, s_kw, s_vw, s_C, s_n, s_m, s_conv)


_drawn_inputs = setup_inputs


def setup_inputs(seed=0):
    import zlib

    import numpy as np

    out = dict(_drawn_inputs(seed))
    spreads = {}
    factors = {'b_phi1': 4.605, 'pe_cmp': 3.848}
    for name, (base, spread) in spreads.items():
        noise = np.random.default_rng([zlib.crc32(name.encode()), seed]).standard_normal(out[name].shape)
        drawn = base * np.exp(spread * noise) if base else spread * noise
        out[name] = __import__('jax').numpy.asarray(drawn.astype(out[name].dtype))
    for name, factor in factors.items():
        out[name] = (out[name] * factor).astype(out[name].dtype)
    return out
```

```python
import numpy as np
import concourse.bass as bass
from concourse import mybir
from contextlib import ExitStack

F32 = mybir.dt.float32
U32 = mybir.dt.uint32
I32 = mybir.dt.int32
ALU = mybir.AluOpType
ACT = mybir.ActivationFunctionType
AX = mybir.AxisListType.X

P = 128
D = 1024
KC = D // P
SEQ, DB, DT = 512, 8, 4
PT = SEQ // P
NS = DB * DT
T = SEQ + NS
TILES = PT + 1
ROWS = [P] * PT + [NS]
PAST, PAGE, POOL = 2048, 128, 160
NH, NKV, NG, HD = 8, 2, 4, 64
MH, MD = 4, 128
CB, CS = 32, 16
NCH = PAST // CS
NBLK = NCH - 1
PCH = SEQ // CS
PBLK = PCH - 1
SELB, NSEL, TOPK = 64, 33, 16
WIN = 512
SCALE = HD ** -0.5
KSCALE = MD ** -0.5
ALPHA = 2.0 ** 0.25
EPS = 1e-5
NEG = -1e30
PH, NK = 8, 128
SLOTS = PH * TOPK
QB = P // NS
INW = 3360
CQ, CKV, CQK, CV, CO, CIF = 0, 512, 1304, 2328, 2840, 3352


def const_layout():
    at, out = 0, {}
    for name, n in (("ident", 128), ("ident4", 32), ("caus", 128), ("cvalid", PT * PBLK), ("cadd", PT * PBLK),
                    ("cos", TILES * 32), ("sin", TILES * 32), ("tri", 128), ("sblk", 128), ("hb", 32),
                    ("grp", 128), ("selh", 512), ("winm", 4), ("newm", 64), ("iota", 16), ("pm8", 1),
                    ("seltok", 256), ("seltokT", 64), ("hind", 8), ("ones", 1), ("forced", NSEL), ("eps", 1)):
        out[name] = (at, n)
        at += n
    return out, at


CL, CW = const_layout()


def const_array():
    c = np.zeros((P, CW), np.float32)

    def put(name, a):
        at, n = CL[name]
        a = np.asarray(a, np.float32)
        a = a.reshape(a.shape[0], -1)
        c[:a.shape[0], at:at + n] = a

    p = np.arange(P)
    put("ident", np.eye(P))
    put("ident4", p[:, None] % NS == np.arange(NS)[None, :])
    put("caus", np.where(p[None, :] <= p[:, None], 0.0, NEG))
    tok = (np.arange(PT)[None, :, None] * P + p[:, None, None])
    ok = tok >= np.arange(PBLK)[None, None, :] * CS + CB - 1
    put("cvalid", ok)
    put("cadd", np.where(ok, 0.0, NEG))
    half = HD // 2
    inv = np.float32(10000.0) ** (-np.arange(half, dtype=np.float32) / np.float32(half))
    pos = np.zeros((P, TILES), np.float32)
    pos[:, :PT] = np.arange(PT)[None, :] * P + p[:, None]
    pos[:, PT] = PAST + p % DT
    ang = (pos[:, :, None] * inv[None, None, :]).astype(np.float32)
    put("cos", np.cos(ang.astype(np.float64)))
    put("sin", np.sin(ang.astype(np.float64)))
    put("tri", p[:, None] <= p[None, :])
    put("sblk", (p[:, None] // DT == p[None, :] // DT) & (p[:, None] <= p[None, :]))
    put("hb", p[:, None] // DT == np.arange(32)[None, :])
    put("grp", p[:, None] // NG == p[None, :] // NG)
    sel = np.zeros((MH, MH, P))
    for h in range(MH):
        sel[h, h] = 1
    put("selh", sel)
    b4, n, t, g = p // 32, p // 16 % 2, p // 4 % 4, p % 4
    put("winm", np.where(np.arange(4)[None, :] <= t[:, None], NEG, 0.0))
    s = np.arange(NS)
    newm = np.zeros((P, 2, NS))
    seltok = np.zeros((NS, 2, P))
    for G in range(2):
        mine = (s[None, :] // DT == 4 * G + b4[:, None]) & (s[None, :] % DT <= t[:, None])
        newm[:, G] = np.where(mine, 0.0, NEG)
        seltok[:, G] = s[:, None] == ((4 * G + b4) * DT + t)[None, :]
    put("newm", newm)
    put("seltok", seltok)
    put("seltokT", seltok.transpose(2, 1, 0))
    put("iota", np.broadcast_to(np.arange(16), (P, 16)))
    put("pm8", (p % 8)[:, None])
    put("hind", (n * NG + g)[:, None] == np.arange(NH)[None, :])
    put("ones", np.ones((P, 1)))
    f = np.zeros((P, NSEL))
    f[:, [0, NSEL - 2, NSEL - 1]] = 1e30
    put("forced", f)
    put("eps", np.full((P, 1), EPS))
    return c


PARW = KC * 4 + KC + 4 + 2 * 16


def program(nc, i, o):
    ctx = ExitStack()
    with ctx:
        WORDS = 53000
        arena = ctx.enter_context(nc.sbuf_tensor("arena", [P, WORDS], F32))
        PB = [ctx.enter_context(nc.psum_tensor(f"bank{n}", [P, 512], F32)) for n in range(8)]

        def sem(name):
            return ctx.enter_context(nc.semaphore(name))

        class Place:
            def __init__(self, at):
                self.at = at

            def take(self, n):
                self.at += n
                assert self.at <= WORDS, self.at
                return arena[:, self.at - n:self.at]

        base = Place(0)
        consts = base.take(CW)
        par = base.take(PARW)
        x_sb = base.take(TILES * D).rearrange("p (t d) -> p t d", t=TILES)
        small = base.take(700)
        front = base.at
        mix = base.take(TILES * D).rearrange("p (t d) -> p t d", t=TILES)
        zq = base.take(TILES * 512).rearrange("p (t c) -> p t c", t=TILES)
        zkv = base.take(TILES * 768).rearrange("p (t c) -> p t c", t=TILES)
        gates = base.take(TILES * 24).rearrange("p (t c) -> p t c", t=TILES)
        mid = base.at
        v1 = base.take(PT * MH * 129).rearrange("p (t h c) -> p t h c", t=PT, h=MH)
        v1s = base.take(129)
        zo = base.take(TILES * 512).rearrange("p (t c) -> p t c", t=TILES)
        zpad = base.take(KC * (3 + SEQ)).rearrange("p (c s) -> p c s", c=KC)
        zspad = base.take(KC * DB * 7).rearrange("p (c b s) -> p c b s", c=KC, b=DB)
        qkT = base.take(KC * T).rearrange("p (c s) -> p c s", c=KC)
        late = base.at
        p1 = Place(late)
        xT = p1.take(KC * T).rearrange("p (c s) -> p c s", c=KC)
        wst = [p1.take(KC * 512).rearrange("p (c n) -> p c n", c=KC) for _ in range(2)]
        p2 = Place(late)
        C0 = p2.take(32 * 129).rearrange("p (g v) -> p g v", g=32)
        VB = p2.take(32 * 129).rearrange("p (g v) -> p g v", g=32)
        BC = p2.take(MH * 192).rearrange("p (h q s) -> p h q s", h=MH, q=6)
        smt = p2.take(128)
        SWs = p2.take(128)
        kws = p2.take(128)
        numT = p2.take(128)
        prod = p2.take(128)
        h_s = p2.take(128)
        Cout = p2.take(MH * 129).rearrange("p (h v) -> p h v", h=MH)
        cols = p2.take(32).rearrange("p (q t h) -> p q t h", q=2, t=PT)
        ktok = p2.take(PT * 512).rearrange("p (t c) -> p t c", t=PT)
        assert p2.at <= p1.at
        p2b = Place(p1.at)
        SWb = VB.rearrange("p g v -> p (g v)")[:, 0:PT * 512].rearrange("p (i s) -> p i s", i=PT)
        wt = p2b.take(2 * 512).rearrange("p (z s) -> p z s", z=2)
        sg = mix.rearrange("p t d -> p (t d)")[:, 0:2 * T].rearrange("p (z s) -> p z s", z=2)
        qcs = p2b.take(128)
        kcs = p2b.take(128)
        rows = Place(p2b.at)

        def row(n=T):
            return rows.take(n)[0:MH, :]

        def C(name, parts=P):
            at, n = CL[name]
            return consts[0:parts, at:at + n]

        ident = C("ident")
        conv_w = par[:, 0:32].rearrange("p (c j) -> p c j", c=KC)
        conv_b = par[:, 32:40]
        b1 = par[:, 40:44]
        pe = par[:, 44:76]

        s_const = sem("const_loaded")
        s_x = sem("x_loaded")
        s_xT = sem("xT_loaded")
        s_w = [sem(f"w_in_loaded{k}") for k in range(2)]
        s_st = sem("state_small_loaded")
        s_c0 = sem("C0_loaded")
        s_out = sem("outputs_written")
        s_p2w = sem("states_written")
        P2W = 16 * (1 + KC + 4)
        s_zps = sem("z_in_psum")
        s_zev = sem("z_copied")
        s_bc0 = sem("v1_ones_set")
        s_pad = sem("conv_pad_set")
        s_dve = sem("vector_step")
        s_act = sem("scalar_step")
        s_cv = sem("conv_done")
        s_sg = sem("conv_sigmoid")
        s_qk = sem("qk_activated")
        s_fabs = sem("f_abs")
        s_fexp = sem("f_exp")
        s_rows = sem("gate_rows_done")
        s_rexp = sem("gate_rows_exp")
        s_ktp = sem("ktok_psum")
        s_kte = sem("ktok_copied")
        s_colp = sem("cols_psum")
        s_cole = sem("cols_copied")
        s_bcp = sem("negM_broadcast")
        s_sp = sem("mlstm_scores_psum")
        s_wmin = sem("mlstm_exponent")
        s_wexp = sem("mlstm_weights")
        s_sw = sem("mlstm_weighted")
        s_np = sem("mlstm_num_psum")
        s_nev = sem("mlstm_num_used")
        s_wx = sem("C_weights")
        s_kw = sem("k_weighted")
        s_cp = sem("C_psum")
        s_ce = sem("C_copied")
        s_zog = sem("o_gate")
        s_bcs = sem("sample_rows_psum")
        s_bce = sem("sample_rows_copied")
        s_sps = sem("sample_scores_psum")
        s_sws = sem("sample_weighted")
        s_sx = sem("sample_exponent")
        s_sxe = sem("sample_weights")
        s_ni = sem("sample_inter_psum")
        s_nie = sem("sample_inter_copied")
        s_prod = sem("sample_qn0")
        s_kts = sem("sample_k_psum")
        s_kse = sem("sample_k_weighted")
        s_nit = sem("sample_inter_T")
        s_nin = sem("sample_num_psum")
        s_vb = sem("v_blocks")
        s_cup = sem("C_update_psum")
        s_cue = sem("C_updated")
        s_omix = sem("mlstm_mix_done")
        s_kw_out = sem("window_copied")

        GROUPS = [("qk", CQK, 512), ("qk", CQK + 512, 512), ("if", CIF, 8), ("v", CV, 512), ("o", CO, 512),
                  ("q", CQ, 512), ("kv", CKV, 512), ("kvg", CKV + 512, 280)]
        units = []
        for g, (kind, c0, n) in enumerate(GROUPS):
            if kind == "qk":
                for c in range(4):
                    units.append((g, kind, 4 * (g % 2) + c, "prompt", c * 128))
                    units.append((g, kind, 4 * (g % 2) + c, "sample", c * 128))
            elif kind == "if":
                for c in range(2):
                    units.append((g, kind, c, "prompt", 4 * c))
                    units.append((g, kind, c, "sample", 4 * c))
            else:
                for t in range(TILES):
                    units.append((g, kind, t, "tile", 0))
        NU = len(units)

        def after_unit(kind, last=True):
            return max(n for n, u in enumerate(units) if u[1] == kind) + 1

        U_QK, U_IF, U_V, U_O, U_Q, U_KVG = (after_unit(k) for k in ("qk", "if", "v", "o", "q", "kvg"))

        r_ig, r_f, r_ab, r_ex = row(), row(), row(), row()
        r_b0, r_b1, r_m = row(), row(), row()
        SR = rows.take(6 * NS)[0:MH, :].rearrange("p (q s) -> p q s", q=6)
        wcol = rows.take(3 * PT * MH)
        b_if = small[0:MH, 0:2]
        m0r = small[0:MH, 2:10]
        m_last = small[0:MH, 232:240]
        rs8 = small[:, 16:144]

        p3 = Place(mid)
        W1 = p3.take(2 * 16 * 256).rearrange("p (v k n) -> p v k n", v=2, k=16)
        ring = [p3.take(2048) for _ in range(4)]
        CT_f = p3.take(4096)
        CT = CT_f.rearrange("p (b n k c) -> p b n k c", b=2, n=2, k=8)
        KTb = [CT_f[:, 2048 * z:2048 * z + 2048] for z in range(2)]
        hid = p3.take(2 * 508).rearrange("p (m c) -> p m c", m=2)
        KCm = p3.take(DB * NBLK).rearrange("p (b c) -> p b c", b=DB)
        KCp = p3.take(PBLK)
        VCm = p3.take(DB * 128).rearrange("p (b c) -> p b c", b=DB)
        VCp = p3.take(128)
        w2v = p3.take(2 * HD).rearrange("p (m d) -> p m d", m=2)
        w2k = p3.take(2 * 2 * 128).rearrange("p (n m d) -> p n m d", n=2, m=2)
        biasc = p3.take(4)
        QP = p3.take(DB * 32).rearrange("p (b r) -> p b r", b=DB)
        KTn = p3.take(64).rearrange("p (v s) -> p v s", v=2)
        OE = p3.take(512)
        tmpo = p3.take(512)
        pidx = small[:, 240:256]
        pages = pidx[:, 0:8].bitcast(I32)
        cidx = pidx[:, 8:16].bitcast(U32)
        p3a = Place(p3.at)
        QT = p3a.take(4 * 512).rearrange("p (j s) -> p j s", j=4)
        KT = p3a.take(2 * 512).rearrange("p (v s) -> p v s", v=2)
        PX = p3a.take(2 * 512).rearrange("p (z s) -> p z s", z=2)
        PTb = p3a.take(2 * 512).rearrange("p (z s) -> p z s", z=2)
        rtmp = mix.rearrange("p t d -> p (t d)")[:, 2 * T:2 * T + 1024].rearrange("p (k s) -> p k s", k=4)
        p3b = Place(p3.at)
        Sslc = p3b.take(PAST + NS)
        Swin = p3b.take(WIN + NS)
        Pc = p3b.take(NBLK)
        impp = p3b.take(136)
        blk = p3b.take(3 * NSEL + 16)
        PTs = p3b.take(17 * P).rearrange("p (k r) -> p k r", k=17)
        PTw = p3b.take(5 * P).rearrange("p (k r) -> p k r", k=5)
        PcT = p3b.take(P)
        oacc = p3b.take(128)
        g4 = p3b.take(248)
        assert p3b.at <= WORDS
        p3w = Place(mid)
        WK = [p3w.take(512) for _ in range(2)]
        WV = [p3w.take(512) for _ in range(4)]
        KTw = p3w.take(512)

        s_rope = sem("rope_done")
        s_pg = sem("pages_loaded")
        s_ci = sem("chunk_index")
        s_kvo = sem("kv_rows_written")
        s_w1 = sem("w_phi_loaded")
        s_tp = sem("transposes_psum")
        s_te = sem("transposes_copied")
        s_s = sem("attn_scores")
        s_nb = sem("attn_max")
        s_px = sem("attn_probs")
        s_pv = sem("attn_out_psum")
        s_ou = sem("attn_out_used")
        s_ga = [sem(f"chunks_loaded{k}") for k in range(4)]
        s_rel = sem("chunks_used")
        s_peb = sem("pe_bias_psum")
        s_bias = sem("phi_bias")
        s_hp = sem("hidden_psum")
        s_hg = sem("hidden_gelu")
        s_w2p = sem("compressed_psum")
        s_w2e = sem("compressed_copied")
        s_cs = sem("cmp_scores")
        s_cx = sem("cmp_exponent")
        s_ce2 = sem("cmp_exp")
        s_cpn = sem("cmp_probs")
        s_cpv = sem("cmp_out_psum")
        s_cou = sem("cmp_out_used")
        s_gc = sem("g_cmp_scores")
        s_gcb = sem("g_cmp_max")
        s_gcx = sem("g_cmp_exp")
        s_gcp = sem("g_cmp_probs")
        s_imp = sem("g_importance")
        s_wk = [sem(f"win_k_loaded{k}") for k in range(2)]
        s_wv = [sem(f"win_v_loaded{k}") for k in range(4)]
        s_wku = sem("win_k_used")
        s_ic = sem("g_importance_copied")
        s_gwb = sem("g_win_max")
        s_gsb = sem("g_slc_max")
        s_gwx = sem("g_win_exp")
        s_gsx = sem("g_slc_exp")
        s_kb = sem("g_keysT_used")
        s_gco = sem("g_cmp_out")
        s_gwo = sem("g_win_out")
        s_oe = sem("g_out_by_head")
        s_ot = sem("g_out_tokens")
        s_ote = sem("g_out_copied")
        s_qp = sem("q_padded_zero")
        s_qpt = sem("q_padded")

        PU = [(br, t, h) for br in range(2) for t in range(PT) for h in range(NH)]
        CSTEPS = [(v, b) for b in [()] + [(2 * k, 2 * k + 1) for k in range(DB // 2)] for v in range(2)]
        GA = [("cmp", v, b) for v, bs in CSTEPS for b in (bs or (None,))]
        NCG = len(GA)
        for G in range(2):
            GA += [("slc", v, 4 * G + k) for v in range(2) for k in range(4)]

        fills = [0]
        drains = [0]
        N_Q, N_PU = 1 + PT * 2, len(PU)

        def loaded(n):
            return 16 * (n // 4 + 1) + (16 if n % 4 < 2 else 0)

        def nsa_sync(sp):
            sp.wait_ge(s_rope, TILES)
            for k, name in enumerate(("kc", "vc", "ks", "vs", "kw", "vw")):
                sp.dma_start(o["p_" + name].rearrange("(t p) c -> p t c", p=P),
                             zkv[:, 0:PT, k * 128:(k + 1) * 128]).then_inc(s_kvo if k < 2 else s_out, 16)
                if k < 4:
                    sp.dma_start(o["s_" + name], zkv[0:NS, PT, k * 128:(k + 1) * 128]).then_inc(s_out, 16)
                else:
                    for b in range(DB):
                        sp.dma_start(o["s_" + name][b, WIN - DT:WIN, :],
                                     zkv[DT * b:DT * b + DT, PT, k * 128:(k + 1) * 128]).then_inc(s_out, 16)
                    src = i["kwin"] if k == 4 else i["vwin"]
                    sp.dma_start(o["s_" + name][:, 0:WIN - DT, :].rearrange("b (k r) c -> b k (r c)", k=4),
                                 src[:, DT:WIN, :].rearrange("b (k r) c -> b k (r c)", k=4)).then_inc(s_out, 16)
            sp.wait_ge(s_omix, 1)
            sp.wait_ge(s_p2w, P2W)
            for v in range(2):
                sp.dma_start(W1[:, v], i["w1"][v].rearrange("(k p) n -> p k n", p=P)).then_inc(s_w1, 16)
            sp.dma_start(w2v, i["w2"][1].rearrange("(m p) d -> p m d", p=P)).then_inc(s_w1, 16)
            for n in range(2):
                sp.dma_start(w2k[:, n], i["w2pad"][n].rearrange("(m p) d -> p m d", p=P)).then_inc(s_w1, 16)
            sp.wait_ge(s_hp, 2 * len(CSTEPS))
            kw_v = i["kwin"].rearrange("b (c k) d -> b c (k d)", k=4)
            vw_v = i["vwin"].rearrange("b (c k) d -> b c (k d)", k=4)
            for b in range(DB):
                if b >= 2:
                    sp.wait_ge(s_wku, b - 1)
                sp.dma_start(WK[b % 2], kw_v[b]).then_inc(s_wk[b % 2], 16)
                if b >= 4:
                    sp.wait_ge(s_gwo, 1)
                sp.dma_start(WV[b % 4], vw_v[b]).then_inc(s_wv[b % 4], 16)

        def nsa_gpsimd(pool):
            pool.dma_start(pages, i["pages"]).then_inc(s_pg, 16)
            pool.wait_ge(s_ci, 1)
            pool.wait_ge(s_omix, 1)
            pool.wait_ge(s_p2w, P2W)
            pool.wait_ge(s_kvo, 32)
            src = {("cmp", 0): "kcmp", ("cmp", 1): "vcmp", ("slc", 0): "kslc", ("slc", 1): "vslc"}
            for n, (what, v, b) in enumerate(GA):
                if 4 <= n < NCG + 4:
                    pool.wait_ge(s_tp, N_Q + N_PU + 4 * (n - 3))
                elif n >= 4:
                    pool.wait_ge(s_rel, n - 3 - NCG)
                if b is None:
                    rows16 = o[("p_kc", "p_vc")[v]].rearrange("(c k) (n d) -> c n k d", k=CS, n=NKV)
                    dst16 = ring[n % 4][0:PCH, :].rearrange("p (n k d) -> p n k d", n=NKV, k=CS)
                    for kvh in range(NKV):
                        pool.dma_start(dst16[:, kvh], rows16[:, kvh]).then_inc(s_ga[n % 4], 16)
                else:
                    pool.indirect_dma_start(ring[n % 4], None, i[src[(what, v)]],
                                            bass.IndirectOffsetOnAxis(cidx[:, b:b + 1], 0))\
                        .then_inc(s_ga[n % 4], 16)

        def nsa_tensor(pe_eng):
            te = nc.tensor

            def mm(out, l, r, start=True, stop=True):
                return te.matmul(out, l, r, start=start, stop=stop)

            def fill(make):
                n = fills[0]
                fills[0] += 1
                if n >= 2:
                    pe_eng.wait_ge(s_te, n - 1)
                make(PB[6 + n % 2]).then_inc(s_tp, 1)
                return n + 1

            def tr(out, in_, parts=P):
                return te.transpose(out, in_, ident[0:parts, 0:parts])

            pe_eng.wait_ge(s_rope, TILES)
            pe_eng.wait_ge(s_p2w, P2W)
            pe_eng.wait_ge(s_omix, 1)

            def pairs(t):
                return [zq[0:ROWS[t], t, g * P:(g + 1) * P] for g in range(NG)]

            def sample_q(bank):
                for g in range(NG):
                    tr(bank[:, g * NS:(g + 1) * NS], pairs(PT)[g], NS)
                for k, c in enumerate((256, 512)):
                    last = tr(bank[:, 128 + k * NS:128 + (k + 1) * NS], zkv[0:NS, PT, c:c + 128], NS)
                return last
            fill(sample_q)
            for t in range(PT):
                def q_fill(bank):
                    for g in range(NG):
                        last = tr(bank[:, g * P:(g + 1) * P], pairs(t)[g])
                    return last

                def k_fill(bank):
                    for k, c in enumerate((256, 512)):
                        last = tr(bank[:, k * P:(k + 1) * P], zkv[:, t, c:c + 128])
                    return last
                fill(q_fill)
                fill(k_fill)
            pe_eng.wait_ge(s_te, fills[0])

            at = {}
            for u in range(N_PU + 2):
                if u < N_PU:
                    br, t, h = PU[u]
                    if u >= 2:
                        pe_eng.wait_ge(s_px, u - 1)
                    r = slice(HD * (h // NG), HD * (h // NG) + HD)
                    mm(PB[u % 2][:, 0:(t + 1) * P], QT[r, h % NG, t * P:(t + 1) * P], KT[r, br, 0:(t + 1) * P])\
                        .then_inc(s_s, 1)
                if 1 <= u <= N_PU:
                    br, t, h = PU[u - 1]
                    pe_eng.wait_ge(s_px, u)

                    def p_fill(bank):
                        for k in range(t + 1):
                            last = tr(bank[:, k * P:(k + 1) * P], PX[:, (u - 1) % 2, k * P:(k + 1) * P])
                        return last
                    at[u - 1] = fill(p_fill)
                if u >= 2:
                    br, t, h = PU[u - 2]
                    pe_eng.wait_ge(s_te, at[u - 2])
                    bt = (u - 2) // NH
                    if h == 0 and bt >= 2:
                        pe_eng.wait_ge(s_ou, bt - 1)
                    for k in range(t + 1):
                        c = (3 if br == 0 else 5) * 128 + HD * (h // NG)
                        last = mm(PB[2 + bt % 2][:, h * HD:(h + 1) * HD], PTb[:, (u - 2) % 2, k * P:(k + 1) * P],
                                  zkv[:, k, c:c + HD], k == 0, k == t)
                    last.then_inc(s_pv, 1)

            pe_eng.wait_ge(s_w1, 80)
            for v in range(2):
                for m in range(2):
                    for k in range(16):
                        last = mm(PB[4][:, 2 * v + m:2 * v + m + 1], W1[:, v, k, m * P:(m + 1) * P],
                                  pe[:, 16 * v + k:16 * v + k + 1], k == 0, k == 15)
            last.then_inc(s_peb, 1)
            pe_eng.wait_ge(s_ou, 8)
            g_at = 0
            for n, (v, bs) in enumerate(CSTEPS):
                ch = NCH if bs else PCH
                nblk = ch - 1
                nb = len(bs) or 1
                for bi in range(nb):
                    pe_eng.wait_ge(s_ga[g_at % 4], loaded(g_at))
                    rows_v = ring[g_at % 4].rearrange("p (n k c) -> p n k c", n=NKV, k=8)
                    for kvh in range(NKV):
                        for q4 in range(2):
                            def c_fill(bank):
                                for k in range(4):
                                    last = tr(bank[:, k * P:k * P + ch], rows_v[0:ch, kvh, 4 * q4 + k, :], ch)
                                return last
                            fl = fill(c_fill)
                    g_at += 1
                pe_eng.wait_ge(s_te, fl)
                for m in range(2):
                    if n >= 1:
                        pe_eng.wait_ge(s_hg, 2 * (n - 1) + m + 1)
                    for k in range(16):
                        off = k // 8
                        last = mm(PB[m][:, 0:nb * 2 * nblk].rearrange("p (b n c) -> p b n c", b=nb, n=2),
                                  W1[:, v, k, m * P:(m + 1) * P], CT[:, 0:nb, :, k % 8, off:off + nblk],
                                  k == 0, k == 15)
                    last.then_inc(s_hp, 1)
                pe_eng.wait_ge(s_hg, 2 * n + 2)
                if n >= 2:
                    pe_eng.wait_ge(s_w2e, n - 1)
                hv = hid[:, :, 0:nb * 2 * nblk].rearrange("p m (b n c) -> p m b n c", b=nb, n=2)
                if v == 0:
                    for k in range(4):
                        kvh, m = k // 2, k % 2
                        last = mm(PB[2][:, 0:nb * nblk].rearrange("p (b c) -> p b c", b=nb), w2k[:, kvh, m, :],
                                  hv[:, m, :, kvh, :], k == 0, k == 3)
                else:
                    for bi in range(nb):
                        for kvh in range(2):
                            c = (2 * bi + kvh) * HD
                            for m in range(2):
                                last = mm(PB[3][0:nblk, c:c + HD], hv[:, m, bi, kvh, :], w2v[:, m, :], m == 0, m == 1)
                last.then_inc(s_w2p, 1)

            pe_eng.wait_ge(s_w2e, len(CSTEPS))
            for t in range(PT):
                if t:
                    pe_eng.wait_ge(s_cx, t)
                for h in range(NH):
                    r = slice(HD * (h // NG), HD * (h // NG) + HD)
                    last = mm(PB[h // NG][:, (h % NG) * PBLK:(h % NG + 1) * PBLK], QT[r, h % NG, t * P:(t + 1) * P], KCp[r, :])
                    if h == NG - 1:
                        last.then_inc(s_cs, 1)
                last.then_inc(s_cs, 1)
                pe_eng.wait_ge(s_cpn, t + 1)
                for q4 in range(2):
                    def pc_fill(bank):
                        for k in range(4):
                            h = 4 * q4 + k
                            last = tr(bank[0:PBLK, k * P:(k + 1) * P], PX_c[:, h, :])
                        return last
                    fl = fill(pc_fill)
                pe_eng.wait_ge(s_te, fl)
                if t:
                    pe_eng.wait_ge(s_cou, t)
                for h in range(NH):
                    last = mm(PB[2][:, h * HD:(h + 1) * HD], PT_c[0:PBLK, h, :],
                              VCp[0:PBLK, HD * (h // NG):HD * (h // NG) + HD])
                last.then_inc(s_cpv, 1)

            pe_eng.wait_ge(s_qpt, 1)
            pe_eng.wait_ge(s_cou, PT)
            for G in range(2):
                if G:
                    pe_eng.wait_ge(s_ote, G)
                q32 = [slice(32 * k, 32 * k + 32) for k in range(4)]
                for k in range(4):
                    last = mm(PB[4][q32[k], 0:NBLK], QP[:, 4 * G + k, :], KCm[:, 4 * G + k, :])
                    mm(PB[4][q32[k], 160:192], QP[:, 4 * G + k, :], KTn[:, 1, :])
                    mm(PB[4][q32[k], 192:224], QP[:, 4 * G + k, :], KTn[:, 0, :])
                mm(PB[4][:, 224:248], C("seltok", NS)[:, G * P:(G + 1) * P], gates[0:NS, PT, :]).then_inc(s_gc, 1)
                for k in range(4):
                    b = 4 * G + k
                    pe_eng.wait_ge(s_wk[b % 2], 16 * (b // 2 + 1))

                    def wk_fill(bank):
                        for j in range(4):
                            last = tr(bank[:, j * P:(j + 1) * P], WK[b % 2][:, j * P:(j + 1) * P])
                        return last
                    fl = fill(wk_fill)
                    pe_eng.wait_ge(s_te, fl)
                    mm(PB[5][q32[k], :], QP[:, b, :], KTw).then_inc(s_wku, 1)
                pe_eng.wait_ge(s_gcp, G + 1)
                mm(PB[4][:, 256:256 + NBLK], C("grp"), Pc).then_inc(s_imp, 1)
                fl = fill(lambda bank: tr(bank[0:NBLK, 0:P], Pc))
                pe_eng.wait_ge(s_te, fl)
                pe_eng.wait_ge(s_ic, G + 1)
                for k in range(4):
                    last = mm(PB[4][q32[k], 384:512], PcT[0:NBLK, q32[k]], VCm[0:NBLK, 4 * G + k, :])
                last.then_inc(s_gco, 1)
                for k in range(4):
                    pe_eng.wait_ge(s_ga[g_at % 4], loaded(g_at))
                    rv = ring[g_at % 4]
                    for q4 in range(4):
                        def sk_fill(bank):
                            for j in range(4):
                                c = (4 * q4 + j) * P
                                last = tr(bank[:, j * P:(j + 1) * P], rv[:, c:c + P])
                            return last
                        fl = fill(sk_fill)
                    g_at += 1
                    pe_eng.wait_ge(s_te, fl)
                    for q4 in range(4):
                        last = mm(PB[q4][q32[k], :], QP[:, 4 * G + k, :], KTb[k % 2][:, q4 * 512:(q4 + 1) * 512])
                    last.then_inc(s_rel, 1)
                pe_eng.wait_ge(s_gwx, G + 1)

                def spread(P_, n_old, dst):
                    for q4 in range(n_old // 4):
                        def o_fill(bank):
                            for j in range(4):
                                c = (4 * q4 + j) * P
                                last = tr(bank[:, j * P:(j + 1) * P], P_[:, c:c + P])
                            return last
                        fill(o_fill)
                    return fill(lambda bank: tr(bank[0:NS, 0:P], P_[:, n_old * P:n_old * P + NS]))
                fl = spread(Swin, 4, PTw)
                pe_eng.wait_ge(s_te, fl)
                for k in range(4):
                    b = 4 * G + k
                    pe_eng.wait_ge(s_wv[b % 4], 16 * (b // 4 + 1))
                    for j in range(4):
                        mm(PB[5][q32[k], 128:256], PTw[:, j, q32[k]], WV[b % 4][:, j * P:(j + 1) * P], j == 0, False)
                    last = mm(PB[5][q32[k], 128:256], PTw[0:NS, 4, q32[k]], zkv[0:NS, PT, 640:768], False, True)
                last.then_inc(s_gwo, 1)
                pe_eng.wait_ge(s_gsx, G + 1)
                fl = spread(Sslc, 16, PTs)
                pe_eng.wait_ge(s_te, fl)
                for k in range(4):
                    pe_eng.wait_ge(s_ga[g_at % 4], loaded(g_at))
                    for j in range(16):
                        mm(PB[5][q32[k], 0:128], PTs[:, j, q32[k]], ring[g_at % 4][:, j * P:(j + 1) * P],
                           j == 0, False)
                    last = mm(PB[5][q32[k], 0:128], PTs[0:NS, 16, q32[k]], zkv[0:NS, PT, 384:512], False, True)
                    last.then_inc(s_rel, 1)
                    g_at += 1
                pe_eng.wait_ge(s_oe, G + 1)
                mm(PB[0][0:NS, :], C("seltokT")[:, G * NS:(G + 1) * NS], OE).then_inc(s_ot, 1)

        def nsa_scalar(act):
            sc = nc.scalar

            def drain(dst, src_of, ready=None):
                n = drains[0]
                drains[0] += 1
                act.wait_ge(s_tp, n + 1)
                sc.activation(dst, src_of(PB[6 + n % 2]), ACT.Copy).then_inc(s_te, 1)

            act.wait_ge(s_omix, 1)
            act.wait_ge(s_p2w, P2W)
            act.wait_ge(s_qp, 1)
            act.wait_ge(s_tp, 1)
            for n in range(NKV):
                r = slice(HD * n, HD * n + HD)
                for g in range(NG):
                    dst = QP[r].rearrange("p b (n t g) -> p b n t g", n=NKV, t=DT)[:, :, n, :, g]
                    sc.activation(dst, PB[6][r, g * NS:(g + 1) * NS].rearrange("p (b t) -> p b t", b=DB), ACT.Copy)\
                      .then_inc(s_qpt, 1) if (n, g) == (1, 3) else \
                        sc.activation(dst, PB[6][r, g * NS:(g + 1) * NS].rearrange("p (b t) -> p b t", b=DB),
                                      ACT.Copy)
            drain(KTn, lambda b: b[:, 128:192].rearrange("p (v s) -> p v s", v=2))
            for t in range(PT):
                drain(QT[:, :, t * P:(t + 1) * P], lambda b: b[:, :].rearrange("p (j s) -> p j s", j=4))
                drain(KT[:, :, t * P:(t + 1) * P], lambda b: b[:, 0:256].rearrange("p (v s) -> p v s", v=2))
            for u in range(N_PU + 1):
                if u < N_PU:
                    br, t, h = PU[u]
                    L = (t + 1) * P
                    act.wait_ge(s_nb, u + 1)
                    if u >= 2:
                        act.wait_ge(s_tp, N_Q + u - 1)
                    if h == 0 and u >= 2 * NH:
                        act.wait_ge(s_ou, u // NH - 1)
                    sc.activation(PX[:, u % 2, 0:L], PB[u % 2][:, 0:L], ACT.Exp, bias=nbu[:, u % 4:u % 4 + 1],
                                  scale=SCALE, accum_out=rsu[:, (u // NH) % 2, h:h + 1]).then_inc(s_px, 1)
                if u >= 1:
                    br, t, h = PU[u - 1]
                    if u >= 3:
                        act.wait_ge(s_pv, u - 2)
                    drain(PTb[:, (u - 1) % 2, 0:(t + 1) * P], lambda b: b[:, 0:(t + 1) * P])

            act.wait_ge(s_bias, 1)
            for n, (v, bs) in enumerate(CSTEPS):
                ch = NCH if bs else PCH
                nblk = ch - 1
                nb = len(bs) or 1
                if n:
                    act.wait_ge(s_hp, 2 * n)
                for bi in range(nb):
                    for kvh in range(NKV):
                        for q4 in range(2):
                            drain(CT[:, bi, kvh, 4 * q4:4 * q4 + 4, 0:ch],
                                  lambda b: b[:, :].rearrange("p (k c) -> p k c", k=4)[:, :, 0:ch])
                if n:
                    act.wait_ge(s_w2p, n)
                for m in range(2):
                    act.wait_ge(s_hp, 2 * n + m + 1)
                    w = nb * 2 * nblk
                    sc.activation(hid[:, m, 0:w], PB[m][:, 0:w], ACT.Gelu, bias=biasc[:, 2 * v + m:2 * v + m + 1])\
                      .then_inc(s_hg, 1)
            for t in range(PT):
                act.wait_ge(s_cx, t + 1)
                sc.activation(PX_c, PX_c, ACT.Exp, scale=SCALE).then_inc(s_ce2, 1)
                for q4 in range(2):
                    if t and q4 == 0:
                        act.wait_ge(s_cpv, t)
                    drain(PT_c[0:PBLK, 4 * q4:4 * q4 + 4, :],
                          lambda b: b[0:PBLK, :].rearrange("p (k s) -> p k s", k=4))
            for G in range(2):
                act.wait_ge(s_gcb, G + 1)
                sc.activation(Pc, g4[:, 0:NBLK], ACT.Exp, bias=gst[:, 0:1], scale=SCALE, accum_out=gst[:, 1:2])\
                  .then_inc(s_gcx, 1)
                for k in range(4):
                    if k or G:
                        act.wait_ge(s_wku, 4 * G + k)
                    drain(KTw, lambda b: b[:, :])
                if G:
                    act.wait_ge(s_gco, G)
                drain(PcT[0:NBLK, :], lambda b: b[0:NBLK, 0:P])
                for k in range(4):
                    for q4 in range(4):
                        if k >= 2 and q4 == 0:
                            act.wait_ge(s_rel, 8 * G + k - 1)
                        drain(KTb[k % 2][:, 512 * q4:512 * q4 + 512], lambda b: b[:, :])
                act.wait_ge(s_gwb, G + 1)
                sc.activation(Swin, Swin, ACT.Exp, bias=gst[:, 2:3], scale=SCALE, accum_out=gst[:, 3:4])\
                  .then_inc(s_gwx, 1)
                drain(PTw[:, 0:4, :], lambda b: b[:, :].rearrange("p (k r) -> p k r", k=4))
                drain(PTw[0:NS, 4, :], lambda b: b[0:NS, 0:P])
                act.wait_ge(s_gsb, G + 1)
                sc.activation(Sslc, Sslc, ACT.Exp, bias=gst[:, 4:5], scale=SCALE, accum_out=gst[:, 5:6])\
                  .then_inc(s_gsx, 1)
                for q4 in range(4):
                    drain(PTs[:, 4 * q4:4 * q4 + 4, :], lambda b: b[:, :].rearrange("p (k r) -> p k r", k=4))
                drain(PTs[0:NS, 16, :], lambda b: b[0:NS, 0:P])

        nbu = small[:, 170:174]
        rsu = small[:, 174:190].rearrange("p (z h) -> p z h", z=2)
        rcu = small[:, 190:198]
        gst = small[:, 200:206]
        grow = small[:, 206:209]
        gcoef = small[:, 209:212]
        mx1 = small[:, 212:216]
        c8 = small[:, 216:224]
        PX_c = PX.rearrange("p z s -> p (z s)")[:, 0:NH * PBLK].rearrange("p (h c) -> p h c", h=NH)
        PT_c = PTb.rearrange("p z s -> p (z s)").rearrange("p (h s) -> p h s", h=NH)

        def nsa_vector(dve, link, settle):
            ve = nc.vector
            dve.wait_ge(s_p2w, P2W)
            ve.memset(QP.rearrange("p b r -> p (b r)"), 0.0)
            ve.memset(impp, 0.0).then_inc(s_qp, 1)
            settle(s_qp)
            def combine(bank, t, br, sums, first):
                gv = gates[:, t, :].rearrange("p (h c) -> p h c", h=NH)[:, :, br]
                link(ve.reciprocal(rcu, sums))
                link(ve.tensor_tensor(rcu, rcu, gv, ALU.mult))
                rb = rcu.unsqueeze(2).to_broadcast([P, NH, HD])
                bv = bank[:, :].rearrange("p (h d) -> p h d", h=NH)
                mv = mix[:, t, 0:512].rearrange("p (h d) -> p h d", h=NH)
                if first:
                    return ve.tensor_tensor(mv, bv, rb, ALU.mult)
                tv = tmpo.rearrange("p (h d) -> p h d", h=NH)
                link(ve.tensor_tensor(tv, bv, rb, ALU.mult))
                return ve.tensor_tensor(mv, mv, tv, ALU.add)

            for u in range(N_PU + 3):
                if u < N_PU:
                    br, t, h = PU[u]
                    L = (t + 1) * P
                    dve.wait_ge(s_s, u + 1)
                    dg = PB[u % 2][:, t * P:L]
                    link(ve.tensor_tensor(dg, dg, C("caus"), ALU.add))
                    link(ve.reduce_max(mx1[:, 0:1], PB[u % 2][:, 0:L], axis=AX))
                    ve.tensor_scalar(nbu[:, u % 4:u % 4 + 1], mx1[:, 0:1], -SCALE, None, ALU.mult).then_inc(s_nb, 1)
                    settle(s_nb)
                if u >= 3 and (u - 3) % NH == NH - 1:
                    bt = (u - 3) // NH
                    br, t, h = PU[u - 3]
                    dve.wait_ge(s_pv, NH * (bt + 1))
                    combine(PB[2 + bt % 2], t, 1 + br, rsu[:, bt % 2, :], br == 0).then_inc(s_ou, 1)
                    settle(s_ou)
            dve.wait_ge(s_ou, 2 * PT)
            dve.wait_ge(s_peb, 1)
            ve.tensor_tensor(biasc, PB[4][:, 0:4], b1, ALU.add).then_inc(s_bias, 1)
            settle(s_bias)
            for n, (v, bs) in enumerate(CSTEPS):
                nblk = (NCH if bs else PCH) - 1
                nb = len(bs) or 1
                dve.wait_ge(s_w2p, n + 1)
                if v == 0:
                    dst = KCm[:, bs[0]:bs[0] + 2, :] if bs else KCp.unsqueeze(1)
                    ve.tensor_copy(dst, PB[2][:, 0:nb * nblk].rearrange("p (b c) -> p b c", b=nb)).then_inc(s_w2e, 1)
                    settle(s_w2e)
                else:
                    dst = VCm[0:nblk, bs[0]:bs[0] + 2, :] if bs else VCp[0:nblk, :].unsqueeze(1)
                    ve.tensor_copy(dst, PB[3][0:nblk, 0:nb * P].rearrange("p (b c) -> p b c", b=nb))\
                      .then_inc(s_w2e, 1)
                    settle(s_w2e)
            cadd = C("cadd").rearrange("p (t c) -> p t c", t=PT)
            cval = C("cvalid").rearrange("p (t c) -> p t c", t=PT)
            for t in range(PT):
                sh = [P, NH, PBLK]
                dve.wait_ge(s_cs, 2 * t + 2)
                for n in range(NKV):
                    last = ve.tensor_tensor(PX_c[:, NG * n:NG * n + NG, :],
                                            PB[n][:, 0:NG * PBLK].rearrange("p (h c) -> p h c", h=NG),
                                            cadd[:, t, :].unsqueeze(1).to_broadcast([P, NG, PBLK]), ALU.add)
                link(last)
                link(ve.reduce_max(c8, PX_c, axis=AX))
                ve.tensor_tensor(PX_c, PX_c, c8.unsqueeze(2).to_broadcast(sh), ALU.subtract).then_inc(s_cx, 1)
                settle(s_cx)
                dve.wait_ge(s_ce2, t + 1)
                link(ve.reduce_sum(c8, PX_c, axis=AX))
                ve.tensor_tensor(PX_c, PX_c, cval[:, t, :].unsqueeze(1).to_broadcast(sh), ALU.mult)\
                  .then_inc(s_cpn, 1)
                settle(s_cpn)
                dve.wait_ge(s_cpv, t + 1)
                combine(PB[2], t, 0, c8, False).then_inc(s_cou, 1)
                settle(s_cou)
            dve.wait_ge(s_cou, PT)
            hind = C("hind")
            for G in range(2):
                dve.wait_ge(s_gc, G + 1)
                ve.tensor_copy(g4[:, 0:NBLK], PB[4][:, 0:NBLK])
                link(ve.tensor_copy(g4[:, 160:248], PB[4][:, 160:248]))
                link(ve.reduce_max(mx1[:, 0:1], g4[:, 0:NBLK], axis=AX))
                ve.tensor_scalar(gst[:, 0:1], mx1[:, 0:1], -SCALE, None, ALU.mult).then_inc(s_gcb, 1)
                settle(s_gcb)
                g3 = tmpo[:, 0:24].rearrange("p (c h) -> p c h", c=3)
                link(ve.tensor_tensor(g3, g4[:, 224:248].rearrange("p (h c) -> p c h", c=3),
                                      hind.unsqueeze(1).to_broadcast([P, 3, NH]), ALU.mult))
                link(ve.reduce_sum(grow, g3, axis=AX))
                dve.wait_ge(s_gcx, G + 1)
                link(ve.reciprocal(gcoef[:, 0:1], gst[:, 1:2]))
                ve.tensor_scalar(Pc, Pc, gcoef[:, 0:1], None, ALU.mult).then_inc(s_gcp, 1)
                settle(s_gcp)
                dve.wait_ge(s_wku, 4 * G + 4)
                link(ve.tensor_copy(Swin[:, 0:WIN], PB[5][:, :]))
                first4 = Swin[:, 0:WIN].rearrange("p (k c) -> p k c", k=4)[:, :, 0]
                ve.tensor_tensor(first4, first4, C("winm"), ALU.add)
                newm = C("newm")[:, G * NS:(G + 1) * NS]
                ve.tensor_tensor(Sslc[:, PAST:PAST + NS], g4[:, 192:224], newm, ALU.add)
                link(ve.tensor_tensor(Swin[:, WIN:WIN + NS], g4[:, 160:192], newm, ALU.add))
                link(ve.reduce_max(mx1[:, 1:2], Swin, axis=AX))
                ve.tensor_scalar(gst[:, 2:3], mx1[:, 1:2], -SCALE, None, ALU.mult).then_inc(s_gwb, 1)
                settle(s_gwb)
                dve.wait_ge(s_imp, G + 1)
                ve.tensor_copy(impp[:, 1:1 + NBLK], PB[4][:, 256:256 + NBLK]).then_inc(s_ic, 1)
                settle(s_ic)
                b0, b1_, b2_, t8 = blk[:, 0:NSEL], blk[:, NSEL:2 * NSEL], blk[:, 2 * NSEL:3 * NSEL], blk[:, 99:107]
                link(ve.reduce_sum(b0, impp[:, 0:132].rearrange("p (j k) -> p j k", k=4), axis=AX))
                link(ve.tensor_tensor(b0, b0, impp[:, 4:136].rearrange("p (j k) -> p j k", k=4)[:, :, 0], ALU.add))
                link(ve.tensor_tensor(b0, b0, C("forced"), ALU.max))
                link(ve.max(t8, b0))
                link(ve.match_replace(b1_, t8, b0, NEG))
                link(ve.max(t8, b1_))
                link(ve.match_replace(b2_, t8, b1_, NEG))
                link(ve.tensor_scalar(b2_, b2_, NEG / 10, NEG, ALU.is_gt, ALU.mult))
                dve.wait_ge(s_rel, 8 * G + 4)
                for k in range(4):
                    last = ve.tensor_tensor(
                        Sslc[:, 512 * k:512 * k + 512].rearrange("p (k j c) -> p k j c", k=4, c=4),
                        PB[k][:, :].rearrange("p (k j c) -> p k j c", k=4, c=4),
                        b2_[:, 0:32].unsqueeze(1).unsqueeze(3).to_broadcast([P, 4, 32, 4]), ALU.add)
                link(last)
                link(ve.reduce_max(mx1[:, 2:3], Sslc, axis=AX))
                ve.tensor_scalar(gst[:, 4:5], mx1[:, 2:3], -SCALE, None, ALU.mult).then_inc(s_gsb, 1)
                settle(s_gsb)
                dve.wait_ge(s_gco, G + 1)
                link(ve.tensor_scalar(oacc, PB[4][:, 384:512], grow[:, 0:1], None, ALU.mult))
                dve.wait_ge(s_gwo, G + 1)
                dve.wait_ge(s_rel, 8 * G + 8)
                for k, (br, st, c) in enumerate(((2, 3, 128), (1, 5, 0))):
                    link(ve.reciprocal(gcoef[:, 1 + k:2 + k], gst[:, st:st + 1]))
                    link(ve.tensor_tensor(gcoef[:, 1 + k:2 + k], gcoef[:, 1 + k:2 + k], grow[:, br:br + 1], ALU.mult))
                    link(ve.scalar_tensor_tensor(oacc, PB[5][:, c:c + 128], gcoef[:, 1 + k:2 + k], oacc,
                                                 ALU.mult, ALU.add))
                sh = [P, NG, HD]
                for n in range(NKV):
                    last = ve.tensor_tensor(
                        OE[:, 256 * n:256 * n + 256].rearrange("p (g d) -> p g d", g=NG),
                        oacc[:, HD * n:HD * n + HD].unsqueeze(1).to_broadcast(sh),
                        hind[:, NG * n:NG * n + NG].unsqueeze(2).to_broadcast(sh), ALU.mult)
                last.then_inc(s_oe, 1)
                settle(s_oe)
                dve.wait_ge(s_ot, G + 1)
                mv = mix[0:NS, PT, 0:512]
                if G == 0:
                    ve.tensor_copy(mv, PB[0][0:NS, :]).then_inc(s_ote, 1)
                    settle(s_ote)
                else:
                    ve.tensor_tensor(mv, mv, PB[0][0:NS, :], ALU.add).then_inc(s_ote, 1)
                    settle(s_ote)

        p4 = Place(front + TILES * D)
        g_ln = p4.take(4 * D).rearrange("p (k d) -> p k d", k=4)
        eidx = p4.take(TILES * SLOTS).rearrange("p (t s) -> p t s", t=TILES)
        eidx_u = eidx.bitcast(U32)
        gw = p4.take(TILES * SLOTS).rearrange("p (t s) -> p t s", t=TILES)
        stat = p4.take(TILES * 2 * 16)
        after_ln = p4.at
        wout = p4.take(KC * D).rearrange("p (c n) -> p c n", c=KC)
        mixT = p4.take(2 * 1024).rearrange("p (z c s) -> p z c s", z=2, c=KC)
        p5 = Place(after_ln)
        wpq = p5.take(KC * 2048).rearrange("p (c n) -> p c n", c=KC)
        subk = p5.take(2048).rearrange("p (g k) -> p g k", g=16)
        hT = p5.take(1024).rearrange("p (c s) -> p c s", c=KC)
        qpT = p5.take(2048).rearrange("p (g s) -> p g s", g=16)
        SC = p5.take(2 * 2048).rearrange("p (z g k) -> p z g k", z=2, g=16)
        SC2 = p5.take(2048).rearrange("p (g k) -> p g k", g=16)
        cand = p5.take(2048).rearrange("p (h k) -> p h k", h=PH)
        OH = cand
        OH2 = SC2.rearrange("p g k -> p (g k)")
        topv = p5.take(256).rearrange("p (g k) -> p g k", g=16)
        topi = p5.take(256).rearrange("p (g k) -> p g k", g=16)
        topf = p5.take(256).rearrange("p (g k) -> p g k", g=16)
        fv = p5.take(128).rearrange("p (h k) -> p h k", h=PH)
        fp = p5.take(128).rearrange("p (h k) -> p h k", h=PH)
        fa = p5.take(256).rearrange("p (z s) -> p z s", z=2)
        ff = p5.take(256).rearrange("p (z s) -> p z s", z=2)
        gs8 = p5.take(8)
        assert p5.at <= WORDS
        p6 = Place(after_ln)
        NR = 8
        uv = [p6.take(2 * D) for _ in range(NR)]
        dscr = p6.take(D)
        dots = p6.take(8)
        gel = p6.take(8)
        w8 = p6.take(8)
        diag = [p6.take(128) for _ in range(NR)]
        istage = p6.take(8).bitcast(U32)
        zeros = p6.take(512)
        p6_end = p6.at
        assert p6_end <= WORDS

        s_wo = sem("w_out_loaded")
        s_ln = sem("ln_params_loaded")
        s_wpq = sem("w_pq_loaded")
        s_mo = sem("projected")
        s_lv = sem("ln_variance")
        s_ls = sem("ln_std")
        s_h = sem("h_done")
        s_qf = sem("peer_q_psum")
        s_qe = sem("peer_q_copied")
        s_sf = sem("peer_scores_psum")
        s_se = sem("peer_scores_copied")
        s_tk = sem("peer_scores_used")
        s_gx = sem("peer_gate_exponent")
        s_ge = sem("peer_gate_exp")
        s_idx = sem("peer_tile_retrieved")
        s_free = sem("ring_quarters_free")
        s_stage = sem("indices_staged")
        s_uv = [sem(f"expert_rows_loaded{k}") for k in range(NR)]
        s_dot = sem("dots_done")
        s_gl = sem("gelu_done")
        s_w8 = sem("weights_done")
        s_dg = sem("diagonals_done")
        s_zero = sem("zeros_set")
        s_y = sem("experts_summed")
        s_fin = sem("y_done")

        GATHERS = [SLOTS] * PT + [SLOTS // QB]
        GRP0 = [sum(GATHERS[:t]) // 4 for t in range(TILES)]

        def tail_sync(sp):
            sp.wait_ge(s_ote, 2)
            sp.wait_ge(s_kvo, 32)
            sp.wait_ge(s_out, 16 * (4 + 4 + 2 * DB + 2))
            wo_v = i["w_out"].rearrange("(c p) n -> p c n", p=P)
            for k in range(2):
                sp.dma_start(wout[:, :, k * 512:(k + 1) * 512], wo_v[:, :, k * 512:(k + 1) * 512]).then_inc(s_wo, 16)
            for k in range(4):
                sp.dma_start(g_ln[:, k, :], i["ln"][k:k + 1, :].to_broadcast([P, D])).then_inc(s_ln, 16)
            sp.wait_ge(s_mo, TILES)
            wq_v = i["w_pq"].rearrange("(c p) n -> p c n", p=P)
            sp.dma_start(wpq[:, :, 0:1024], wq_v[:, :, 0:1024]).then_inc(s_wpq, 16)
            sp.dma_start(wpq[:, :, 1024:2048], wq_v[:, :, 1024:2048]).then_inc(s_wpq, 16)
            sp.dma_start(subk, i["subk"]).then_inc(s_wpq, 16)
            for t in range(TILES):
                sp.wait_ge(s_fin, t + 1)
                sp.dma_start(o["y"][t * P:t * P + ROWS[t], :], x_sb[0:ROWS[t], t, :]).then_inc(s_out, 16)
            sp.wait_ge(s_p2w, P2W)
            sp.wait_ge(s_kvo, 32)
            sp.wait_ge(s_out, 16 * (4 + 4 + 2 * DB + 2 + TILES))

        def tail_gpsimd(pool):
            pool.wait_ge(s_idx, TILES)
            for t in range(TILES):
                n_it = GATHERS[t] // 8
                stage_of = eidx_u[:, t, :]
                with pool.Fori(0, n_it) as it:
                    for quarter in range(4):
                        r0 = 2 * quarter
                        pool.wait_ge(s_free, it * 4 + (2 * GRP0[t] + quarter + 1))
                        nc.gpsimd.tensor_copy(istage[:, r0:r0 + 2],
                                              stage_of[:, bass.ds(it * 8 + r0, 2)]).then_inc(s_stage, 1)
                        pool.wait_ge(s_idx, TILES)
                        pool.wait_ge(s_stage, it * 4 + (2 * GRP0[t] + quarter + 1))
                        for r in (r0, r0 + 1):
                            nc.gpsimd.indirect_dma_start(uv[r], None, i["uv"],
                                                         bass.IndirectOffsetOnAxis(istage[:, r:r + 1], 0))\
                                .then_inc(s_uv[r], 16)

        def tail_tensor(pe_eng):
            te = nc.tensor

            def mm(out, l, r, start=True, stop=True):
                return te.matmul(out, l, r, start=start, stop=stop)

            def fill8(src, R, ready=None):
                for q4 in range(2):
                    n = fills[0]
                    fills[0] += 1
                    if n >= 2:
                        pe_eng.wait_ge(s_te, n - 1)
                    for j in range(4):
                        c = (4 * q4 + j) * P
                        last = te.transpose(PB[6 + n % 2][:, j * P:j * P + R], src[0:R, c:c + P], ident[0:R, 0:R])
                    last.then_inc(s_tp, 1)
                return fills[0]

            pe_eng.wait_ge(s_ote, 2)
            fl = fill8(mix[:, 0, :], P)
            for t in range(TILES):
                R = ROWS[t]
                f0 = fl
                if t + 1 < TILES:
                    fl = fill8(mix[:, t + 1, :], ROWS[t + 1])
                pe_eng.wait_ge(s_te, f0)
                pe_eng.wait_ge(s_wo, 32)
                if t:
                    pe_eng.wait_ge(s_lv, t)
                for c2 in range(2):
                    for c in range(KC):
                        last = mm(PB[c2][0:R, :], mixT[:, t % 2, c, 0:R], wout[:, c, c2 * 512:c2 * 512 + 512],
                                  c == 0, c == KC - 1)
                last.then_inc(s_mo, 1)
            pe_eng.wait_ge(s_wpq, 48)
            nq = 0
            for t in range(TILES):
                R = ROWS[t]
                pe_eng.wait_ge(s_h, t + 1)
                fl = fill8(x_sb[:, t, :], R)
                pe_eng.wait_ge(s_te, fl)
                for q4 in range(4):
                    if nq >= 2:
                        pe_eng.wait_ge(s_qe, nq - 1)
                    for j in range(4):
                        for c in range(KC):
                            m0 = (4 * q4 + j) * P
                            last = mm(PB[nq % 2][:, j * P:j * P + R], wpq[:, c, m0:m0 + P], hT[:, c, 0:R],
                                      c == 0, c == KC - 1)
                    last.then_inc(s_qf, 1)
                    nq += 1
                for q4 in range(4):
                    pe_eng.wait_ge(s_qe, 4 * t + q4 + 1)
                    if t:
                        pe_eng.wait_ge(s_se, 4 * (t - 1) + q4 + 1)
                    for j in range(4):
                        g = 4 * q4 + j
                        last = mm(PB[2 + q4][0:R, j * P:(j + 1) * P], qpT[:, g, 0:R], subk[:, g, :])
                    last.then_inc(s_sf, 1)
            pe_eng.wait_ge(s_se, 4 * TILES)
            pe_eng.wait_ge(s_zero, 1)
            for t in range(TILES):
                M = P if t < PT else NS
                if t >= 2:
                    pe_eng.wait_ge(s_lv, TILES + t - 1)
                acc = [PB[2 * (t % 2) + c2][0:M, :] for c2 in range(2)]
                for c4 in range(4 if t == 0 else 2):
                    last = mm(acc[c4 % 2], zeros[:, 0:M], zeros, c4 < 2, False)
                    if t == 0:
                        last.then_inc(s_free, 1)
                with pe_eng.Fori(0, GATHERS[t] // 8) as it:
                    for half in range(2):
                        for k in range(4):
                            r = 4 * half + k
                            pe_eng.wait_ge(s_dg, it * 8 + (4 * GRP0[t] + r + 1))
                            for c2 in range(2):
                                last = te.matmul(acc[c2], diag[r][:, 0:M], uv[r][:, D + c2 * 512:D + c2 * 512 + 512],
                                                 start=False, stop=False, skip_group_check=True)
                            if k % 2:
                                last.then_inc(s_free, 1)
                for c2 in range(2):
                    last = mm(acc[c2], zeros[:, 0:M], zeros, False, True)
                last.then_inc(s_y, 1)

        def tail_scalar(act):
            sc = nc.scalar

            def drain8(dst, R):
                for q4 in range(2):
                    n = drains[0]
                    drains[0] += 1
                    act.wait_ge(s_tp, n + 1)
                    sc.activation(dst[:, 4 * q4:4 * q4 + 4, 0:R],
                                  PB[6 + n % 2][:, :].rearrange("p (c s) -> p c s", c=4)[:, :, 0:R], ACT.Copy)\
                      .then_inc(s_te, 1)

            def std(n):
                act.wait_ge(s_lv, n + 1)
                R = ROWS[n % TILES]
                st = stat[0:R, 16 * n:16 * n + 16]
                sc.activation(st[:, 14:15], st[:, 13:14], ACT.Sqrt, bias=C("eps")[0:R, :]).then_inc(s_ls, 1)

            drain8(mixT[:, 0], P)
            for t in range(TILES):
                if t + 1 < TILES:
                    if t >= 1:
                        act.wait_ge(s_mo, t)
                    drain8(mixT[:, (t + 1) % 2], ROWS[t + 1])
                std(t)
            act.wait_ge(s_wpq, 48)
            nq = 0
            for t in range(TILES):
                R = ROWS[t]
                if t:
                    act.wait_ge(s_qf, 4 * t)
                drain8(hT, R)
                for q4 in range(4):
                    act.wait_ge(s_qf, nq + 1)
                    if t:
                        act.wait_ge(s_sf, 4 * (t - 1) + q4 + 1)
                    sc.activation(qpT[:, 4 * q4:4 * q4 + 4, 0:R],
                                  PB[nq % 2][:, :].rearrange("p (g s) -> p g s", g=4)[:, :, 0:R], ACT.Copy)\
                      .then_inc(s_qe, 1)
                    nq += 1
                for q4 in range(4):
                    act.wait_ge(s_sf, 4 * t + q4 + 1)
                    if t >= 2:
                        act.wait_ge(s_tk, t - 1)
                    sc.activation(SC[0:R, t % 2, 4 * q4:4 * q4 + 4, :],
                                  PB[2 + q4][0:R, :].rearrange("p (g k) -> p g k", g=4), ACT.Copy)\
                      .then_inc(s_se, 1)
                if t:
                    gate_exp(act, sc, t - 1)
            gate_exp(act, sc, TILES - 1)
            for t in range(TILES):
                M = P if t < PT else NS
                idm = ident if t < PT else C("ident4")
                with act.Fori(0, GATHERS[t] // 8) as it:
                    for half in range(2):
                        grp = it * 2 + (GRP0[t] + half + 1)
                        h4 = slice(4 * half, 4 * half + 4)
                        act.wait_ge(s_dot, grp)
                        sc.activation(gel[:, h4], dots[:, h4], ACT.Gelu).then_inc(s_gl, 1)
                        act.wait_ge(s_w8, grp)
                        for k in range(4):
                            r = 4 * half + k
                            if k % 2 == 0:
                                act.wait_ge(s_free, it * 4 + (2 * GRP0[t] + r // 2 + 1))
                            sc.activation(diag[r][:, 0:M], idm, ACT.Copy, scale=w8[:, r:r + 1]).then_inc(s_dg, 1)
                std(TILES + t)

        def gate_exp(act, sc, t):
            act.wait_ge(s_gx, t + 1)
            sc.activation(fv[0:ROWS[t]], fv[0:ROWS[t]], ACT.Exp).then_inc(s_ge, 1)

        def tail_vector(dve, link, settle):
            ve = nc.vector

            def layer_norm(n, add):
                t, which = n % TILES, n // TILES
                R = ROWS[t]
                st = stat[0:R, 16 * n:16 * n + 16]
                for c2 in range(2):
                    xv = x_sb[0:R, t, c2 * 512:c2 * 512 + 512]
                    last = ve.scalar_tensor_tensor(xv, xv, ALPHA, add[c2][0:R, :], ALU.mult, ALU.add)
                link(last)
                for c2 in range(2):
                    last = ve.bn_stats(st[:, 6 * c2:6 * c2 + 6], x_sb[0:R, t, c2 * 512:c2 * 512 + 512])
                link(last)
                ve.bn_aggr(st[:, 12:14], st[:, 0:12].rearrange("p (k s) -> p k s", k=2)).then_inc(s_lv, 1)
                settle(s_lv)
                dve.wait_ge(s_ls, n + 1)
                link(ve.reciprocal(st[:, 15:16], st[:, 14:15]))
                xt = x_sb[0:R, t, :]
                link(ve.tensor_scalar(xt, xt, st[:, 12:13], st[:, 15:16], ALU.subtract, ALU.mult))
                link(ve.tensor_tensor(xt, xt, g_ln[0:R, which, :], ALU.mult))
                return ve.tensor_tensor(xt, xt, g_ln[0:R, 2 + which, :], ALU.add)

            dve.wait_ge(s_x, 32)
            dve.wait_ge(s_ln, 64)
            for t in range(TILES):
                dve.wait_ge(s_mo, t + 1)
                layer_norm(t, PB).then_inc(s_h, 1)
                settle(s_h)
            dve.wait_ge(s_h, TILES)
            dve.wait_ge(s_wpq, 48)

            def top16(n, vals, idx, src, spare, R):
                for k in range(2):
                    from_ = src if k == 0 else spare
                    for g in range(n):
                        last = ve.max(vals[0:R, g, 8 * k:8 * k + 8], from_[:, g, :])
                    link(last)
                    for g in range(n):
                        last = ve.max_index(idx[0:R, g, 8 * k:8 * k + 8], vals[0:R, g, 8 * k:8 * k + 8],
                                            from_[:, g, :])
                        if k == 0:
                            last = ve.match_replace(spare[:, g, :], vals[0:R, g, 0:8], src[:, g, :], NEG * 10)
                    link(last)

            iota_v = C("iota")
            for t in range(TILES):
                R = ROWS[t]
                dve.wait_ge(s_se, 4 * t + 4)
                topiu, fpu = topi.bitcast(U32), fp.bitcast(U32)
                top16(16, topv, topiu, SC[0:R, t % 2], SC2[0:R], R)
                ve.tensor_copy(topf[0:R], topiu[0:R]).then_inc(s_tk, 1)
                settle(s_tk)
                tv = topv[0:R].rearrange("p (h z) k -> p h z k", h=PH)
                tf = topf[0:R].rearrange("p (h z) k -> p h z k", h=PH)
                sh = [R, PH, TOPK, TOPK]
                c4 = cand[0:R].rearrange("p h (a b) -> p h a b", a=TOPK)
                link(ve.tensor_tensor(c4, tv[:, :, 0, :].unsqueeze(3).to_broadcast(sh),
                                      tv[:, :, 1, :].unsqueeze(2).to_broadcast(sh), ALU.add))
                sp2 = SC2[0:R].rearrange("p g k -> p (g k)").rearrange("p (h k) -> p h k", h=PH)
                top16(PH, fv, fpu, cand[0:R], sp2, R)
                fpf = fpu[0:R].rearrange("p h k -> p (h k)")
                fau = fa.bitcast(U32)
                ve.tensor_scalar(fau[0:R, 0, :], fpf, 4, None, ALU.logical_shift_right)
                link(ve.tensor_scalar(fau[0:R, 1, :], fpf, 15, None, ALU.bitwise_and))
                link(ve.tensor_copy(ff[0:R], fau[0:R]))
                s4 = [R, PH, TOPK, TOPK]
                for z in range(2):
                    rk = ff[0:R, z, :].unsqueeze(2).to_broadcast([R, SLOTS, TOPK])
                    oh = OH[0:R].rearrange("p h k -> p (h k)").rearrange("p (s a) -> p s a", a=TOPK)
                    link(ve.tensor_tensor(oh, rk, iota_v[0:R].unsqueeze(1).to_broadcast([R, SLOTS, TOPK]),
                                          ALU.is_equal))
                    o4 = OH[0:R].rearrange("p h (k a) -> p h k a", a=TOPK)
                    link(ve.tensor_tensor(o4, o4, tf[:, :, z, :].unsqueeze(2).to_broadcast(s4), ALU.mult))
                    link(ve.reduce_sum(fa[0:R, z, :], oh, axis=AX))
                dst = eidx_u[0:R, t, :]
                link(ve.scalar_tensor_tensor(fa[0:R, 0, :], fa[0:R, 0, :], float(NK), fa[0:R, 1, :],
                                             ALU.mult, ALU.add))
                link(ve.tensor_copy(dst, fa[0:R, 0, :]))
                link(ve.tensor_copy(gs8[0:R], fv[0:R, :, 0]))
                ve.tensor_tensor(fv[0:R], fv[0:R], gs8[0:R].unsqueeze(2).to_broadcast([R, PH, TOPK]),
                                 ALU.subtract).then_inc(s_gx, 1)
                settle(s_gx)
                dve.wait_ge(s_ge, t + 1)
                link(ve.reduce_sum(gs8[0:R], fv[0:R], axis=AX))
                link(ve.reciprocal(gs8[0:R], gs8[0:R]))
                last = ve.tensor_tensor(gw[0:R, t, :].rearrange("p (h k) -> p h k", h=PH), fv[0:R],
                                        gs8[0:R].unsqueeze(2).to_broadcast([R, PH, TOPK]), ALU.mult)
                if t == PT:
                    link(last)
                    for q in range(1, QB):
                        qr = slice(NS * q, NS * q + NS)
                        ve.tensor_copy(x_sb[qr, PT, :], x_sb[0:NS, PT, :])
                        ve.tensor_copy(gw[qr, PT, 0:NS], gw[0:NS, PT, NS * q:NS * q + NS])
                        last = ve.tensor_copy(eidx_u[qr, PT, 0:NS], eidx_u[0:NS, PT, NS * q:NS * q + NS])
                last.then_inc(s_idx, 1)
                settle(s_idx)
            dve.wait_ge(s_idx, TILES)
            ve.memset(zeros, 0.0).then_inc(s_zero, 1)
            settle(s_zero)

            base_n = 0
            for t in range(TILES):
                with dve.Fori(0, GATHERS[t] // 8) as it:
                    for half in range(2):
                        grp = it * 2 + (GRP0[t] + half + 1)
                        for k in range(4):
                            r = 4 * half + k
                            dve.wait_ge(s_uv[r], it * 16 + (16 * (GRP0[t] // 2) + 16))
                            last = ve.tensor_tensor_reduce(out=dscr, in0=uv[r][:, 0:D], in1=x_sb[:, t, :],
                                                           scale=1.0, scalar=0.0, op0=ALU.mult, op1=ALU.add,
                                                           accum_out=dots[:, r:r + 1])
                            if k < 3:
                                last.then_inc(s_dst, 1)
                                dve.wait_ge(s_dst, it * 6 + (3 * GRP0[t] + 3 * half + k + 1))
                            else:
                                last.then_inc(s_dot, 1)
                                dve.wait_ge(s_dot, grp)
                        dve.wait_ge(s_gl, grp)
                        ve.tensor_tensor(w8[:, 4 * half:4 * half + 4], gel[:, 4 * half:4 * half + 4],
                                         gw[:, t, bass.ds(it * 8 + 4 * half, 4)], ALU.mult).then_inc(s_w8, 1)
                dve.wait_ge(s_y, t + 1)
                layer_norm(TILES + t, [PB[2 * (t % 2)], PB[2 * (t % 2) + 1]]).then_inc(s_fin, 1)
                settle(s_fin)

        s_dst = sem("dot_step")

        block = ctx.enter_context(nc.Block())

        @block.sync
        def _(sp):
            sp.dma_start(xT, i["xT"].rearrange("(c p) s -> p c s", p=P)).then_inc(s_xT, 16)
            w_v = i["w_in"].rearrange("(c p) n -> p c n", p=P)
            for g, (kind, c0, n) in enumerate(GROUPS):
                if g >= 2:
                    used = max(k for k, u in enumerate(units) if u[0] == g - 2) + 1
                    sp.wait_ge(s_zps, used)
                sp.dma_start(wst[g % 2][:, :, 0:n], w_v[:, :, c0:c0 + n]).then_inc(s_w[g % 2], 16)
                if g == 1:
                    sp.dma_start(consts, i["consts"]).then_inc(s_const, 16)
                    sp.dma_start(par, i["par"]).then_inc(s_const, 16)
                    sp.dma_start(b_if, i["b_if"]).then_inc(s_st, 16)
                    sp.dma_start(m0r, i["m0"]).then_inc(s_st, 16)
                    for c in range(KC):
                        sp.dma_start(zspad[:, c, :, 0:3],
                                     i["stconv"][c * P:(c + 1) * P, :].rearrange("p (b j) -> p b j", b=DB))\
                          .then_inc(s_st, 16)
            sp.dma_start(x_sb[:, 0:PT, :], i["x"][0:SEQ, :].rearrange("(t p) d -> p t d", p=P)).then_inc(s_x, 16)
            sp.dma_start(x_sb[0:NS, PT, :], i["x"][SEQ:T, :]).then_inc(s_x, 16)
            sp.wait_ge(s_zps, NU)
            sp.dma_start(C0, i["C0"].rearrange("p (g v) -> p g v", g=32)).then_inc(s_c0, 16)
            sp.wait_ge(s_zev, U_QK)
            sp.dma_start(o["p_conv"].rearrange("(c p) j -> p c j", p=P), zpad[:, :, SEQ:SEQ + 3]).then_inc(s_p2w, 16)
            for c in range(KC):
                sp.dma_start(o["s_conv"][c * P:(c + 1) * P, :].rearrange("p (b j) -> p b j", b=DB),
                             zspad[:, c, :, 4:7]).then_inc(s_p2w, 16)
            sp.wait_ge(s_rows, 1)
            sp.dma_start(o["p_m"], r_m[:, SEQ - 1:SEQ]).then_inc(s_p2w, 16)
            sp.dma_start(o["s_m"], m_last).then_inc(s_p2w, 16)
            sp.wait_ge(s_ce, MH)
            sp.dma_start(o["p_C"], Cout).then_inc(s_p2w, 16)
            sp.wait_ge(s_cue, 11)
            sp.dma_start(o["s_C"].rearrange("p (g v) -> p g v", g=32), C0).then_inc(s_p2w, 16)
            nsa_sync(sp)
            tail_sync(sp)

        @block.tensor
        def _(pe_eng):
            te = nc.tensor

            def mm(out, l, r, start=True, stop=True):
                return te.matmul(out, l, r, start=start, stop=stop)

            pe_eng.wait_ge(s_xT, 16)
            for n, (g, kind, a, what, off) in enumerate(units):
                pe_eng.wait_ge(s_w[g % 2], 16 * (g // 2 + 1))
                if n >= 4:
                    pe_eng.wait_ge(s_zev, n - 3)
                w = wst[g % 2]
                bank = PB[n % 4]
                for c in range(KC):
                    if what == "tile":
                        r0 = a * P
                        cn = GROUPS[g][2]
                        last = mm(bank[0:ROWS[a], 0:cn], xT[:, c, r0:r0 + ROWS[a]], w[:, c, 0:cn],
                                  c == 0, c == KC - 1)
                    else:
                        s0, s1 = (0, SEQ) if what == "prompt" else (SEQ, T)
                        m = P if kind == "qk" else MH
                        last = mm(bank[0:m, 0:s1 - s0], w[:, c, off:off + m], xT[:, c, s0:s1],
                                  c == 0, c == KC - 1)
                last.then_inc(s_zps, 1)

            pe_eng.wait_ge(s_const, 32)
            pe_eng.wait_ge(s_zev, NU)
            pe_eng.wait_ge(s_qk, KC)
            for t in range(PT):
                if t >= 1:
                    pe_eng.wait_ge(s_kte, t)
                for h in range(MH):
                    last = te.transpose(PB[7][:, h * P:(h + 1) * P], qkT[:, MH + h, t * P:(t + 1) * P], ident)
                last.then_inc(s_ktp, 1)
            pe_eng.wait_ge(s_rows, 1)
            pe_eng.wait_ge(s_rexp, 1)
            for q, r in ((0, r_ig), (1, r_ex)):
                for t in range(PT):
                    c0 = (q * PT + t) * MH
                    last = te.transpose(PB[6][:, c0:c0 + MH], r[:, t * P:(t + 1) * P], C("ident")[0:MH, 0:MH])
            last.then_inc(s_colp, 1)
            selh = C("selh", MH).rearrange("p (h s) -> p h s", h=MH)
            mm(PB[0][:, :], selh[:, 0, :], r_b0[:, 0:SEQ]).then_inc(s_bcp, 1)
            for h in range(MH):
                for t in range(PT):
                    n = PT * h + t
                    if n >= 2:
                        pe_eng.wait_ge(s_sw, n - 1)
                    L = SEQ - t * P
                    mm(PB[2 + n % 2][:, 0:L], qkT[:, MH + h, t * P:(t + 1) * P], qkT[:, h, t * P:SEQ])\
                        .then_inc(s_sp, 1)
                if h + 1 < MH:
                    if h >= 1:
                        pe_eng.wait_ge(s_wmin, PT * h)
                    mm(PB[(h + 1) % 2][:, :], selh[:, h + 1, :], r_b0[:, 0:SEQ]).then_inc(s_bcp, 1)
                for t in range(PT):
                    n = PT * h + t
                    pe_eng.wait_ge(s_sw, n + 1)
                    if n >= 2:
                        pe_eng.wait_ge(s_nev, n - 1)
                    for k in range(t + 1):
                        last = mm(PB[4 + n % 2][:, 0:129], SWb[:, k, t * P:(t + 1) * P], v1[:, k, h, :],
                                  k == 0, k == t)
                    last.then_inc(s_np, 1)
            pe_eng.wait_ge(s_cole, 1)
            pe_eng.wait_ge(s_kte, PT)
            for h in range(MH):
                pe_eng.wait_ge(s_kw, PT * (h + 1))
                if h >= 2:
                    pe_eng.wait_ge(s_ce, h - 1)
                for t in range(PT):
                    last = mm(PB[6 + h % 2][:, 0:129], ktok[:, t, h * P:(h + 1) * P],
                              v1[:, t, h, :], t == 0, t == PT - 1)
                last.then_inc(s_cp, 1)
            pe_eng.wait_ge(s_wmin, PT * MH)
            for h in range(MH):
                last = mm(PB[h // 2][:, (h % 2) * 192:(h % 2) * 192 + 192], selh[:, h, :],
                          SR.rearrange("p q s -> p (q s)"))
            last.then_inc(s_bcs, 1)
            pe_eng.wait_ge(s_sw, PT * MH)
            pe_eng.wait_ge(s_prod, 1)
            mm(PB[2][:, 0:128], kcs, qcs)
            mm(PB[2][:, 128:129], prod, C("ones")).then_inc(s_sps, 1)
            pe_eng.wait_ge(s_c0, 16)
            for g in range(32):
                last = mm(PB[3][:, 4 * g:4 * g + 4], C0[:, g, 0:128], qcs[:, 4 * g:4 * g + 4])
            last.then_inc(s_ni, 1)
            pe_eng.wait_ge(s_nev, PT * MH)
            te.transpose(PB[4][:, 0:128], kcs, ident).then_inc(s_kts, 1)
            pe_eng.wait_ge(s_nie, 1)
            te.transpose(PB[5][:, 0:128], numT, ident).then_inc(s_nit, 1)
            pe_eng.wait_ge(s_sws, 1)
            pe_eng.wait_ge(s_kse, 1)
            mm(PB[4][:, 0:129], SWs, v1s).then_inc(s_nin, 1)
            pe_eng.wait_ge(s_vb, 1)
            pe_eng.wait_ge(s_ce, MH)
            VBf = VB.rearrange("p g v -> p (g v)")
            for n in range(11):
                if n >= 2:
                    pe_eng.wait_ge(s_cue, n - 1)
                c0, c1 = n * 387, min(32 * 129, (n + 1) * 387)
                mm(PB[6 + n % 2][:, 0:c1 - c0], kws, VBf[:, c0:c1]).then_inc(s_cup, 1)
            nsa_tensor(pe_eng)
            tail_tensor(pe_eng)

        @block.scalar
        def _(act):
            sc = nc.scalar

            act.wait_ge(s_st, 32 + 16 * KC)
            act.wait_ge(s_pad, 1)
            for n, (g, kind, a, what, off) in enumerate(units):
                act.wait_ge(s_zps, n + 1)
                bank = PB[n % 4]
                if kind == "qk":
                    if what == "prompt":
                        last = sc.activation(zpad[:, a, 3:3 + SEQ], bank[:, :], ACT.Copy)
                    else:
                        last = sc.activation(zspad[:, a, :, 3:7],
                                             bank[:, 0:NS].rearrange("p (b t) -> p b t", b=DB), ACT.Copy)
                elif kind == "if":
                    s0, s1 = (0, SEQ) if what == "prompt" else (SEQ, T)
                    dst = (r_ig, r_f)[a]
                    last = sc.activation(dst[:, s0:s1], bank[0:MH, 0:s1 - s0], ACT.Identity,
                                         bias=b_if[:, a:a + 1])
                elif kind == "v":
                    if a < PT:
                        last = sc.activation(v1[:, a, :, 0:128], bank[:, :].rearrange("p (h v) -> p h v", h=MH),
                                             ACT.Copy)
                    else:
                        for h in range(MH):
                            last = sc.activation(v1s[NS * h:NS * h + NS, 0:128],
                                                 bank[0:NS, h * P:(h + 1) * P], ACT.Copy)
                elif kind == "o":
                    last = sc.activation(zo[0:ROWS[a], a, :], bank[0:ROWS[a], :], ACT.Sigmoid)
                elif kind == "q":
                    last = sc.activation(
                        zq[0:ROWS[a], a, :].rearrange("p (g n d) -> p n g d", g=NG, n=NKV),
                        bank[0:ROWS[a], :].rearrange("p (n g d) -> p n g d", n=NKV, g=NG), ACT.Copy)
                elif kind == "kv":
                    last = sc.activation(zkv[0:ROWS[a], a, 0:512], bank[0:ROWS[a], :], ACT.Copy)
                else:
                    sc.activation(zkv[0:ROWS[a], a, 512:768], bank[0:ROWS[a], 0:256], ACT.Copy)
                    last = sc.activation(gates[0:ROWS[a], a, :], bank[0:ROWS[a], 256:280], ACT.Sigmoid)
                last.then_inc(s_zev, 1)
                if n >= 3 and n % 2 and n // 2 - 1 < KC:
                    c = n // 2 - 1
                    act.wait_ge(s_cv, c + 1)
                    if c >= 2:
                        act.wait_ge(s_qk, c - 1)
                    sc.activation(sg[:, c % 2, :], qkT[:, c, :], ACT.Sigmoid).then_inc(s_sg, 1)
                if n == U_IF + 2:
                    act.wait_ge(s_fabs, 1)
                    sc.activation(r_ex, r_ab, ACT.Exp, scale=-1.0).then_inc(s_act, 1)
                    act.wait_ge(s_act, 1)
                    sc.activation(r_ex, r_ex, ACT.Ln, bias=C("ones", MH)).then_inc(s_fexp, 1)

            for t in range(PT):
                act.wait_ge(s_ktp, t + 1)
                sc.activation(ktok[:, t, :], PB[7][:, :], ACT.Copy).then_inc(s_kte, 1)
            act.wait_ge(s_rows, 1)
            sc.activation(r_ex[:, 0:SEQ], r_m[:, 0:SEQ], ACT.Exp, scale=-1.0)
            sc.activation(SR[:, 2, :], r_m[:, SEQ:T], ACT.Exp, scale=-1.0)
            sc.activation(SR[:, 3:6, :], SR[:, 3:6, :], ACT.Exp).then_inc(s_rexp, 1)
            for n in range(PT * MH):
                L = SEQ - (n % PT) * P
                act.wait_ge(s_wmin, n + 1)
                sc.activation(wt[:, n % 2, 0:L], wt[:, n % 2, 0:L], ACT.Exp).then_inc(s_wexp, 1)
            act.wait_ge(s_wmin, PT * MH)
            sc.activation(wcol[:, 0:16], wcol[:, 0:16], ACT.Exp).then_inc(s_wx, 1)
            for h in range(MH):
                act.wait_ge(s_cp, h + 1)
                sc.activation(Cout[:, h, :], PB[6 + h % 2][:, 0:129], ACT.Copy).then_inc(s_ce, 1)
            act.wait_ge(s_bcs, 1)
            for k in range(2):
                last = sc.activation(BC[:, 2 * k:2 * k + 2, :, :],
                                     PB[k][:, 0:384].rearrange("p (h q s) -> p h q s", h=2, q=6), ACT.Copy)
            last.then_inc(s_bce, 1)
            act.wait_ge(s_sx, 1)
            sc.activation(smt, smt, ACT.Exp).then_inc(s_sxe, 1)
            act.wait_ge(s_ni, 1)
            sc.activation(numT, PB[3][:, 0:128], ACT.Copy).then_inc(s_nie, 1)
            nsa_scalar(act)
            tail_scalar(act)

        @block.vector
        def _(dve):
            ve = nc.vector
            chain = [0]

            def link(ins):
                chain[0] += 1
                ins.then_inc(s_dve, 1)
                dve.wait_ge(s_dve, chain[0])

            settled = {}

            def settle(s):
                settled[s.name] = settled.get(s.name, 0) + 1
                dve.wait_ge(s, settled[s.name])

            ve.memset(v1[:, 0:PT, :, 128:129], 1.0)
            ve.memset(v1s[:, 128:129], 1.0)
            ve.memset(zpad[:, :, 0:3], 0.0).then_inc(s_pad, 1)
            settle(s_pad)
            dve.wait_ge(s_const, 32)
            dve.wait_ge(s_st, 32 + 16 * KC)
            for c in range(KC):
                dve.wait_ge(s_zev, 2 * c + 2)
                d0 = qkT[:, c, 0:SEQ]
                d1 = qkT[:, c, SEQ:T].rearrange("p (b t) -> p b t", b=DB)
                for j in range(4):
                    s0 = zpad[:, c, j:j + SEQ]
                    s1 = zspad[:, c, :, j:j + DT]
                    if j == 0:
                        ve.tensor_scalar(d0, s0, conv_w[:, c, 0:1], conv_b[:, c:c + 1], ALU.mult, ALU.add)
                        link(ve.tensor_scalar(d1, s1, conv_w[:, c, 0:1], conv_b[:, c:c + 1], ALU.mult, ALU.add))
                    else:
                        ve.scalar_tensor_tensor(d0, s0, conv_w[:, c, j:j + 1], d0, ALU.mult, ALU.add)
                        last = ve.scalar_tensor_tensor(d1, s1, conv_w[:, c, j:j + 1], d1, ALU.mult, ALU.add)
                        if j < 3:
                            link(last)
                        else:
                            last.then_inc(s_cv, 1)
                            settle(s_cv)
                if c >= 1:
                    dve.wait_ge(s_sg, c)
                    ve.scalar_tensor_tensor(qkT[:, c - 1, :], qkT[:, c - 1, :], 1.0 if c - 1 < MH else KSCALE,
                                            sg[:, (c - 1) % 2, :], ALU.mult, ALU.mult).then_inc(s_qk, 1)
                    settle(s_qk)
            dve.wait_ge(s_sg, KC)
            ve.scalar_tensor_tensor(qkT[:, KC - 1, :], qkT[:, KC - 1, :], KSCALE, sg[:, (KC - 1) % 2, :],
                                    ALU.mult, ALU.mult).then_inc(s_qk, 1)
            settle(s_qk)
            dve.wait_ge(s_zev, U_IF)
            ve.scalar_tensor_tensor(r_ab, r_f, -1.0, r_f, ALU.mult, ALU.max).then_inc(s_fabs, 1)
            settle(s_fabs)
            dve.wait_ge(s_fexp, 1)
            link(ve.scalar_tensor_tensor(r_b0, r_f, 0.0, r_ex, ALU.min, ALU.subtract))

            def scan(src, other, op):
                d = 1
                while d < SEQ:
                    link(ve.tensor_copy(other[:, 0:d], src[:, 0:d]))
                    ve.tensor_tensor(other[:, d:SEQ], src[:, d:SEQ], src[:, 0:SEQ - d], op)
                    s3 = src[:, SEQ:T].rearrange("p (b t) -> p b t", b=DB)
                    o3 = other[:, SEQ:T].rearrange("p (b t) -> p b t", b=DB)
                    if d < DT:
                        ve.tensor_copy(o3[:, :, 0:d], s3[:, :, 0:d])
                        link(ve.tensor_tensor(o3[:, :, d:DT], s3[:, :, d:DT], s3[:, :, 0:DT - d], op))
                    else:
                        link(ve.tensor_copy(other[:, SEQ:T], src[:, SEQ:T]))
                    src, other = other, src
                    d *= 2
                return src, other

            cum, free = scan(r_b0, r_b1, ALU.add)
            link(ve.tensor_tensor(r_ig, r_ig, cum, ALU.subtract))
            link(ve.tensor_copy(r_f, r_ig))
            mx, _ = scan(r_f, r_ab, ALU.max)
            link(ve.tensor_scalar(mx[:, 0:SEQ], mx[:, 0:SEQ], 0.0, None, ALU.max))
            m03 = m0r.unsqueeze(2).to_broadcast([MH, DB, DT])

            def s3(a):
                return a.rearrange("p (b t) -> p b t", b=DB)

            link(ve.tensor_tensor(s3(mx[:, SEQ:T]), s3(mx[:, SEQ:T]), m03, ALU.max))
            link(ve.tensor_tensor(r_m, mx, cum, ALU.add))
            ve.tensor_copy(m_last, r_m[:, SEQ:T].rearrange("p (b t) -> p b t", b=DB)[:, :, 3])
            link(ve.tensor_scalar(free, mx, -1.0, None, ALU.mult))
            nml = s3(free[:, SEQ:T])[:, :, 3:4].to_broadcast([MH, DB, DT])
            nml_c = small[:, 165:166]
            ve.tensor_copy(SR[:, 0, :], r_ig[:, SEQ:T])
            ve.tensor_copy(SR[:, 1, :], free[:, SEQ:T])
            ve.tensor_tensor(s3(SR[:, 3, :]), s3(free[:, SEQ:T]), m03, ALU.add)
            ve.tensor_tensor(s3(SR[:, 4, :]), s3(r_ig[:, SEQ:T]), nml, ALU.add)
            ve.tensor_tensor(s3(SR[:, 5, :]), nml, m03, ALU.add).then_inc(s_rows, 1)
            settle(s_rows)
            ve.tensor_copy(qcs.rearrange("p (h s) -> p h s", h=MH), qkT[:, 0:MH, SEQ:T])
            link(ve.tensor_copy(kcs.rearrange("p (h s) -> p h s", h=MH), qkT[:, MH:2 * MH, SEQ:T]))
            dve.wait_ge(s_pg, 16)
            ve.tensor_scalar(cidx, pages, 8.0, C("pm8"), ALU.mult, ALU.add).then_inc(s_ci, 1)
            settle(s_ci)
            dve.wait_ge(s_zev, U_KVG)
            cosv = C("cos").rearrange("p (t d) -> p t d", t=TILES)
            sinv = C("sin").rearrange("p (t d) -> p t d", t=TILES)
            for t in range(TILES):
                R = ROWS[t]
                qv = zq[0:R, t, :].rearrange("p (h d) -> p h d", h=NH)
                kv = zkv[0:R, t, :].rearrange("p (b v n d) -> p b v n d", b=3, v=2, n=NKV)[:, :, 0, :, :]
                for x1, x2, shape in ((qv[:, :, 0:32], qv[:, :, 32:64], [R, NH, 32]),
                                      (kv[:, :, :, 0:32], kv[:, :, :, 32:64], [R, 3, NKV, 32])):
                    cs, sn = cosv[0:R, t, :], sinv[0:R, t, :]
                    for _ in shape[1:-1]:
                        cs, sn = cs.unsqueeze(1), sn.unsqueeze(1)
                    cs, sn = cs.to_broadcast(shape), sn.to_broadcast(shape)
                    n = int(np.prod(shape[1:]))

                    def tm(k):
                        a = rtmp[0:R, k, 0:n]
                        return a.rearrange("p (h d) -> p h d", d=32) if len(shape) == 3 else \
                            a.rearrange("p (b n d) -> p b n d", b=3, n=NKV)
                    ve.tensor_tensor(tm(0), x1, cs, ALU.mult)
                    ve.tensor_tensor(tm(1), x2, sn, ALU.mult)
                    ve.tensor_tensor(tm(2), x2, cs, ALU.mult)
                    link(ve.tensor_tensor(tm(3), x1, sn, ALU.mult))
                    ve.tensor_tensor(x1, tm(0), tm(1), ALU.subtract)
                    last = ve.tensor_tensor(x2, tm(2), tm(3), ALU.add)
                    if len(shape) == 3:
                        link(last)
                    else:
                        last.then_inc(s_rope, 1)
                        settle(s_rope)
            dve.wait_ge(s_rope, TILES)

            dve.wait_ge(s_colp, 1)
            ve.tensor_copy(cols, PB[6][:, 0:32].rearrange("p (q t h) -> p q t h", q=2, t=PT)).then_inc(s_cole, 1)
            settle(s_cole)

            NM = PT * MH

            def exponent(n):
                h, t = n // PT, n % PT
                L = SEQ - t * P
                dve.wait_ge(s_bcp, h + 1)
                if t == PT - 1:
                    link(ve.tensor_copy(nml_c, PB[h % 2][:, SEQ - 1:SEQ]))
                    ve.tensor_scalar(wcol[:, 4 * h:4 * h + 4], cols[:, 0, :, h], nml_c, None, ALU.add)
                ve.tensor_scalar(wt[:, n % 2, 0:L], PB[h % 2][:, t * P:SEQ], cols[:, 0, t, h:h + 1], 0.0,
                                 ALU.add, ALU.min).then_inc(s_wmin, 1)
                settle(s_wmin)

            def weighted(n):
                h, t = n // PT, n % PT
                L = SEQ - t * P
                dve.wait_ge(s_wexp, n + 1)
                link(ve.tensor_tensor(wt[:, n % 2, 0:P], wt[:, n % 2, 0:P], C("tri"), ALU.mult))
                dve.wait_ge(s_sp, n + 1)
                if t == 0 and h:
                    dve.wait_ge(s_np, PT * h)
                ve.tensor_tensor(SWb[:, t, t * P:SEQ], PB[2 + n % 2][:, 0:L], wt[:, n % 2, 0:L], ALU.mult)\
                  .then_inc(s_sw, 1)
                settle(s_sw)

            def divide(n):
                h, t = n // PT, n % PT
                bank = PB[4 + n % 2]
                dve.wait_ge(s_np, n + 1)
                d = rs8[:, 2 * (n % 8):2 * (n % 8) + 1]
                link(ve.tensor_copy(d, bank[:, 128:129]))
                link(ve.scalar_tensor_tensor(d, d, -1.0, d, ALU.mult, ALU.max))
                link(ve.tensor_tensor(d, d, cols[:, 1, t, h:h + 1], ALU.max))
                link(ve.reciprocal(d, d))
                ve.scalar_tensor_tensor(mix[:, t, 512 + h * P:512 + (h + 1) * P], bank[:, 0:128], d,
                                        zo[:, t, h * P:(h + 1) * P], ALU.mult, ALU.mult).then_inc(s_nev, 1)
                settle(s_nev)

            dve.wait_ge(s_zev, U_O)
            exponent(0)
            for n in range(NM):
                if n + 1 < NM:
                    exponent(n + 1)
                weighted(n)
                if n % PT == PT - 1:
                    for k in range(n - PT + 1, n + 1):
                        divide(k)
            dve.wait_ge(s_wx, 1)
            dve.wait_ge(s_kte, PT)
            for h in range(MH):
                for t in range(PT):
                    kk = ktok[:, t, h * P:(h + 1) * P]
                    ve.tensor_scalar(kk, kk, wcol[:, 4 * h + t:4 * h + t + 1], None, ALU.mult).then_inc(s_kw, 1)
                    settle(s_kw)
            dve.wait_ge(s_c0, 16)
            ve.tensor_tensor(prod.rearrange("p (g t) -> p g t", t=DT), qcs.rearrange("p (g t) -> p g t", t=DT),
                             C0[:, :, 128:129].to_broadcast([P, 32, DT]), ALU.mult).then_inc(s_prod, 1)
            settle(s_prod)
            dve.wait_ge(s_sps, 1)
            dve.wait_ge(s_bce, 1)
            colv = small[:, 160:164]
            idh = ident.rearrange("p (h s) -> p h s", h=MH)
            for k, q in enumerate((0, 2, 3, 4)):
                link(ve.tensor_tensor(smt.rearrange("p (h s) -> p h s", h=MH), BC[:, :, q, :], idh, ALU.mult))
                link(ve.reduce_sum(colv[:, k:k + 1], smt, axis=AX))
            ve.tensor_scalar(smt.rearrange("p (h s) -> p h s", h=MH), BC[:, :, 1, :], colv[:, 0:1], 0.0,
                             ALU.add, ALU.min).then_inc(s_sx, 1)
            settle(s_sx)
            dve.wait_ge(s_sxe, 1)
            link(ve.tensor_tensor(smt, smt, C("sblk"), ALU.mult))
            ve.tensor_tensor(SWs, PB[2][:, 0:128], smt, ALU.mult).then_inc(s_sws, 1)
            settle(s_sws)
            ve.tensor_tensor(VB, v1s.unsqueeze(1).to_broadcast([P, 32, 129]),
                             C("hb").unsqueeze(2).to_broadcast([P, 32, 129]), ALU.mult).then_inc(s_vb, 1)
            settle(s_vb)
            dve.wait_ge(s_kts, 1)
            ve.tensor_scalar(kws, PB[4][:, 0:128], colv[:, 3:4], None, ALU.mult).then_inc(s_kse, 1)
            settle(s_kse)
            dve.wait_ge(s_nit, 1)
            link(ve.tensor_scalar(h_s, PB[5][:, 0:128], colv[:, 2:3], None, ALU.mult))
            d = small[:, 164:165]
            link(ve.tensor_scalar(d, PB[2][:, 128:129], colv[:, 2:3], None, ALU.mult))
            dve.wait_ge(s_nin, 1)
            link(ve.tensor_tensor(h_s, h_s, PB[4][:, 0:128], ALU.add))
            link(ve.tensor_tensor(d, d, PB[4][:, 128:129], ALU.add))
            link(ve.scalar_tensor_tensor(d, d, -1.0, d, ALU.mult, ALU.max))
            link(ve.tensor_tensor(d, d, colv[:, 1:2], ALU.max))
            link(ve.reciprocal(d, d))
            link(ve.tensor_scalar(h_s, h_s, d, None, ALU.mult))
            for h in range(MH):
                last = ve.tensor_copy(mix[0:NS, PT, 512 + h * P:512 + (h + 1) * P], h_s[NS * h:NS * h + NS, :])
            link(last)
            ve.tensor_tensor(mix[0:NS, PT, 512:1024], mix[0:NS, PT, 512:1024], zo[0:NS, PT, :], ALU.mult)\
              .then_inc(s_omix, 1)
            settle(s_omix)
            wp = BC[:, :, 5, :].rearrange("p h (b t) -> p h b t", b=DB)[:, :, :, 3]
            for h in range(MH):
                cc = C0[:, h * DB:(h + 1) * DB, :]
                last = ve.tensor_tensor(cc, cc, wp[:, h, :].unsqueeze(2).to_broadcast([P, DB, 129]), ALU.mult)
            link(last)
            C0f = C0.rearrange("p g v -> p (g v)")
            for n in range(11):
                dve.wait_ge(s_cup, n + 1)
                c0, c1 = n * 387, min(32 * 129, (n + 1) * 387)
                ve.tensor_tensor(C0f[:, c0:c1], C0f[:, c0:c1], PB[6 + n % 2][:, 0:c1 - c0], ALU.add)\
                  .then_inc(s_cue, 1)
                settle(s_cue)
            nsa_vector(dve, link, settle)
            tail_vector(dve, link, settle)

        @block.gpsimd
        def _(pool):
            nsa_gpsimd(pool)
            tail_gpsimd(pool)


INS = ["x", "xT", "consts", "par", "b_if", "m0", "stconv", "C0", "w_in", "kcmp", "vcmp", "kslc", "vslc", "kwin",
       "vwin", "pages", "w1", "w2", "w2pad", "w_out", "ln", "w_pq", "subk", "uv"]
OUTS = {
    "y": (T, D), "p_kc": (SEQ, 128), "p_vc": (SEQ, 128), "p_ks": (SEQ, 128), "p_vs": (SEQ, 128),
    "p_kw": (SEQ, 128), "p_vw": (SEQ, 128), "p_C": (P, MH, 129), "p_m": (MH, 1), "p_conv": (1024, 3),
    "s_kc": (NS, 128), "s_vc": (NS, 128), "s_ks": (NS, 128), "s_vs": (NS, 128),
    "s_kw": (DB, WIN, 128), "s_vw": (DB, WIN, 128), "s_C": (P, 32 * 129), "s_m": (MH, DB), "s_conv": (1024, 24),
}


def kernel(**a):
    import concourse.bacc as bacc
    from concourse.bass_utils import run_bass_kernel_spmd

    a = {k: np.asarray(v) for k, v in a.items()}
    f = {}
    f["x"] = np.concatenate([a["x_prompt"].reshape(SEQ, D), a["x_sample"].reshape(NS, D)])
    f["xT"] = np.ascontiguousarray(f["x"].T)
    f["consts"] = const_array()
    cols = [a["conv_w"][0].reshape(4, KC, P).transpose(2, 1, 0).reshape(P, -1),
            a["conv_b"][0].reshape(KC, P).T,
            a["b_phi1"][0].reshape(4, P).T,
            a["pe_cmp"][0].reshape(2 * 16, P).T]
    f["par"] = np.concatenate(cols, axis=1)
    f["b_if"] = np.ascontiguousarray(a["b_if"][0].reshape(2, MH).T)
    f["m0"] = np.ascontiguousarray(a["state_m"][0].T)
    f["stconv"] = np.ascontiguousarray(a["state_conv"][0].reshape(DB * 3, 1024).T)
    f["C0"] = np.concatenate([a["state_C"][0].transpose(2, 1, 0, 3),
                              a["state_n"][0].transpose(2, 1, 0)[..., None]], axis=3).reshape(P, 32 * 129)
    f["w_in"] = a["w_in"][0]
    for k in ("k_cmp", "v_cmp"):
        f[k.replace("_", "")] = a["cache_" + k].reshape(POOL * 8, 16, NKV, HD).transpose(0, 2, 1, 3)\
            .reshape(POOL * 8, 2048)
    for k in ("k_slc", "v_slc"):
        f[k.replace("_", "")] = a["cache_" + k].reshape(POOL * 8, 2048)
    f["kwin"] = a["cache_k_win"].reshape(DB, WIN, 128)
    f["vwin"] = a["cache_v_win"].reshape(DB, WIN, 128)
    f["pages"] = np.ascontiguousarray(np.repeat(a["page_table"], 8, axis=1).T)
    f["w1"] = a["w_phi1"][0]
    f["w2"] = a["w_phi2"][0]
    pad = np.zeros((2, 256, 128), np.float32)
    pad[0, :, :HD] = a["w_phi2"][0, 0]
    pad[1, :, HD:] = a["w_phi2"][0, 0]
    f["w2pad"] = pad
    f["w_out"] = a["w_out"][0]
    f["ln"] = np.concatenate([a["ln_g"][0], a["ln_b"][0]])
    f["w_pq"] = a["w_pq"][0]
    f["subk"] = np.ascontiguousarray(a["sub_keys"][0].reshape(16, NK, P).transpose(2, 0, 1))
    f["uv"] = np.concatenate([a["u_tab"][0], a["v_tab"][0]], axis=1)

    nc = bacc.Bacc("TRN2", target_bir_lowering=False, num_devices=1)
    arrays, i, o = {}, {}, {}
    for name in INS:
        x = np.ascontiguousarray(f[name])
        arrays[f"in_{name}"] = x
        i[name] = nc.dram_tensor(f"in_{name}", x.shape, mybir.dt.from_np(x.dtype), kind="ExternalInput").ap()
    for name, shape in OUTS.items():
        o[name] = nc.dram_tensor(f"out_{name}", shape, F32, kind="ExternalOutput").ap()
    program(nc, i, o)
    r = run_bass_kernel_spmd(nc, [arrays], core_ids=[0]).results[0]
    g = {name: np.asarray(r[f"out_{name}"]) for name in OUTS}

    def kv(name, *lead):
        return g[name].reshape(1, *lead, NKV, HD)

    sC = g["s_C"].reshape(P, MH, DB, 129)
    sconv = g["s_conv"].T.reshape(1, DB, 3, 1024)
    return (g["y"][:SEQ].reshape(1, SEQ, D), g["y"][SEQ:].reshape(DB, DT, D),
            *(kv(n, 1, SEQ) for n in ("p_kc", "p_vc", "p_ks", "p_vs", "p_kw", "p_vw")),
            g["p_C"][:, :, :128].transpose(1, 0, 2)[None, None], g["p_C"][:, :, 128].T[None, None],
            g["p_m"].reshape(1, 1, MH), g["p_conv"].T[None, None],
            *(kv(n, DB, DT) for n in ("s_kc", "s_vc", "s_ks", "s_vs")),
            *(kv(n, DB, WIN) for n in ("s_kw", "s_vw")),
            sC[..., :128].transpose(2, 1, 0, 3)[None], sC[..., 128].transpose(2, 1, 0)[None],
            g["s_m"].T[None], sconv)
```

```python
import numpy as np
import concourse.bass as bass
from concourse import mybir
from contextlib import ExitStack

F32 = mybir.dt.float32
U32 = mybir.dt.uint32
I32 = mybir.dt.int32
ALU = mybir.AluOpType
ACT = mybir.ActivationFunctionType
AX = mybir.AxisListType.X

P = 128
D = 1024
KC = D // P
SEQ, DB, DT = 512, 8, 4
PT = SEQ // P
NS = DB * DT
T = SEQ + NS
TILES = PT + 1
ROWS = [P] * PT + [NS]
PAST, PAGE, POOL = 2048, 128, 160
NH, NKV, NG, HD = 8, 2, 4, 64
MH, MD = 4, 128
CB, CS = 32, 16
NCH = PAST // CS
NBLK = NCH - 1
PCH = SEQ // CS
PBLK = PCH - 1
SELB, NSEL, TOPK = 64, 33, 16
WIN = 512
SCALE = HD ** -0.5
KSCALE = MD ** -0.5
ALPHA = 2.0 ** 0.25
EPS = 1e-5
NEG = -1e30
PH, NK = 8, 128
SLOTS = PH * TOPK
QB = P // NS
INW = 3360
CQ, CKV, CQK, CV, CO, CIF = 0, 512, 1304, 2328, 2840, 3352
GROUPS = [("qk", CQK, 512), ("qk", CQK + 512, 512), ("if", CIF, 8), ("v", CV, 512), ("o", CO, 512),
          ("q", CQ, 512), ("kv", CKV, 512), ("kvg", CKV + 512, 280)]


def const_layout():
    at, out = 0, {}
    for name, n in (("ident", 128), ("ident4", 32), ("grp", 128), ("winm", 4), ("newm", 64), ("iota", 16), ("pm8", 1),
                    ("seltok", 256), ("seltokT", 64), ("hind", 8), ("ones", 1), ("forced", NSEL), ("eps", 1),
                    ("cos", TILES * 32), ("sin", TILES * 32), ("tri", 128), ("sblk", 128), ("hb", 32),
                    ("selh", 512), ("caus", 128), ("cvalid", PT * PBLK), ("cadd", PT * PBLK)):
        out[name] = (at, n)
        at += n
    return out, at


CL, CW = const_layout()


def const_array():
    c = np.zeros((P, CW), np.float32)

    def put(name, a):
        at, n = CL[name]
        a = np.asarray(a, np.float32)
        a = a.reshape(a.shape[0], -1)
        c[:a.shape[0], at:at + n] = a

    p = np.arange(P)
    put("ident", np.eye(P))
    put("ident4", p[:, None] % NS == np.arange(NS)[None, :])
    put("caus", np.where(p[None, :] <= p[:, None], 0.0, NEG))
    tok = (np.arange(PT)[None, :, None] * P + p[:, None, None])
    ok = tok >= np.arange(PBLK)[None, None, :] * CS + CB - 1
    put("cvalid", ok)
    put("cadd", np.where(ok, 0.0, NEG))
    half = HD // 2
    inv = np.float32(10000.0) ** (-np.arange(half, dtype=np.float32) / np.float32(half))
    pos = np.zeros((P, TILES), np.float32)
    pos[:, :PT] = np.arange(PT)[None, :] * P + p[:, None]
    pos[:, PT] = PAST + p % DT
    ang = (pos[:, :, None] * inv[None, None, :]).astype(np.float32)
    put("cos", np.cos(ang.astype(np.float64)))
    put("sin", np.sin(ang.astype(np.float64)))
    put("tri", p[:, None] <= p[None, :])
    put("sblk", (p[:, None] // DT == p[None, :] // DT) & (p[:, None] <= p[None, :]))
    put("hb", p[:, None] // DT == np.arange(32)[None, :])
    put("grp", p[:, None] // NG == p[None, :] // NG)
    sel = np.zeros((MH, MH, P))
    for h in range(MH):
        sel[h, h] = 1
    put("selh", sel)
    b4, n, t, g = p // 32, p // 16 % 2, p // 4 % 4, p % 4
    put("winm", np.where(np.arange(4)[None, :] <= t[:, None], NEG, 0.0))
    s = np.arange(NS)
    newm = np.zeros((P, 2, NS))
    seltok = np.zeros((NS, 2, P))
    for G in range(2):
        mine = (s[None, :] // DT == 4 * G + b4[:, None]) & (s[None, :] % DT <= t[:, None])
        newm[:, G] = np.where(mine, 0.0, NEG)
        seltok[:, G] = s[:, None] == ((4 * G + b4) * DT + t)[None, :]
    put("newm", newm)
    put("seltok", seltok)
    put("seltokT", seltok.transpose(2, 1, 0))
    put("iota", np.broadcast_to(np.arange(16), (P, 16)))
    put("pm8", (p % 8)[:, None])
    put("hind", (n * NG + g)[:, None] == np.arange(NH)[None, :])
    put("ones", np.ones((P, 1)))
    f = np.zeros((P, NSEL))
    f[:, [0, NSEL - 2, NSEL - 1]] = 1e30
    put("forced", f)
    put("eps", np.full((P, 1), EPS))
    return c


PARW = KC * 4 + KC + 4 + 2 * 16


def program(nc, i, o):
    ctx = ExitStack()
    with ctx:
        WORDS = 53200
        arena = ctx.enter_context(nc.sbuf_tensor("arena", [P, WORDS], F32))
        PB = [ctx.enter_context(nc.psum_tensor(f"bank{n}", [P, 512], F32)) for n in range(8)]

        def sem(name):
            return ctx.enter_context(nc.semaphore(name))

        class Place:
            def __init__(self, at, end=WORDS):
                self.at, self.end = at, end

            def take(self, n):
                self.at += n
                assert self.at <= self.end, (self.at, self.end)
                return arena[:, self.at - n:self.at]

        base = Place(0)
        consts = base.take(CW)
        par = base.take(PARW)
        x_sb = base.take(TILES * D).rearrange("p (t d) -> p t d", t=TILES)
        small = base.take(262)
        gates = base.take(TILES * 24).rearrange("p (t c) -> p t c", t=TILES)
        mix_s = base.take(D)
        zkv_s = base.take(768)
        QP = base.take(DB * 32).rearrange("p (b r) -> p b r", b=DB)
        KTn = base.take(64).rearrange("p (v s) -> p v s", v=2)
        biasc = base.take(4)
        w2v = base.take(2 * HD).rearrange("p (m d) -> p m d", m=2)
        w2k = base.take(2 * 2 * 128).rearrange("p (n m d) -> p n m d", n=2, m=2)
        long = base.at
        pv_ = Place(long)
        v1 = pv_.take(PT * MH * 129).rearrange("p (t h c) -> p t h c", t=PT, h=MH)
        v1s = pv_.take(129)
        zo = pv_.take(TILES * 512).rearrange("p (t c) -> p t c", t=TILES)
        pl = Place(long)
        g_ln = pl.take(4 * D).rearrange("p (k d) -> p k d", k=4)
        eidx = pl.take(TILES * SLOTS).rearrange("p (t s) -> p t s", t=TILES)
        eidx_u = eidx.bitcast(U32)
        gw = pl.take(TILES * SLOTS).rearrange("p (t s) -> p t s", t=TILES)
        stat = pl.take(TILES * 2 * 16)
        front = max(pv_.at, pl.at)
        pf = Place(front)
        zq_all = pf.take(TILES * 512).rearrange("p (t c) -> p t c", t=TILES)
        mix_p = pf.take(PT * D)
        zkv_p = pf.take(PT * 768).rearrange("p (t c) -> p t c", t=PT)
        zq = [zq_all[:, t, :] for t in range(TILES)]
        mix = [mix_p[:, t * D:(t + 1) * D] for t in range(PT)] + [mix_s]
        zkv = [zkv_p[:, t, :] for t in range(PT)] + [zkv_s]
        mid = pf.at
        p12 = Place(mid)
        zpad = p12.take(KC * (3 + SEQ)).rearrange("p (c s) -> p c s", c=KC)
        zspad = p12.take(KC * DB * 7).rearrange("p (c b s) -> p c b s", c=KC, b=DB)
        qkT = p12.take(KC * T).rearrange("p (c s) -> p c s", c=KC)
        late = p12.at
        p1 = Place(late)
        xT = p1.take(KC * T).rearrange("p (c s) -> p c s", c=KC)
        wst = [p1.take(KC * 512) for _ in range(2)]
        p2 = Place(late, p1.at)
        C0 = p2.take(32 * 129).rearrange("p (g v) -> p g v", g=32)
        VB = p2.take(32 * 129).rearrange("p (g v) -> p g v", g=32)
        BC = p2.take(MH * 192).rearrange("p (h q s) -> p h q s", h=MH, q=6)
        smt = p2.take(128)
        SWs = p2.take(128)
        kws = p2.take(128)
        numT = p2.take(128)
        prod = p2.take(128)
        h_s = p2.take(128)
        Cout = p2.take(MH * 129).rearrange("p (h v) -> p h v", h=MH)
        cols = p2.take(32).rearrange("p (q t h) -> p q t h", q=2, t=PT)
        ktok = p2.take(PT * 512).rearrange("p (t c) -> p t c", t=PT)
        SWb = VB.rearrange("p g v -> p (g v)")[:, 0:PT * 512].rearrange("p (i s) -> p i s", i=PT)
        p2b = Place(p1.at)
        wt = p2b.take(2 * 512).rearrange("p (z s) -> p z s", z=2)
        sg = mix_p[:, 0:2 * T].rearrange("p (z s) -> p z s", z=2)
        rtmp = mix_p[:, 2 * T:2 * T + 1024].rearrange("p (k s) -> p k s", k=4)
        qcs = p2b.take(128)
        kcs = p2b.take(128)
        rows = Place(p2b.at)

        def row(n=T):
            return rows.take(n)[0:MH, :]

        def C(name, parts=P):
            at, n = CL[name]
            return consts[0:parts, at:at + n]

        ident = C("ident")
        conv_w = par[:, 0:32].rearrange("p (c j) -> p c j", c=KC)
        conv_b = par[:, 32:40]
        b1 = par[:, 40:44]
        pe = par[:, 44:76]

        s_const = sem("const_loaded")
        s_x = sem("x_loaded")
        s_xT = sem("xT_loaded")
        s_w = [sem(f"w_in_loaded{k}") for k in range(2)]
        s_st = sem("state_small_loaded")
        s_c0 = sem("C0_loaded")
        s_out = sem("outputs_written")
        s_p2w = sem("states_written")
        P2W = 16 * (1 + KC + 4)
        s_zps = sem("z_in_psum")
        s_zev = sem("z_copied")
        s_pad = sem("conv_pad_set")
        s_dve = sem("vector_step")
        s_act = sem("scalar_step")
        s_cv = sem("conv_done")
        s_sg = sem("conv_sigmoid")
        s_qk = sem("qk_activated")
        s_fabs = sem("f_abs")
        s_fexp = sem("f_exp")
        s_rows = sem("gate_rows_done")
        s_rexp = sem("gate_rows_exp")
        s_ktp = sem("ktok_psum")
        s_kte = sem("ktok_copied")
        s_colp = sem("cols_psum")
        s_cole = sem("cols_copied")
        s_bcp = sem("negM_broadcast")
        s_sp = sem("mlstm_scores_psum")
        s_wmin = sem("mlstm_exponent")
        s_wexp = sem("mlstm_weights")
        s_sw = sem("mlstm_weighted")
        s_np = sem("mlstm_num_psum")
        s_nev = sem("mlstm_num_used")
        s_wx = sem("C_weights")
        s_kw = sem("k_weighted")
        s_cp = sem("C_psum")
        s_ce = sem("C_copied")
        s_bcs = sem("sample_rows_psum")
        s_bce = sem("sample_rows_copied")
        s_sps = sem("sample_scores_psum")
        s_sws = sem("sample_weighted")
        s_sx = sem("sample_exponent")
        s_sxe = sem("sample_weights")
        s_ni = sem("sample_inter_psum")
        s_nie = sem("sample_inter_copied")
        s_prod = sem("sample_qn0")
        s_kts = sem("sample_k_psum")
        s_kse = sem("sample_k_weighted")
        s_nit = sem("sample_inter_T")
        s_nin = sem("sample_num_psum")
        s_vb = sem("v_blocks")
        s_cup = sem("C_update_psum")
        s_cue = sem("C_updated")
        s_omix = sem("mlstm_mix_done")

        units = []
        for g, (kind, c0, n) in enumerate(GROUPS):
            if kind == "qk":
                for c in range(4):
                    units.append((g, kind, 4 * (g % 2) + c, "prompt", c * 128))
                    units.append((g, kind, 4 * (g % 2) + c, "sample", c * 128))
            elif kind == "if":
                for c in range(2):
                    units.append((g, kind, c, "prompt", 4 * c))
                    units.append((g, kind, c, "sample", 4 * c))
            else:
                for t in range(TILES):
                    units.append((g, kind, t, "tile", 0))
        NU = len(units)

        def after_unit(kind):
            return max(n for n, u in enumerate(units) if u[1] == kind) + 1

        U_QK, U_IF, U_V, U_O, U_Q, U_KVG = (after_unit(k) for k in ("qk", "if", "v", "o", "q", "kvg"))

        r_ig, r_f, r_ab, r_ex = row(), row(), row(), row()
        r_b0, r_b1, r_m = row(), row(), row()
        SR = rows.take(6 * NS)[0:MH, :].rearrange("p (q s) -> p q s", q=6)
        wcol = rows.take(3 * PT * MH)
        b_if = small[0:MH, 0:2]
        m0r = small[0:MH, 2:10]
        m_last = small[0:MH, 232:240]
        rs8 = small[:, 16:144]

        p3 = Place(mid)
        W1_p = p3.take(2 * 16 * 256).rearrange("p (v k n) -> p v k n", v=2, k=16)
        ring_p = [p3.take(2048) for _ in range(2)]
        CT_p = p3.take(4096).rearrange("p (b n k c) -> p b n k c", b=2, n=2, k=8)
        hid_p = [p3.take(508) for _ in range(2)]
        KCp = p3.take(PBLK)
        VCp = p3.take(128)
        tmpo_p = p3.take(512)
        QT = p3.take(4 * 512).rearrange("p (j s) -> p j s", j=4)
        KT = p3.take(2 * 512).rearrange("p (v s) -> p v s", v=2)
        PX = p3.take(2 * 512).rearrange("p (z s) -> p z s", z=2)
        PTb = p3.take(2 * 512).rearrange("p (z s) -> p z s", z=2)
        PX_c = PX.rearrange("p z s -> p (z s)")[:, 0:NH * PBLK].rearrange("p (h c) -> p h c", h=NH)
        PT_c = PTb.rearrange("p z s -> p (z s)").rearrange("p (h s) -> p h s", h=NH)
        pidx = small[:, 240:256]
        pages = pidx[:, 0:8].bitcast(I32)
        cidx = pidx[:, 8:16].bitcast(U32)

        p4 = Place(mid)
        wout = p4.take(KC * D).rearrange("p (z c n) -> p z c n", z=2, c=KC)
        mixT = p4.take(2 * 1024).rearrange("p (z c s) -> p z c s", z=2, c=KC)
        SC = arena[:, mid:mid + PT * 2048].rearrange("p (z g k) -> p z g k", z=PT, g=16)
        qpT = mixT.rearrange("p z c s -> p (z c s)").rearrange("p (g s) -> p g s", g=16)
        NR = 8
        ring_at = mid + 10986
        p5w = Place(ring_at)
        wpq = p5w.take(KC * 2048).rearrange("p (z c n) -> p z c n", z=4, c=KC)
        p5 = Place(front, mid)
        subk = p5.take(2048).rearrange("p (g k) -> p g k", g=16)
        hT = p5.take(1024).rearrange("p (c s) -> p c s", c=KC)
        SC2 = p5.take(2048).rearrange("p (g k) -> p g k", g=16)
        cand = p5.take(2048).rearrange("p (h k) -> p h k", h=PH)
        OH = cand
        topv = p5.take(256).rearrange("p (g k) -> p g k", g=16)
        topi = p5.take(256).rearrange("p (g k) -> p g k", g=16)
        topf = p5.take(256).rearrange("p (g k) -> p g k", g=16)
        fv = p5.take(128).rearrange("p (h k) -> p h k", h=PH)
        fp = p5.take(128).rearrange("p (h k) -> p h k", h=PH)
        fa = p5.take(256).rearrange("p (z s) -> p z s", z=2)
        ff = p5.take(256).rearrange("p (z s) -> p z s", z=2)
        acc_v = p5.take(D)

        p6 = Place(ring_at - 8 * 128 - 24)
        dots = p6.take(8)
        gel = p6.take(8)
        w8 = p6.take(8)
        diag = [p6.take(128) for _ in range(NR)]
        uv = [p6.take(2 * D) for _ in range(NR)]

        early = Place(CL["cos"][0], CW)
        KCm = early.take(DB * NBLK).rearrange("p (b c) -> p b c", b=DB)
        Pc = early.take(NBLK)
        impp = early.take(136)
        blk = early.take(3 * NSEL + 16)
        ps = Place(front, mid - D)
        ring_s = [ps.take(2048) for _ in range(2)]
        CT_f = ps.take(4096)
        CT_s = CT_f.rearrange("p (b n k c) -> p b n k c", b=2, n=2, k=8)
        KTb = [CT_f[:, 2048 * z:2048 * z + 2048] for z in range(2)]
        PTs = CT_f[:, 0:17 * P].rearrange("p (k r) -> p k r", k=17)
        pm = Place(mid, ring_at - 8 * 128 - 24)
        W1_s = pm.take(2 * 16 * 256).rearrange("p (v k n) -> p v k n", v=2, k=16)
        hid_s = [ps.take(508), pm.take(508)]
        VCm = pm.take(DB * 128).rearrange("p (b c) -> p b c", b=DB)
        pa = Place(mid, mid + 2 * 16 * 256)
        Sslc = pa.take(PAST + NS)
        Swin = pa.take(WIN + NS)
        PTw = pa.take(5 * P).rearrange("p (k r) -> p k r", k=5)
        PcT = pa.take(P)
        oacc = pa.take(128)
        g4 = pa.take(248)
        OE = pa.take(512)
        g3f = pa.take(24)
        KTw = pa.take(512)
        WK = [pa.take(512) for _ in range(2)]
        WV = [pa.take(512) for _ in range(4)]
        wq_s = [arena[:, mid + 4096 * k:mid + 4096 * k + 4096].rearrange("p (c n) -> p c n", c=KC) for k in range(2)]
        early_s = Place(CL["cos"][0], CW)
        SC_s = [early_s.take(1024)]
        mixT_s = early_s.take(KC * NS).rearrange("p (c s) -> p c s", c=KC)
        pv_s = Place(mid + 8192, ring_at - 8 * 128 - 24)
        SC_s = [a.rearrange("p (g k) -> p g k", g=8) for a in SC_s + [pv_s.take(1024)]]
        qpT_s = pv_s.take(16 * NS).rearrange("p (g s) -> p g s", g=16)

        s_rope = sem("rope_done")
        s_pg = sem("pages_loaded")
        s_ci = sem("chunk_index")
        s_kvo = sem("kv_rows_written")
        s_w1 = sem("w_phi_loaded")
        s_tp = sem("transposes_psum")
        s_te = sem("transposes_copied")
        s_s = sem("attn_scores")
        s_nb = sem("attn_max")
        s_px = sem("attn_probs")
        s_pv = sem("attn_out_psum")
        s_ou = sem("attn_out_used")
        s_ga = [sem(f"chunks_loaded{k}") for k in range(2)]
        s_rel = sem("chunks_used")
        s_peb = sem("pe_bias_psum")
        s_bias = sem("phi_bias")
        s_hp = sem("hidden_psum")
        s_hg = sem("hidden_gelu")
        s_w2p = sem("compressed_psum")
        s_w2e = sem("compressed_copied")
        s_cs = sem("cmp_scores")
        s_cx = sem("cmp_exponent")
        s_ce2 = sem("cmp_exp")
        s_cpn = sem("cmp_probs")
        s_cpv = sem("cmp_out_psum")
        s_cou = sem("cmp_out_used")
        s_gc = sem("g_cmp_scores")
        s_gcb = sem("g_cmp_max")
        s_gcx = sem("g_cmp_exp")
        s_gcp = sem("g_cmp_probs")
        s_imp = sem("g_importance")
        s_wk = [sem(f"win_k_loaded{k}") for k in range(2)]
        s_wv = [sem(f"win_v_loaded{k}") for k in range(4)]
        s_wku = sem("win_k_used")
        s_ic = sem("g_importance_copied")
        s_ss = sem("g_slc_scores")
        s_sev = sem("g_slc_scores_copied")
        s_gwb = sem("g_win_max")
        s_gsb = sem("g_slc_max")
        s_gwx = sem("g_win_exp")
        s_gsx = sem("g_slc_exp")
        s_gco = sem("g_cmp_out")
        s_gwo = sem("g_win_out")
        s_oe = sem("g_out_by_head")
        s_ot = sem("g_out_tokens")
        s_ote = sem("g_out_copied")
        s_qp = sem("q_padded_zero")
        s_qpt = sem("q_padded")
        s_wo = sem("w_out_loaded")
        s_ln = sem("ln_params_loaded")
        s_wpq = [sem(f"w_pq_loaded{k}") for k in range(4)]
        s_sk = sem("sub_keys_loaded")
        s_mo = sem("projected")
        s_lv = sem("ln_variance")
        s_ls = sem("ln_std")
        s_h = sem("h_done")
        s_qf = sem("peer_q_psum")
        s_qe = sem("peer_q_copied")
        s_sf = sem("peer_scores_psum")
        s_se = sem("peer_scores_copied")
        s_tk = sem("peer_scores_used")
        s_gx = sem("peer_gate_exponent")
        s_ge = sem("peer_gate_exp")
        s_idx = sem("peer_tile_retrieved")
        s_free = sem("ring_quarters_multiplied")
        s_vf = sem("ring_rows_added")
        s_uv = [sem(f"expert_rows_loaded{k}") for k in range(NR)]
        s_dot = sem("dots_done")
        s_gl = sem("gelu_done")
        s_w8 = sem("weights_done")
        s_dg = sem("diagonals_done")
        s_y = sem("experts_summed")
        s_fin = sem("y_done")

        PU = [(br, t, h) for br in range(2) for t in range(PT) for h in range(NH)]
        N_PU = len(PU)
        CSTEPS = [(v, b) for b in [()] + [(2 * k, 2 * k + 1) for k in range(DB // 2)] for v in range(2)]
        NC_P, NC_S = 2, len(CSTEPS) - 2
        GA = [("cmp", v, b) for v, bs in CSTEPS for b in (bs or (None,))]
        NCG = len(GA)
        for G in range(2):
            GA += [("slc", v, 4 * G + k) for v in range(2) for k in range(4)]

        K0, PER_STEP, PER_G = 7, 6, 11
        K_ATT = K0 + PER_STEP * NC_S
        K_TAIL = K_ATT + 2 * PER_G
        K_NORM, K_SCORES = K_TAIL + 2, K_TAIL + 7
        N_PIECES = K_TAIL + 14
        WEIGHT = [12] * (K0 - 1) + [4] + ([6] * 2 + [12] * 4) * NC_S + [7, 6, 4, 13, 13, 13, 13, 9, 7, 13, 14] * 2 \
            + [14, 12, 4, 13, 13, 13, 13, 10] + [13] * 6
        GATHERS = [SLOTS] * PT + [SLOTS // QB]
        IT0 = [sum(GATHERS[:t]) // NR for t in range(TILES)]
        N_IT = IT0[PT]

        AFTER = [int((sum(WEIGHT[:k]) + WEIGHT[k] / 2) * (N_IT - 2) / sum(WEIGHT)) for k in range(N_PIECES)]
        assert IT0[PT - 1] <= AFTER[K_NORM] < N_IT - 1

        def pieces_at(j):
            return AFTER.count(j)

        fills = [0]
        drains = [0]
        N_Q = 1 + PT * 2
        chunk_freed = {}

        def loaded(n):
            return 16 * (n // 2 + 2)

        def norm_of(t):
            return PT + t + (1 if t >= PT - 1 else 0)

        def slots_of(j):
            t = max(t for t in range(TILES) if IT0[t] <= j)
            return t, NR * (j - IT0[t])

        nbu = small[:, 170:174]
        rsu = small[:, 174:190].rearrange("p (z h) -> p z h", z=2)
        rcu = small[:, 190:198]
        gst = small[:, 200:206]
        grow = small[:, 206:209]
        gcoef = small[:, 209:212]
        mx1 = small[:, 212:216]
        c8 = small[:, 216:224]
        gs8 = small[:, 224:232]

        KV_OUT = 16 * (4 + 4 + 2 * DB + 2)

        def rest_sync(sp):
            sp.wait_ge(s_rope, TILES)
            for k, name in enumerate(("kc", "vc", "ks", "vs", "kw", "vw")):
                sp.dma_start(o["p_" + name].rearrange("(t p) c -> p t c", p=P),
                             zkv_p[:, :, k * 128:(k + 1) * 128]).then_inc(s_kvo if k < 2 else s_out, 16)
                if k < 4:
                    sp.dma_start(o["s_" + name], zkv_s[0:NS, k * 128:(k + 1) * 128]).then_inc(s_out, 16)
                else:
                    for b in range(DB):
                        sp.dma_start(o["s_" + name][b, WIN - DT:WIN, :],
                                     zkv_s[DT * b:DT * b + DT, k * 128:(k + 1) * 128]).then_inc(s_out, 16)
                    src = i["kwin"] if k == 4 else i["vwin"]
                    sp.dma_start(o["s_" + name][:, 0:WIN - DT, :].rearrange("b (k r) c -> b k (r c)", k=4),
                                 src[:, DT:WIN, :].rearrange("b (k r) c -> b k (r c)", k=4)).then_inc(s_out, 16)
            sp.wait_ge(s_omix, 1)
            sp.wait_ge(s_p2w, P2W)
            for v in range(2):
                sp.dma_start(W1_p[:, v], i["w1"][v].rearrange("p (k n) -> p k n", k=16)).then_inc(s_w1, 16)
            sp.dma_start(w2v, i["w2"][1].rearrange("(m p) d -> p m d", p=P)).then_inc(s_w1, 16)
            for n in range(2):
                sp.dma_start(w2k[:, n], i["w2pad"][n].rearrange("(m p) d -> p m d", p=P)).then_inc(s_w1, 16)
            for k in range(4):
                sp.dma_start(g_ln[:, k, :], i["ln"][k:k + 1, :].to_broadcast([P, D])).then_inc(s_ln, 16)
            def load_w_out():
                for k in range(2):
                    sp.dma_start(wout[:, k], i["w_out"][k].rearrange("p (c n) -> p c n", c=KC)).then_inc(s_wo, 16)

            def load_w_pq(q4, dst):
                sp.dma_start(dst, i["w_pq"][q4].rearrange("p (c n) -> p c n", c=KC)).then_inc(s_wpq[q4], 16)

            sp.wait_ge(s_hp, 2 * NC_P)
            load_w_out()
            sp.wait_ge(s_cou, PT)
            for q4 in range(4):
                load_w_pq(q4, wpq[:, q4])
            sp.wait_ge(s_mo, PT)
            sp.wait_ge(s_kvo, 32)
            sp.wait_ge(s_out, KV_OUT)
            sp.dma_start(subk, i["subk"]).then_inc(s_sk, 16)
            sp.wait_ge(s_idx, PT)
            for v in range(2):
                sp.dma_start(W1_s[:, v], i["w1"][v].rearrange("p (k n) -> p k n", k=16)).then_inc(s_w1, 16)
            sp.wait_ge(s_hp, 2 * len(CSTEPS))
            kw_v = i["kwin"].rearrange("b (c k) d -> b c (k d)", k=4)
            vw_v = i["vwin"].rearrange("b (c k) d -> b c (k d)", k=4)
            for b in range(DB):
                if b >= 2:
                    sp.wait_ge(s_wku, b - 1)
                sp.dma_start(WK[b % 2], kw_v[b]).then_inc(s_wk[b % 2], 16)
                if b >= 4:
                    sp.wait_ge(s_gwo, 1)
                sp.dma_start(WV[b % 4], vw_v[b]).then_inc(s_wv[b % 4], 16)
            sp.wait_ge(s_ote, 2)
            load_w_out()
            sp.dma_start(subk, i["subk"]).then_inc(s_sk, 16)
            sp.wait_ge(s_mo, TILES)
            for q4 in range(4):
                if q4 >= 2:
                    sp.wait_ge(s_qf, 4 * PT + q4 - 1)
                load_w_pq(q4, wq_s[q4 % 2])
            for t in range(TILES):
                sp.wait_ge(s_fin, t + 1)
                sp.dma_start(o["y"][t * P:t * P + ROWS[t], :], x_sb[0:ROWS[t], t, :]).then_inc(s_out, 16)
            sp.wait_ge(s_p2w, P2W)
            sp.wait_ge(s_kvo, 32)
            sp.wait_ge(s_out, KV_OUT + 16 * TILES)

        def rest_gpsimd(pool):
            pool.dma_start(pages, i["pages"]).then_inc(s_pg, 16)
            pool.wait_ge(s_ci, 1)
            pool.wait_ge(s_omix, 1)
            pool.wait_ge(s_p2w, P2W)
            pool.wait_ge(s_kvo, 32)
            for v in range(2):
                rows16 = o[("p_kc", "p_vc")[v]].rearrange("(c k) (n d) -> c n k d", k=CS, n=NKV)
                dst16 = ring_p[v][0:PCH, :].rearrange("p (n k d) -> p n k d", n=NKV, k=CS)
                for kvh in range(NKV):
                    pool.dma_start(dst16[:, kvh], rows16[:, kvh]).then_inc(s_ga[v], 16)
            src = {("cmp", 0): "kcmp", ("cmp", 1): "vcmp", ("slc", 0): "kslc", ("slc", 1): "vslc"}

            def load_chunk(n):
                what, v, b = GA[n]
                if n < NC_P + 2:
                    pool.wait_ge(s_idx, PT)
                elif n - 2 < NCG:
                    pool.wait_ge(s_tp, chunk_freed[n - 2])
                else:
                    pool.wait_ge(s_rel, n - 2 - NCG + 1)
                pool.indirect_dma_start(ring_s[n % 2], None, i[src[(what, v)]],
                                        bass.IndirectOffsetOnAxis(cidx[:, b:b + 1], 0)).then_inc(s_ga[n % 2], 16)

            uses = {NC_P + 2 * st + bi: K0 + PER_STEP * st + bi for st in range(NC_S) for bi in range(2)}
            for G in range(2):
                for k in range(4):
                    uses[NCG + 8 * G + k] = K_ATT + PER_G * G + 3 + k
                    uses[NCG + 8 * G + 4 + k] = K_ATT + PER_G * G + 9 + k // 2
            issue = {}
            for n, used in uses.items():
                j = AFTER[uses.get(n - 2, K0 - 2)] + 1
                assert j <= AFTER[used]
                issue.setdefault(j, []).append(n)

            def iteration(j):
                t, s0 = slots_of(j)
                for r in range(NR):
                    if j and r % 4 == 0:
                        pool.wait_ge(s_free, 2 * (j - 1) + r // 4 + 1)
                    if j and r % 4 == 2:
                        pool.wait_ge(s_vf, 2 * (j - 1) + r // 4 + 1)
                    nc.gpsimd.indirect_dma_start(uv[r], None, i["uv"],
                                                 bass.IndirectOffsetOnAxis(eidx_u[:, t, s0 + r:s0 + r + 1], 0))\
                        .then_inc(s_uv[r], 16)

            pool.wait_ge(s_qf, 4 * PT)
            for j in range(N_IT):
                if j in IT0:
                    pool.wait_ge(s_idx, IT0.index(j) + 1)
                iteration(j)
                for n in issue.get(j, ()):
                    load_chunk(n)
            pool.wait_ge(s_idx, TILES)
            for j in range(N_IT, N_IT + GATHERS[PT] // NR):
                iteration(j)

        def rest_tensor(pe_eng):
            te = nc.tensor

            def mm(out, l, r, start=True, stop=True):
                return te.matmul(out, l, r, start=start, stop=stop)

            def fill(make):
                n = fills[0]
                fills[0] += 1
                if n >= 2:
                    pe_eng.wait_ge(s_te, n - 1)
                make(PB[6 + n % 2]).then_inc(s_tp, 1)
                return n + 1

            def tr(out, in_, parts=P):
                return te.transpose(out, in_, ident[0:parts, 0:parts])

            pe_eng.wait_ge(s_rope, TILES)
            pe_eng.wait_ge(s_p2w, P2W)
            pe_eng.wait_ge(s_omix, 1)

            def sample_q(bank):
                for g in range(NG):
                    tr(bank[:, g * NS:(g + 1) * NS], zq[PT][0:NS, g * P:(g + 1) * P], NS)
                for k, c in enumerate((256, 512)):
                    last = tr(bank[:, 128 + k * NS:128 + (k + 1) * NS], zkv_s[0:NS, c:c + 128], NS)
                return last
            fill(sample_q)
            for t in range(PT):
                def q_fill(bank):
                    for g in range(NG):
                        last = tr(bank[:, g * P:(g + 1) * P], zq[t][:, g * P:(g + 1) * P])
                    return last

                def k_fill(bank):
                    for k, c in enumerate((256, 512)):
                        last = tr(bank[:, k * P:(k + 1) * P], zkv[t][:, c:c + 128])
                    return last
                fill(q_fill)
                fill(k_fill)
            pe_eng.wait_ge(s_te, fills[0])

            at = {}
            for u in range(N_PU + 2):
                if u < N_PU:
                    br, t, h = PU[u]
                    if u >= 2:
                        pe_eng.wait_ge(s_px, u - 1)
                    r = slice(HD * (h // NG), HD * (h // NG) + HD)
                    mm(PB[u % 2][:, 0:(t + 1) * P], QT[r, h % NG, t * P:(t + 1) * P], KT[r, br, 0:(t + 1) * P])\
                        .then_inc(s_s, 1)
                if 1 <= u <= N_PU:
                    br, t, h = PU[u - 1]
                    pe_eng.wait_ge(s_px, u)

                    def p_fill(bank):
                        for k in range(t + 1):
                            last = tr(bank[:, k * P:(k + 1) * P], PX[:, (u - 1) % 2, k * P:(k + 1) * P])
                        return last
                    at[u - 1] = fill(p_fill)
                if u >= 2:
                    br, t, h = PU[u - 2]
                    pe_eng.wait_ge(s_te, at[u - 2])
                    bt = (u - 2) // NH
                    if h == 0 and bt >= 2:
                        pe_eng.wait_ge(s_ou, bt - 1)
                    for k in range(t + 1):
                        c = (3 if br == 0 else 5) * 128 + HD * (h // NG)
                        last = mm(PB[2 + bt % 2][:, h * HD:(h + 1) * HD], PTb[:, (u - 2) % 2, k * P:(k + 1) * P],
                                  zkv[k][:, c:c + HD], k == 0, k == t)
                    last.then_inc(s_pv, 1)

            pe_eng.wait_ge(s_w1, 80)
            for v in range(2):
                for m in range(2):
                    for k in range(16):
                        last = mm(PB[4][:, 2 * v + m:2 * v + m + 1], W1_p[:, v, k, m * P:(m + 1) * P],
                                  pe[:, 16 * v + k:16 * v + k + 1], k == 0, k == 15)
            last.then_inc(s_peb, 1)
            pe_eng.wait_ge(s_ou, 2 * PT)

            def blocks_of(n):
                v, bs = CSTEPS[n]
                ch = NCH if bs else PCH
                return v, bs, len(bs) or 1, ch, ch - 1

            def compress(n):
                v, bs, nb, ch, nblk = blocks_of(n)
                W1, CT = (W1_s, CT_s) if bs else (W1_p, CT_p)
                for bi in range(nb):
                    g = NC_P + 2 * (n - NC_P) + bi if bs else n
                    pe_eng.wait_ge(s_ga[g % 2], loaded(g))
                    rows_v = (ring_s if bs else ring_p)[g % 2].rearrange("p (n k c) -> p n k c", n=NKV, k=8)
                    for kvh in range(NKV):
                        for q4 in range(2):
                            def c_fill(bank):
                                for k in range(4):
                                    last = tr(bank[:, k * P:k * P + ch], rows_v[0:ch, kvh, 4 * q4 + k, :], ch)
                                return last
                            fl = fill(c_fill)
                    chunk_freed[g] = fl
                    yield
                pe_eng.wait_ge(s_te, fl)
                for m in range(2):
                    if n >= 1:
                        pe_eng.wait_ge(s_hg, 2 * (n - 1) + m + 1)
                    for k in range(16):
                        off = k // 8
                        last = mm(PB[2 + m][:, 0:nb * 2 * nblk].rearrange("p (b n c) -> p b n c", b=nb, n=2),
                                  W1[:, v, k, m * P:(m + 1) * P], CT[:, 0:nb, :, k % 8, off:off + nblk],
                                  k == 0, k == 15)
                        if k == 15:
                            last.then_inc(s_hp, 1)
                        if k % 8 == 7:
                            yield

            def compress_out(n):
                v, bs, nb, ch, nblk = blocks_of(n)
                hid = hid_s if bs else hid_p
                pe_eng.wait_ge(s_hg, 2 * n + 2)
                if n >= 2:
                    pe_eng.wait_ge(s_w2e, n - 1)
                hv = [a[:, 0:nb * 2 * nblk].rearrange("p (b n c) -> p b n c", b=nb, n=2) for a in hid]
                if v == 0:
                    for k in range(4):
                        kvh, m = k // 2, k % 2
                        last = mm(PB[4][:, 0:nb * nblk].rearrange("p (b c) -> p b c", b=nb), w2k[:, kvh, m, :],
                                  hv[m][:, :, kvh, :], k == 0, k == 3)
                else:
                    for bi in range(nb):
                        for kvh in range(2):
                            c = (2 * bi + kvh) * HD
                            for m in range(2):
                                last = mm(PB[5][0:nblk, c:c + HD], hv[m][:, bi, kvh, :], w2v[:, m, :], m == 0, m == 1)
                last.then_inc(s_w2p, 1)

            for n in range(NC_P):
                for _ in compress(n):
                    pass
                compress_out(n)

            pe_eng.wait_ge(s_w2e, NC_P)
            for t in range(PT):
                if t:
                    pe_eng.wait_ge(s_cx, t)
                for h in range(NH):
                    r = slice(HD * (h // NG), HD * (h // NG) + HD)
                    last = mm(PB[h // NG][:, (h % NG) * PBLK:(h % NG + 1) * PBLK],
                              QT[r, h % NG, t * P:(t + 1) * P], KCp[r, :])
                    if h == NG - 1:
                        last.then_inc(s_cs, 1)
                last.then_inc(s_cs, 1)
                pe_eng.wait_ge(s_cpn, t + 1)
                for q4 in range(2):
                    def pc_fill(bank):
                        for k in range(4):
                            last = tr(bank[0:PBLK, k * P:(k + 1) * P], PX_c[:, 4 * q4 + k, :])
                        return last
                    fl = fill(pc_fill)
                pe_eng.wait_ge(s_te, fl)
                if t:
                    pe_eng.wait_ge(s_cou, t)
                for h in range(NH):
                    last = mm(PB[2][:, h * HD:(h + 1) * HD], PT_c[0:PBLK, h, :],
                              VCp[0:PBLK, HD * (h // NG):HD * (h // NG) + HD])
                last.then_inc(s_cpv, 1)

            def fill8(src, R):
                for q4 in range(2):
                    def block_fill(bank):
                        for j in range(4):
                            c = (4 * q4 + j) * P
                            last = te.transpose(bank[:, j * P:j * P + R], src[0:R, c:c + P], ident[0:R, 0:R])
                        return last
                    fl = fill(block_fill)
                return fl

            def project(t, transposed):
                R = ROWS[t]
                pe_eng.wait_ge(s_te, transposed)
                for c2 in range(2):
                    for c in range(KC):
                        last = mm(PB[c2][0:R, :], mixT[:, t % 2, c, 0:R], wout[:, c2, c, :],
                                  c == 0, c == KC - 1)
                last.then_inc(s_mo, 1)

            def query(t):
                R = ROWS[t]
                pe_eng.wait_ge(s_h, t + 1)
                fl = fill8(x_sb[:, t, :], R)
                pe_eng.wait_ge(s_te, fl)
                for q4 in range(4):
                    nq = 4 * t + q4
                    pe_eng.wait_ge(s_wpq[q4], 16)
                    if nq >= 2:
                        pe_eng.wait_ge(s_qe, nq - 1)
                    for j in range(4):
                        for c in range(KC):
                            last = mm(PB[nq % 2][:, j * P:j * P + R], wpq[:, q4, c, j * P:j * P + P], hT[:, c, 0:R],
                                      c == 0, c == KC - 1)
                    last.then_inc(s_qf, 1)
                pe_eng.wait_ge(s_sk, 16)
                for q4 in range(4):
                    pe_eng.wait_ge(s_qe, 4 * t + q4 + 1)
                    if t:
                        pe_eng.wait_ge(s_se, 4 * (t - 1) + q4 + 1)
                    for j in range(4):
                        g = 4 * q4 + j
                        last = mm(PB[2 + q4][0:R, j * P:(j + 1) * P], qpT[:, g, 0:R], subk[:, g, :])
                    last.then_inc(s_sf, 1)

            pe_eng.wait_ge(s_cou, PT)
            fl = fill8(mix[0], P)
            for t in range(PT):
                f0 = fl
                if t + 1 < PT:
                    fl = fill8(mix[t + 1], P)
                pe_eng.wait_ge(s_wo, 32)
                if t:
                    pe_eng.wait_ge(s_lv, t)
                project(t, f0)
            pe_eng.wait_ge(s_h, PT)
            for t in range(PT):
                query(t)

            def pieces():
                for _ in range(K0):
                    yield
                pe_eng.wait_ge(s_w1, 112)
                for n in range(NC_P, len(CSTEPS)):
                    if n > NC_P:
                        compress_out(n - 1)
                    yield from compress(n)
                compress_out(len(CSTEPS) - 1)
                pe_eng.wait_ge(s_w2e, len(CSTEPS))
                pe_eng.wait_ge(s_qpt, 1)
                q32 = [slice(32 * k, 32 * k + 32) for k in range(4)]
                for G in range(2):
                    g_at = NCG + 8 * G
                    if G:
                        pe_eng.wait_ge(s_ote, G)
                    for k in range(4):
                        mm(PB[4][q32[k], 0:NBLK], QP[:, 4 * G + k, :], KCm[:, 4 * G + k, :])
                        mm(PB[4][q32[k], 160:192], QP[:, 4 * G + k, :], KTn[:, 1, :])
                        mm(PB[4][q32[k], 192:224], QP[:, 4 * G + k, :], KTn[:, 0, :])
                    mm(PB[4][:, 224:248], C("seltok", NS)[:, G * P:(G + 1) * P], gates[0:NS, PT, :]).then_inc(s_gc, 1)
                    for k in range(4):
                        b = 4 * G + k
                        pe_eng.wait_ge(s_wk[b % 2], 16 * (b // 2 + 1))

                        def wk_fill(bank):
                            for j in range(4):
                                last = tr(bank[:, j * P:(j + 1) * P], WK[b % 2][:, j * P:(j + 1) * P])
                            return last
                        fl = fill(wk_fill)
                        pe_eng.wait_ge(s_te, fl)
                        mm(PB[5][q32[k], :], QP[:, b, :], KTw).then_inc(s_wku, 1)
                        if k % 2:
                            yield
                    pe_eng.wait_ge(s_gcp, G + 1)
                    mm(PB[4][:, 256:256 + NBLK], C("grp"), Pc).then_inc(s_imp, 1)
                    fl = fill(lambda bank: tr(bank[0:NBLK, 0:P], Pc))
                    pe_eng.wait_ge(s_te, fl)
                    pe_eng.wait_ge(s_ic, G + 1)
                    for k in range(4):
                        last = mm(PB[4][q32[k], 384:512], PcT[0:NBLK, q32[k]], VCm[0:NBLK, 4 * G + k, :])
                    last.then_inc(s_gco, 1)
                    yield
                    for k in range(4):
                        g = g_at + k
                        pe_eng.wait_ge(s_ga[g % 2], loaded(g))
                        for q4 in range(4):
                            def sk_fill(bank):
                                for j in range(4):
                                    c = (4 * q4 + j) * P
                                    last = tr(bank[:, j * P:(j + 1) * P], ring_s[g % 2][:, c:c + P])
                                return last
                            fl = fill(sk_fill)
                        pe_eng.wait_ge(s_te, fl)
                        for q4 in range(4):
                            if q4 >= 2:
                                pe_eng.wait_ge(s_sev, 4 * (4 * G + k) + q4 - 1)
                            last = mm(PB[2 + q4 % 2][q32[k], :], QP[:, 4 * G + k, :],
                                      KTb[k % 2][:, q4 * 512:(q4 + 1) * 512])
                            last.then_inc(s_ss if q4 < 3 else s_rel, 1)
                        yield

                    def spread(P_, n_old):
                        for q4 in range(n_old // 4):
                            def o_fill(bank):
                                for j in range(4):
                                    c = (4 * q4 + j) * P
                                    last = tr(bank[:, j * P:(j + 1) * P], P_[:, c:c + P])
                                return last
                            fill(o_fill)
                        return fill(lambda bank: tr(bank[0:NS, 0:P], P_[:, n_old * P:n_old * P + NS]))
                    pe_eng.wait_ge(s_gwx, G + 1)
                    fl = spread(Swin, 4)
                    pe_eng.wait_ge(s_te, fl)
                    for k in range(4):
                        b = 4 * G + k
                        pe_eng.wait_ge(s_wv[b % 4], 16 * (b // 4 + 1))
                        for j in range(4):
                            mm(PB[5][q32[k], 128:256], PTw[:, j, q32[k]], WV[b % 4][:, j * P:(j + 1) * P], j == 0, False)
                        last = mm(PB[5][q32[k], 128:256], PTw[0:NS, 4, q32[k]], zkv_s[0:NS, 640:768], False, True)
                    last.then_inc(s_gwo, 1)
                    yield
                    pe_eng.wait_ge(s_gsx, G + 1)
                    fl = spread(Sslc, 16)
                    yield
                    pe_eng.wait_ge(s_te, fl)
                    for k in range(4):
                        g = g_at + 4 + k
                        pe_eng.wait_ge(s_ga[g % 2], loaded(g))
                        for j in range(16):
                            mm(PB[5][q32[k], 0:128], PTs[:, j, q32[k]], ring_s[g % 2][:, j * P:(j + 1) * P],
                               j == 0, False)
                        last = mm(PB[5][q32[k], 0:128], PTs[0:NS, 16, q32[k]], zkv_s[0:NS, 384:512], False, True)
                        last.then_inc(s_rel, 1)
                        if k == 1:
                            yield
                    pe_eng.wait_ge(s_oe, G + 1)
                    mm(PB[2][0:NS, :], C("seltokT")[:, G * NS:(G + 1) * NS], OE).then_inc(s_ot, 1)
                    yield
                pe_eng.wait_ge(s_ote, 2)
                fl = fill8(mix_s, NS)
                pe_eng.wait_ge(s_te, fl)
                pe_eng.wait_ge(s_wo, 64)
                for c2 in range(2):
                    for c in range(KC):
                        last = mm(PB[2 + c2][0:NS, :], mixT_s[:, c, :], wout[:, c2, c, :],
                                  c == 0, c == KC - 1)
                    if c2 == 1:
                        last.then_inc(s_mo, 1)
                    yield
                yield
                pe_eng.wait_ge(s_h, TILES)
                fl = fill8(x_sb[:, PT, :], NS)
                pe_eng.wait_ge(s_te, fl)
                for q4 in range(4):
                    pe_eng.wait_ge(s_wpq[q4], 32)
                    if q4 >= 2:
                        pe_eng.wait_ge(s_qe, 4 * PT + q4 - 1)
                    for j in range(4):
                        for c in range(KC):
                            last = mm(PB[2 + q4 % 2][:, j * NS:(j + 1) * NS], wq_s[q4 % 2][:, c, j * P:(j + 1) * P],
                                      hT[:, c, 0:NS], c == 0, c == KC - 1)
                    last.then_inc(s_qf, 1)
                    yield
                pe_eng.wait_ge(s_sk, 32)
                pe_eng.wait_ge(s_qe, 4 * TILES)
                for q4 in range(4):
                    if q4 >= 2:
                        pe_eng.wait_ge(s_se, 4 * PT + q4 - 1)
                    for j in range(4):
                        g = 4 * q4 + j
                        last = mm(PB[4 + q4 % 2][0:NS, j * P:(j + 1) * P], qpT_s[:, g, :], subk[:, g, :])
                    last.then_inc(s_sf, 1)
                for _ in range(K_SCORES, N_PIECES):
                    yield

            def iteration(j):
                t, s0 = slots_of(j)
                M = ROWS[t]
                n = 0
                for r in (0, 1, 4, 5):
                    n += 1
                    pe_eng.wait_ge(s_dg, 4 * j + n)
                    for c2 in range(2):
                        last = mm(PB[c2][0:M, :], diag[r][:, 0:M], uv[r][:, D + c2 * 512:D + c2 * 512 + 512],
                                  s0 + r == 0, False)
                    if r % 4 == 1:
                        last.then_inc(s_free, 1)
                if s0 == GATHERS[t] - NR:
                    pe_eng.wait_ge(s_vf, 2 * (j + 1))
                    for c2 in range(2):
                        last = mm(PB[c2][0:M, :], (ident if t < PT else C("ident4"))[:, 0:M],
                                  acc_v[:, c2 * 512:c2 * 512 + 512], False, True)
                    last.then_inc(s_y, 1)

            pe_eng.wait_ge(s_qe, 4 * PT)
            todo = pieces()
            for j in range(N_IT):
                if j in IT0[1:]:
                    pe_eng.wait_ge(s_lv, PT + IT0.index(j))
                iteration(j)
                for _ in range(pieces_at(j)):
                    next(todo)
            pe_eng.wait_ge(s_lv, 2 * PT + 1)
            for j in range(N_IT, N_IT + GATHERS[PT] // NR):
                iteration(j)

        def rest_scalar(act):
            sc = nc.scalar

            def drain(dst, src_of):
                n = drains[0]
                drains[0] += 1
                act.wait_ge(s_tp, n + 1)
                sc.activation(dst, src_of(PB[6 + n % 2]), ACT.Copy).then_inc(s_te, 1)

            act.wait_ge(s_omix, 1)
            act.wait_ge(s_p2w, P2W)
            act.wait_ge(s_qp, 1)
            act.wait_ge(s_tp, 1)
            for n in range(NKV):
                r = slice(HD * n, HD * n + HD)
                for g in range(NG):
                    dst = QP[r].rearrange("p b (n t g) -> p b n t g", n=NKV, t=DT)[:, :, n, :, g]
                    last = sc.activation(dst, PB[6][r, g * NS:(g + 1) * NS].rearrange("p (b t) -> p b t", b=DB),
                                         ACT.Copy)
            last.then_inc(s_qpt, 1)
            drain(KTn, lambda b: b[:, 128:192].rearrange("p (v s) -> p v s", v=2))
            for t in range(PT):
                drain(QT[:, :, t * P:(t + 1) * P], lambda b: b[:, :].rearrange("p (j s) -> p j s", j=4))
                drain(KT[:, :, t * P:(t + 1) * P], lambda b: b[:, 0:256].rearrange("p (v s) -> p v s", v=2))
            for u in range(N_PU + 1):
                if u < N_PU:
                    br, t, h = PU[u]
                    L = (t + 1) * P
                    act.wait_ge(s_nb, u + 1)
                    if u >= 2:
                        act.wait_ge(s_tp, N_Q + u - 1)
                    if h == 0 and u >= 2 * NH:
                        act.wait_ge(s_ou, u // NH - 1)
                    sc.activation(PX[:, u % 2, 0:L], PB[u % 2][:, 0:L], ACT.Exp, bias=nbu[:, u % 4:u % 4 + 1],
                                  scale=SCALE, accum_out=rsu[:, (u // NH) % 2, h:h + 1]).then_inc(s_px, 1)
                if u >= 1:
                    br, t, h = PU[u - 1]
                    if u >= 3:
                        act.wait_ge(s_pv, u - 2)
                    drain(PTb[:, (u - 1) % 2, 0:(t + 1) * P], lambda b: b[:, 0:(t + 1) * P])

            def compress(n):
                v, bs = CSTEPS[n]
                nb = len(bs) or 1
                ch = NCH if bs else PCH
                CT, hid = (CT_s, hid_s) if bs else (CT_p, hid_p)
                if n:
                    act.wait_ge(s_hp, 2 * n)
                for bi in range(nb):
                    for kvh in range(NKV):
                        for q4 in range(2):
                            drain(CT[:, bi, kvh, 4 * q4:4 * q4 + 4, 0:ch],
                                  lambda b: b[:, :].rearrange("p (k c) -> p k c", k=4)[:, :, 0:ch])
                    yield
                if n:
                    act.wait_ge(s_w2p, n)
                for m in range(2):
                    yield
                    act.wait_ge(s_hp, 2 * n + m + 1)
                    w = nb * 2 * (ch - 1)
                    sc.activation(hid[m][:, 0:w], PB[2 + m][:, 0:w], ACT.Gelu, bias=biasc[:, 2 * v + m:2 * v + m + 1])\
                      .then_inc(s_hg, 1)
                    yield

            act.wait_ge(s_bias, 1)
            for n in range(NC_P):
                for _ in compress(n):
                    pass
            for t in range(PT):
                act.wait_ge(s_cx, t + 1)
                sc.activation(PX_c, PX_c, ACT.Exp, scale=SCALE).then_inc(s_ce2, 1)
                for q4 in range(2):
                    if t and q4 == 0:
                        act.wait_ge(s_cpv, t)
                    drain(PT_c[0:PBLK, 4 * q4:4 * q4 + 4, :],
                          lambda b: b[0:PBLK, :].rearrange("p (k s) -> p k s", k=4))

            def drain8(dst, R):
                for q4 in range(2):
                    drain(dst[:, 4 * q4:4 * q4 + 4, 0:R],
                          lambda b: b[:, :].rearrange("p (c s) -> p c s", c=4)[:, :, 0:R])

            def std(n, R):
                act.wait_ge(s_lv, n + 1)
                st = stat[0:R, 16 * n:16 * n + 16]
                sc.activation(st[:, 14:15], st[:, 13:14], ACT.Sqrt, bias=C("eps")[0:R, :]).then_inc(s_ls, 1)

            def query(t):
                R = ROWS[t]
                if t:
                    act.wait_ge(s_qf, 4 * t)
                drain8(hT, R)
                for q4 in range(4):
                    nq = 4 * t + q4
                    act.wait_ge(s_qf, nq + 1)
                    if t:
                        act.wait_ge(s_sf, 4 * (t - 1) + q4 + 1)
                    sc.activation(qpT[:, 4 * q4:4 * q4 + 4, 0:R],
                                  PB[nq % 2][:, :].rearrange("p (g s) -> p g s", g=4)[:, :, 0:R], ACT.Copy)\
                      .then_inc(s_qe, 1)
                for q4 in range(4):
                    act.wait_ge(s_sf, 4 * t + q4 + 1)
                    sc.activation(SC[0:R, t % PT, 4 * q4:4 * q4 + 4, :],
                                  PB[2 + q4][0:R, :].rearrange("p (g k) -> p g k", g=4), ACT.Copy)\
                      .then_inc(s_se, 1)

            def gate_exp(t):
                act.wait_ge(s_gx, t + 1)
                sc.activation(fv[0:ROWS[t]], fv[0:ROWS[t]], ACT.Exp).then_inc(s_ge, 1)

            drain8(mixT[:, 0], P)
            for t in range(PT):
                if t + 1 < PT:
                    if t >= 1:
                        act.wait_ge(s_mo, t)
                    drain8(mixT[:, (t + 1) % 2], P)
                std(t, P)
            for t in range(PT):
                query(t)
                if t:
                    gate_exp(t - 1)

            def pieces():
                for k in range(K0):
                    if k == K0 - 2:
                        gate_exp(PT - 1)
                    yield
                for n in range(NC_P, len(CSTEPS)):
                    yield from compress(n)
                for G in range(2):
                    act.wait_ge(s_gcb, G + 1)
                    sc.activation(Pc, g4[:, 0:NBLK], ACT.Exp, bias=gst[:, 0:1], scale=SCALE, accum_out=gst[:, 1:2])\
                      .then_inc(s_gcx, 1)
                    for k in range(4):
                        if k or G:
                            act.wait_ge(s_wku, 4 * G + k)
                        drain(KTw, lambda b: b[:, :])
                        if k % 2:
                            yield
                    if G:
                        act.wait_ge(s_gco, G)
                    drain(PcT[0:NBLK, :], lambda b: b[0:NBLK, 0:P])
                    yield
                    for k in range(4):
                        for q4 in range(4):
                            if q4 == 0 and k < 2 and G:
                                act.wait_ge(s_rel, 8 * G)
                            if q4 == 0 and k >= 2:
                                act.wait_ge(s_rel, 8 * G + k - 1)
                            drain(KTb[k % 2][:, 512 * q4:512 * q4 + 512], lambda b: b[:, :])
                        yield
                    act.wait_ge(s_gwb, G + 1)
                    sc.activation(Swin, Swin, ACT.Exp, bias=gst[:, 2:3], scale=SCALE, accum_out=gst[:, 3:4])\
                      .then_inc(s_gwx, 1)
                    drain(PTw[:, 0:4, :], lambda b: b[:, :].rearrange("p (k r) -> p k r", k=4))
                    drain(PTw[0:NS, 4, :], lambda b: b[0:NS, 0:P])
                    yield
                    act.wait_ge(s_gsb, G + 1)
                    act.wait_ge(s_rel, 8 * G + 4)
                    sc.activation(Sslc, Sslc, ACT.Exp, bias=gst[:, 4:5], scale=SCALE, accum_out=gst[:, 5:6])\
                      .then_inc(s_gsx, 1)
                    for q4 in range(4):
                        drain(PTs[:, 4 * q4:4 * q4 + 4, :], lambda b: b[:, :].rearrange("p (k r) -> p k r", k=4))
                    drain(PTs[0:NS, 16, :], lambda b: b[0:NS, 0:P])
                    yield
                    yield
                    yield
                act.wait_ge(s_ote, 2)
                drain8(mixT_s, NS)
                yield
                yield
                std(2 * PT - 1, NS)
                yield
                drain8(hT, NS)
                for q4 in range(4):
                    act.wait_ge(s_qf, 4 * PT + q4 + 1)
                    sc.activation(qpT_s[:, 4 * q4:4 * q4 + 4, :],
                                  PB[2 + q4 % 2][:, 0:4 * NS].rearrange("p (g s) -> p g s", g=4), ACT.Copy)\
                      .then_inc(s_qe, 1)
                    yield
                for q4 in range(4):
                    act.wait_ge(s_sf, 4 * PT + q4 + 1)
                    sc.activation(SC_s[q4 // 2][0:NS, 4 * (q4 % 2):4 * (q4 % 2) + 4, :],
                                  PB[4 + q4 % 2][0:NS, :].rearrange("p (g k) -> p g k", g=4), ACT.Copy)\
                      .then_inc(s_se, 1)
                for _ in range(K_SCORES, N_PIECES - 1):
                    yield
                gate_exp(PT)
                yield

            def iteration(j):
                t, s0 = slots_of(j)
                M = ROWS[t]
                idm = ident if t < PT else C("ident4")
                for half in range(2):
                    h4 = slice(4 * half, 4 * half + 4)
                    act.wait_ge(s_dot, 2 * j + half + 1)
                    sc.activation(gel[:, h4], dots[:, h4], ACT.Gelu).then_inc(s_gl, 1)
                    act.wait_ge(s_w8, 2 * j + half + 1)
                    if j:
                        act.wait_ge(s_free, 2 * (j - 1) + half + 1)
                    for r in (4 * half, 4 * half + 1):
                        sc.activation(diag[r][:, 0:M], idm, ACT.Copy, scale=w8[:, r:r + 1]).then_inc(s_dg, 1)

            todo = pieces()
            for j in range(N_IT):
                iteration(j)
                if j + 1 in IT0[1:]:
                    std(norm_of(IT0.index(j + 1) - 1), P)
                for _ in range(pieces_at(j)):
                    next(todo)
            for j in range(N_IT, N_IT + GATHERS[PT] // NR):
                iteration(j)
            std(2 * PT + 1, NS)

        def rest_vector(dve, link, settle):
            ve = nc.vector
            dve.wait_ge(s_p2w, P2W)
            ve.memset(QP.rearrange("p b r -> p (b r)"), 0.0).then_inc(s_qp, 1)
            settle(s_qp)

            def combine(bank, t, br, sums, first):
                gv = gates[:, t, :].rearrange("p (h c) -> p h c", h=NH)[:, :, br]
                link(ve.reciprocal(rcu, sums))
                link(ve.tensor_tensor(rcu, rcu, gv, ALU.mult))
                rb = rcu.unsqueeze(2).to_broadcast([P, NH, HD])
                bv = bank[:, :].rearrange("p (h d) -> p h d", h=NH)
                mv = mix[t][:, 0:512].rearrange("p (h d) -> p h d", h=NH)
                if first:
                    return ve.tensor_tensor(mv, bv, rb, ALU.mult)
                tv = tmpo_p.rearrange("p (h d) -> p h d", h=NH)
                link(ve.tensor_tensor(tv, bv, rb, ALU.mult))
                return ve.tensor_tensor(mv, mv, tv, ALU.add)

            for u in range(N_PU + 3):
                if u < N_PU:
                    br, t, h = PU[u]
                    L = (t + 1) * P
                    dve.wait_ge(s_s, u + 1)
                    dg = PB[u % 2][:, t * P:L]
                    link(ve.tensor_tensor(dg, dg, C("caus"), ALU.add))
                    link(ve.reduce_max(mx1[:, 0:1], PB[u % 2][:, 0:L], axis=AX))
                    ve.tensor_scalar(nbu[:, u % 4:u % 4 + 1], mx1[:, 0:1], -SCALE, None, ALU.mult).then_inc(s_nb, 1)
                    settle(s_nb)
                if u >= 3 and (u - 3) % NH == NH - 1:
                    bt = (u - 3) // NH
                    br, t, h = PU[u - 3]
                    dve.wait_ge(s_pv, NH * (bt + 1))
                    combine(PB[2 + bt % 2], t, 1 + br, rsu[:, bt % 2, :], br == 0).then_inc(s_ou, 1)
                    settle(s_ou)
            dve.wait_ge(s_ou, 2 * PT)
            dve.wait_ge(s_peb, 1)
            ve.tensor_tensor(biasc, PB[4][:, 0:4], b1, ALU.add).then_inc(s_bias, 1)
            settle(s_bias)

            def compressed(n):
                v, bs = CSTEPS[n]
                nblk = (NCH if bs else PCH) - 1
                nb = len(bs) or 1
                dve.wait_ge(s_w2p, n + 1)
                if v == 0:
                    dst = KCm[:, bs[0]:bs[0] + 2, :] if bs else KCp.unsqueeze(1)
                    src = PB[4][:, 0:nb * nblk].rearrange("p (b c) -> p b c", b=nb)
                else:
                    dst = VCm[0:nblk, bs[0]:bs[0] + 2, :] if bs else VCp[0:nblk, :].unsqueeze(1)
                    src = PB[5][0:nblk, 0:nb * P].rearrange("p (b c) -> p b c", b=nb)
                ve.tensor_copy(dst, src).then_inc(s_w2e, 1)
                settle(s_w2e)

            for n in range(NC_P):
                compressed(n)
            cadd = C("cadd").rearrange("p (t c) -> p t c", t=PT)
            cval = C("cvalid").rearrange("p (t c) -> p t c", t=PT)
            for t in range(PT):
                sh = [P, NH, PBLK]
                dve.wait_ge(s_cs, 2 * t + 2)
                for n in range(NKV):
                    last = ve.tensor_tensor(PX_c[:, NG * n:NG * n + NG, :],
                                            PB[n][:, 0:NG * PBLK].rearrange("p (h c) -> p h c", h=NG),
                                            cadd[:, t, :].unsqueeze(1).to_broadcast([P, NG, PBLK]), ALU.add)
                link(last)
                link(ve.reduce_max(c8, PX_c, axis=AX))
                ve.tensor_tensor(PX_c, PX_c, c8.unsqueeze(2).to_broadcast(sh), ALU.subtract).then_inc(s_cx, 1)
                settle(s_cx)
                dve.wait_ge(s_ce2, t + 1)
                link(ve.reduce_sum(c8, PX_c, axis=AX))
                ve.tensor_tensor(PX_c, PX_c, cval[:, t, :].unsqueeze(1).to_broadcast(sh), ALU.mult)\
                  .then_inc(s_cpn, 1)
                settle(s_cpn)
                dve.wait_ge(s_cpv, t + 1)
                combine(PB[2], t, 0, c8, False).then_inc(s_cou, 1)
                settle(s_cou)
            dve.wait_ge(s_cou, PT)

            def layer_norm(n, t, which, R, add):
                st = stat[0:R, 16 * n:16 * n + 16]
                for c2 in range(2):
                    xv = x_sb[0:R, t, c2 * 512:c2 * 512 + 512]
                    last = ve.scalar_tensor_tensor(xv, xv, ALPHA, add[c2][0:R, :], ALU.mult, ALU.add)
                link(last)
                for c2 in range(2):
                    last = ve.bn_stats(st[:, 6 * c2:6 * c2 + 6], x_sb[0:R, t, c2 * 512:c2 * 512 + 512])
                link(last)
                ve.bn_aggr(st[:, 12:14], st[:, 0:12].rearrange("p (k s) -> p k s", k=2)).then_inc(s_lv, 1)
                settle(s_lv)
                dve.wait_ge(s_ls, n + 1)
                link(ve.reciprocal(st[:, 15:16], st[:, 14:15]))
                xt = x_sb[0:R, t, :]
                link(ve.tensor_scalar(xt, xt, st[:, 12:13], st[:, 15:16], ALU.subtract, ALU.mult))
                link(ve.tensor_tensor(xt, xt, g_ln[0:R, which, :], ALU.mult))
                return ve.tensor_tensor(xt, xt, g_ln[0:R, 2 + which, :], ALU.add)

            def top16(n, vals, idx, src, spare, R):
                for k in range(2):
                    from_ = src if k == 0 else spare
                    for g in range(n):
                        last = ve.max(vals[0:R, g, 8 * k:8 * k + 8], from_[g])
                    link(last)
                    for g in range(n):
                        last = ve.max_index(idx[0:R, g, 8 * k:8 * k + 8], vals[0:R, g, 8 * k:8 * k + 8], from_[g])
                        if k == 0:
                            last = ve.match_replace(spare[g], vals[0:R, g, 0:8], src[g], NEG * 10)
                    link(last)
                    if k == 0:
                        yield

            iota_v = C("iota")

            def retrieve(t):
                R = ROWS[t]
                dve.wait_ge(s_se, 4 * t + 4)
                topiu, fpu = topi.bitcast(U32), fp.bitcast(U32)
                scores = [SC[0:R, t, g, :] if t < PT else SC_s[g // 8][0:R, g % 8, :] for g in range(16)]
                yield from top16(16, topv, topiu, scores, [SC2[0:R, g, :] for g in range(16)], R)
                ve.tensor_copy(topf[0:R], topiu[0:R]).then_inc(s_tk, 1)
                settle(s_tk)
                yield
                tv = topv[0:R].rearrange("p (h z) k -> p h z k", h=PH)
                tf = topf[0:R].rearrange("p (h z) k -> p h z k", h=PH)
                sh = [R, PH, TOPK, TOPK]
                c4 = cand[0:R].rearrange("p h (a b) -> p h a b", a=TOPK)
                link(ve.tensor_tensor(c4, tv[:, :, 0, :].unsqueeze(3).to_broadcast(sh),
                                      tv[:, :, 1, :].unsqueeze(2).to_broadcast(sh), ALU.add))
                sp2 = SC2[0:R].rearrange("p g k -> p (g k)").rearrange("p (h k) -> p h k", h=PH)
                yield from top16(PH, fv, fpu, [cand[0:R, h, :] for h in range(PH)],
                                 [sp2[:, h, :] for h in range(PH)], R)
                yield
                fpf = fpu[0:R].rearrange("p h k -> p (h k)")
                fau = fa.bitcast(U32)
                ve.tensor_scalar(fau[0:R, 0, :], fpf, 4, None, ALU.logical_shift_right)
                link(ve.tensor_scalar(fau[0:R, 1, :], fpf, 15, None, ALU.bitwise_and))
                link(ve.tensor_copy(ff[0:R], fau[0:R]))
                for z in range(2):
                    rk = ff[0:R, z, :].unsqueeze(2).to_broadcast([R, SLOTS, TOPK])
                    oh = OH[0:R].rearrange("p h k -> p (h k)").rearrange("p (s a) -> p s a", a=TOPK)
                    link(ve.tensor_tensor(oh, rk, iota_v[0:R].unsqueeze(1).to_broadcast([R, SLOTS, TOPK]),
                                          ALU.is_equal))
                    o4 = OH[0:R].rearrange("p h (k a) -> p h k a", a=TOPK)
                    link(ve.tensor_tensor(o4, o4, tf[:, :, z, :].unsqueeze(2).to_broadcast(sh), ALU.mult))
                    link(ve.reduce_sum(fa[0:R, z, :], oh, axis=AX))
                    if z == 0:
                        yield
                link(ve.scalar_tensor_tensor(fa[0:R, 0, :], fa[0:R, 0, :], float(NK), fa[0:R, 1, :],
                                             ALU.mult, ALU.add))
                link(ve.tensor_copy(eidx_u[0:R, t, :], fa[0:R, 0, :]))
                link(ve.tensor_copy(gs8[0:R], fv[0:R, :, 0]))
                ve.tensor_tensor(fv[0:R], fv[0:R], gs8[0:R].unsqueeze(2).to_broadcast([R, PH, TOPK]),
                                 ALU.subtract).then_inc(s_gx, 1)
                settle(s_gx)
                dve.wait_ge(s_ge, t + 1)
                link(ve.reduce_sum(gs8[0:R], fv[0:R], axis=AX))
                link(ve.reciprocal(gs8[0:R], gs8[0:R]))
                last = ve.tensor_tensor(gw[0:R, t, :].rearrange("p (h k) -> p h k", h=PH), fv[0:R],
                                        gs8[0:R].unsqueeze(2).to_broadcast([R, PH, TOPK]), ALU.mult)
                if t == PT:
                    link(last)
                    for q in range(1, QB):
                        qr = slice(NS * q, NS * q + NS)
                        ve.tensor_copy(x_sb[qr, PT, :], x_sb[0:NS, PT, :])
                        ve.tensor_copy(gw[qr, PT, 0:NS], gw[0:NS, PT, NS * q:NS * q + NS])
                        last = ve.tensor_copy(eidx_u[qr, PT, 0:NS], eidx_u[0:NS, PT, NS * q:NS * q + NS])
                last.then_inc(s_idx, 1)
                settle(s_idx)
                yield

            dve.wait_ge(s_x, 32)
            dve.wait_ge(s_ln, 64)
            for t in range(PT):
                dve.wait_ge(s_mo, t + 1)
                layer_norm(t, t, 0, P, PB).then_inc(s_h, 1)
                settle(s_h)
            dve.wait_ge(s_sk, 16)
            for t in range(PT - 1):
                for _ in retrieve(t):
                    pass

            hind = C("hind")

            def pieces():
                yield from retrieve(PT - 1)
                for _ in range(6, K0):
                    yield
                for n in range(NC_P, len(CSTEPS)):
                    if n > NC_P:
                        compressed(n - 1)
                    for _ in range(PER_STEP):
                        yield
                compressed(len(CSTEPS) - 1)
                ve.memset(impp, 0.0)
                for G in range(2):
                    dve.wait_ge(s_gc, G + 1)
                    ve.tensor_copy(g4[:, 0:NBLK], PB[4][:, 0:NBLK])
                    link(ve.tensor_copy(g4[:, 160:248], PB[4][:, 160:248]))
                    link(ve.reduce_max(mx1[:, 0:1], g4[:, 0:NBLK], axis=AX))
                    ve.tensor_scalar(gst[:, 0:1], mx1[:, 0:1], -SCALE, None, ALU.mult).then_inc(s_gcb, 1)
                    settle(s_gcb)
                    g3 = g3f.rearrange("p (c h) -> p c h", c=3)
                    link(ve.tensor_tensor(g3, g4[:, 224:248].rearrange("p (h c) -> p c h", c=3),
                                          hind.unsqueeze(1).to_broadcast([P, 3, NH]), ALU.mult))
                    link(ve.reduce_sum(grow, g3, axis=AX))
                    dve.wait_ge(s_gcx, G + 1)
                    link(ve.reciprocal(gcoef[:, 0:1], gst[:, 1:2]))
                    ve.tensor_scalar(Pc, Pc, gcoef[:, 0:1], None, ALU.mult).then_inc(s_gcp, 1)
                    settle(s_gcp)
                    yield
                    dve.wait_ge(s_wku, 4 * G + 4)
                    link(ve.tensor_copy(Swin[:, 0:WIN], PB[5][:, :]))
                    first4 = Swin[:, 0:WIN].rearrange("p (k c) -> p k c", k=4)[:, :, 0]
                    ve.tensor_tensor(first4, first4, C("winm"), ALU.add)
                    newm = C("newm")[:, G * NS:(G + 1) * NS]
                    ve.tensor_tensor(Sslc[:, PAST:PAST + NS], g4[:, 192:224], newm, ALU.add)
                    link(ve.tensor_tensor(Swin[:, WIN:WIN + NS], g4[:, 160:192], newm, ALU.add))
                    link(ve.reduce_max(mx1[:, 1:2], Swin, axis=AX))
                    ve.tensor_scalar(gst[:, 2:3], mx1[:, 1:2], -SCALE, None, ALU.mult).then_inc(s_gwb, 1)
                    settle(s_gwb)
                    yield
                    dve.wait_ge(s_imp, G + 1)
                    ve.tensor_copy(impp[:, 1:1 + NBLK], PB[4][:, 256:256 + NBLK]).then_inc(s_ic, 1)
                    settle(s_ic)
                    b0, b1_, b2_ = blk[:, 0:NSEL], blk[:, NSEL:2 * NSEL], blk[:, 2 * NSEL:3 * NSEL]
                    t8 = blk[:, 3 * NSEL:3 * NSEL + 8]
                    link(ve.reduce_sum(b0, impp[:, 0:132].rearrange("p (j k) -> p j k", k=4), axis=AX))
                    link(ve.tensor_tensor(b0, b0, impp[:, 4:136].rearrange("p (j k) -> p j k", k=4)[:, :, 0], ALU.add))
                    link(ve.tensor_tensor(b0, b0, C("forced"), ALU.max))
                    link(ve.max(t8, b0))
                    link(ve.match_replace(b1_, t8, b0, NEG))
                    link(ve.max(t8, b1_))
                    link(ve.match_replace(b2_, t8, b1_, NEG))
                    link(ve.tensor_scalar(b2_, b2_, NEG / 10, NEG, ALU.is_gt, ALU.mult))
                    yield
                    for k in range(4):
                        r32 = slice(32 * k, 32 * k + 32)
                        for q4 in range(4):
                            if q4 < 3:
                                dve.wait_ge(s_ss, 3 * (4 * G + k) + q4 + 1)
                            else:
                                dve.wait_ge(s_rel, 8 * G + k + 1)
                            ve.tensor_copy(Sslc[r32, 512 * q4:512 * q4 + 512], PB[2 + q4 % 2][r32, :])\
                              .then_inc(s_sev, 1)
                            settle(s_sev)
                        if k < 3:
                            yield
                    sv = Sslc[:, 0:PAST].rearrange("p (k j c) -> p k j c", k=16, c=4)
                    link(ve.tensor_tensor(sv, sv, b2_[:, 0:32].unsqueeze(1).unsqueeze(3).to_broadcast([P, 16, 32, 4]),
                                          ALU.add))
                    link(ve.reduce_max(mx1[:, 2:3], Sslc, axis=AX))
                    ve.tensor_scalar(gst[:, 4:5], mx1[:, 2:3], -SCALE, None, ALU.mult).then_inc(s_gsb, 1)
                    settle(s_gsb)
                    for _ in range(4):
                        yield
                    dve.wait_ge(s_gco, G + 1)
                    link(ve.tensor_scalar(oacc, PB[4][:, 384:512], grow[:, 0:1], None, ALU.mult))
                    dve.wait_ge(s_gwo, G + 1)
                    dve.wait_ge(s_rel, 8 * G + 8)
                    for k, (br, st, c) in enumerate(((2, 3, 128), (1, 5, 0))):
                        link(ve.reciprocal(gcoef[:, 1 + k:2 + k], gst[:, st:st + 1]))
                        link(ve.tensor_tensor(gcoef[:, 1 + k:2 + k], gcoef[:, 1 + k:2 + k], grow[:, br:br + 1],
                                              ALU.mult))
                        link(ve.scalar_tensor_tensor(oacc, PB[5][:, c:c + 128], gcoef[:, 1 + k:2 + k], oacc,
                                                     ALU.mult, ALU.add))
                    sh = [P, NG, HD]
                    for n in range(NKV):
                        last = ve.tensor_tensor(
                            OE[:, 256 * n:256 * n + 256].rearrange("p (g d) -> p g d", g=NG),
                            oacc[:, HD * n:HD * n + HD].unsqueeze(1).to_broadcast(sh),
                            hind[:, NG * n:NG * n + NG].unsqueeze(2).to_broadcast(sh), ALU.mult)
                    last.then_inc(s_oe, 1)
                    settle(s_oe)
                    dve.wait_ge(s_ot, G + 1)
                    mv = mix_s[0:NS, 0:512]
                    if G == 0:
                        last = ve.tensor_copy(mv, PB[2][0:NS, :])
                    else:
                        last = ve.tensor_tensor(mv, mv, PB[2][0:NS, :], ALU.add)
                    last.then_inc(s_ote, 1)
                    settle(s_ote)
                    yield
                yield
                yield
                dve.wait_ge(s_mo, TILES)
                layer_norm(2 * PT - 1, PT, 0, NS, PB[2:4]).then_inc(s_h, 1)
                settle(s_h)
                for _ in range(K_NORM, K_SCORES + 1):
                    yield
                dve.wait_ge(s_sk, 32)
                yield from retrieve(PT)

            def dot_rows(j, half):
                t = slots_of(j)[0]
                for r in range(4 * half, 4 * half + 4):
                    dve.wait_ge(s_uv[r], 16 * (j + 1))
                    last = ve.tensor_tensor_reduce(out=uv[r][:, 0:D], in0=uv[r][:, 0:D], in1=x_sb[:, t, :],
                                                   scale=1.0, scalar=0.0, op0=ALU.mult, op1=ALU.add,
                                                   accum_out=dots[:, r:r + 1])
                last.then_inc(s_dot, 1)

            def weigh_rows(j, half):
                t, s0 = slots_of(j)
                h4 = slice(4 * half, 4 * half + 4)
                dve.wait_ge(s_gl, 2 * j + half + 1)
                ve.tensor_tensor(w8[:, h4], gel[:, h4], gw[:, t, s0 + 4 * half:s0 + 4 * half + 4], ALU.mult)\
                  .then_inc(s_w8, 1)
                settle(s_w8)
                for r in (4 * half + 2, 4 * half + 3):
                    if s0 + r == 2:
                        last = ve.tensor_scalar(acc_v, uv[r][:, D:2 * D], w8[:, r:r + 1], None, ALU.mult)
                    else:
                        last = ve.scalar_tensor_tensor(acc_v, uv[r][:, D:2 * D], w8[:, r:r + 1], acc_v,
                                                       ALU.mult, ALU.add)
                    if r % 4 == 2:
                        link(last)
                    else:
                        last.then_inc(s_vf, 1)
                        settle(s_vf)

            dve.wait_ge(s_sf, 4 * PT)
            todo = pieces()
            dot_rows(0, 0)
            for j in range(N_IT):
                weigh_rows(j, 0)
                dot_rows(j, 1)
                weigh_rows(j, 1)
                if j + 1 in IT0[1:]:
                    t = IT0.index(j + 1) - 1
                    dve.wait_ge(s_y, t + 1)
                    layer_norm(norm_of(t), t, 1, P, PB).then_inc(s_fin, 1)
                    settle(s_fin)
                if j + 1 < N_IT:
                    dot_rows(j + 1, 0)
                for _ in range(pieces_at(j)):
                    next(todo)
            for j in range(N_IT, N_IT + GATHERS[PT] // NR):
                for half in range(2):
                    dot_rows(j, half)
                    weigh_rows(j, half)
            dve.wait_ge(s_y, TILES)
            layer_norm(2 * PT + 1, PT, 1, NS, PB).then_inc(s_fin, 1)
            settle(s_fin)

        block = ctx.enter_context(nc.Block())

        @block.sync
        def _(sp):
            sp.dma_start(xT, i["xT"].rearrange("p (c s) -> p c s", c=KC)).then_inc(s_xT, 16)
            for g, (kind, c0, n) in enumerate(GROUPS):
                w0 = KC * sum(m for _, _, m in GROUPS[:g])
                if g >= 2:
                    used = max(k for k, u in enumerate(units) if u[0] == g - 2) + 1
                    sp.wait_ge(s_zps, used)
                sp.dma_start(wst[g % 2][:, 0:KC * n], i["w_in"][:, w0:w0 + KC * n]).then_inc(s_w[g % 2], 16)
                if g == 1:
                    sp.dma_start(consts, i["consts"]).then_inc(s_const, 16)
                    sp.dma_start(par, i["par"]).then_inc(s_const, 16)
                    sp.dma_start(b_if, i["b_if"]).then_inc(s_st, 16)
                    sp.dma_start(m0r, i["m0"]).then_inc(s_st, 16)
                    for c in range(KC):
                        sp.dma_start(zspad[:, c, :, 0:3],
                                     i["stconv"][c * P:(c + 1) * P, :].rearrange("p (b j) -> p b j", b=DB))\
                          .then_inc(s_st, 16)
            sp.dma_start(x_sb[:, 0:PT, :], i["x"][0:SEQ, :].rearrange("(t p) d -> p t d", p=P)).then_inc(s_x, 16)
            sp.dma_start(x_sb[0:NS, PT, :], i["x"][SEQ:T, :]).then_inc(s_x, 16)
            sp.wait_ge(s_zps, NU)
            sp.dma_start(C0, i["C0"].rearrange("p (g v) -> p g v", g=32)).then_inc(s_c0, 16)
            sp.wait_ge(s_zev, U_QK)
            sp.dma_start(o["p_conv"].rearrange("(c p) j -> p c j", p=P), zpad[:, :, SEQ:SEQ + 3]).then_inc(s_p2w, 16)
            for c in range(KC):
                sp.dma_start(o["s_conv"][c * P:(c + 1) * P, :].rearrange("p (b j) -> p b j", b=DB),
                             zspad[:, c, :, 4:7]).then_inc(s_p2w, 16)
            sp.wait_ge(s_rows, 1)
            sp.dma_start(o["p_m"], r_m[:, SEQ - 1:SEQ]).then_inc(s_p2w, 16)
            sp.dma_start(o["s_m"], m_last).then_inc(s_p2w, 16)
            sp.wait_ge(s_ce, MH)
            sp.dma_start(o["p_C"], Cout).then_inc(s_p2w, 16)
            sp.wait_ge(s_cue, 11)
            sp.dma_start(o["s_C"].rearrange("p (g v) -> p g v", g=32), C0).then_inc(s_p2w, 16)
            rest_sync(sp)

        @block.tensor
        def _(pe_eng):
            te = nc.tensor

            def mm(out, l, r, start=True, stop=True):
                return te.matmul(out, l, r, start=start, stop=stop)

            pe_eng.wait_ge(s_xT, 16)
            for n, (g, kind, a, what, off) in enumerate(units):
                pe_eng.wait_ge(s_w[g % 2], 16 * (g // 2 + 1))
                if n >= 4:
                    pe_eng.wait_ge(s_zev, n - 3)
                w = wst[g % 2][:, 0:KC * GROUPS[g][2]].rearrange("p (c n) -> p c n", c=KC)
                bank = PB[n % 4]
                for c in range(KC):
                    if what == "tile":
                        r0 = a * P
                        cn = GROUPS[g][2]
                        last = mm(bank[0:ROWS[a], 0:cn], xT[:, c, r0:r0 + ROWS[a]], w[:, c, 0:cn],
                                  c == 0, c == KC - 1)
                    else:
                        s0, s1 = (0, SEQ) if what == "prompt" else (SEQ, T)
                        m = P if kind == "qk" else MH
                        last = mm(bank[0:m, 0:s1 - s0], w[:, c, off:off + m], xT[:, c, s0:s1],
                                  c == 0, c == KC - 1)
                last.then_inc(s_zps, 1)

            pe_eng.wait_ge(s_const, 32)
            pe_eng.wait_ge(s_zev, NU)
            pe_eng.wait_ge(s_qk, KC)
            for t in range(PT):
                if t >= 1:
                    pe_eng.wait_ge(s_kte, t)
                for h in range(MH):
                    last = te.transpose(PB[7][:, h * P:(h + 1) * P], qkT[:, MH + h, t * P:(t + 1) * P], ident)
                last.then_inc(s_ktp, 1)
            pe_eng.wait_ge(s_rows, 1)
            pe_eng.wait_ge(s_rexp, 1)
            for q, r in ((0, r_ig), (1, r_ex)):
                for t in range(PT):
                    c0 = (q * PT + t) * MH
                    last = te.transpose(PB[6][:, c0:c0 + MH], r[:, t * P:(t + 1) * P], C("ident")[0:MH, 0:MH])
            last.then_inc(s_colp, 1)
            selh = C("selh", MH).rearrange("p (h s) -> p h s", h=MH)
            mm(PB[0][:, :], selh[:, 0, :], r_b0[:, 0:SEQ]).then_inc(s_bcp, 1)
            for h in range(MH):
                for t in range(PT):
                    n = PT * h + t
                    if n >= 2:
                        pe_eng.wait_ge(s_sw, n - 1)
                    L = SEQ - t * P
                    mm(PB[2 + n % 2][:, 0:L], qkT[:, MH + h, t * P:(t + 1) * P], qkT[:, h, t * P:SEQ])\
                        .then_inc(s_sp, 1)
                if h + 1 < MH:
                    if h >= 1:
                        pe_eng.wait_ge(s_wmin, PT * h)
                    mm(PB[(h + 1) % 2][:, :], selh[:, h + 1, :], r_b0[:, 0:SEQ]).then_inc(s_bcp, 1)
                for t in range(PT):
                    n = PT * h + t
                    pe_eng.wait_ge(s_sw, n + 1)
                    if n >= 2:
                        pe_eng.wait_ge(s_nev, n - 1)
                    for k in range(t + 1):
                        last = mm(PB[4 + n % 2][:, 0:129], SWb[:, k, t * P:(t + 1) * P], v1[:, k, h, :],
                                  k == 0, k == t)
                    last.then_inc(s_np, 1)
            pe_eng.wait_ge(s_cole, 1)
            pe_eng.wait_ge(s_kte, PT)
            for h in range(MH):
                pe_eng.wait_ge(s_kw, PT * (h + 1))
                if h >= 2:
                    pe_eng.wait_ge(s_ce, h - 1)
                for t in range(PT):
                    last = mm(PB[6 + h % 2][:, 0:129], ktok[:, t, h * P:(h + 1) * P],
                              v1[:, t, h, :], t == 0, t == PT - 1)
                last.then_inc(s_cp, 1)
            pe_eng.wait_ge(s_wmin, PT * MH)
            for h in range(MH):
                last = mm(PB[h // 2][:, (h % 2) * 192:(h % 2) * 192 + 192], selh[:, h, :],
                          SR.rearrange("p q s -> p (q s)"))
            last.then_inc(s_bcs, 1)
            pe_eng.wait_ge(s_sw, PT * MH)
            pe_eng.wait_ge(s_prod, 1)
            mm(PB[2][:, 0:128], kcs, qcs)
            mm(PB[2][:, 128:129], prod, C("ones")).then_inc(s_sps, 1)
            pe_eng.wait_ge(s_c0, 16)
            for g in range(32):
                last = mm(PB[3][:, 4 * g:4 * g + 4], C0[:, g, 0:128], qcs[:, 4 * g:4 * g + 4])
            last.then_inc(s_ni, 1)
            pe_eng.wait_ge(s_nev, PT * MH)
            te.transpose(PB[4][:, 0:128], kcs, ident).then_inc(s_kts, 1)
            pe_eng.wait_ge(s_nie, 1)
            te.transpose(PB[5][:, 0:128], numT, ident).then_inc(s_nit, 1)
            pe_eng.wait_ge(s_sws, 1)
            pe_eng.wait_ge(s_kse, 1)
            mm(PB[4][:, 0:129], SWs, v1s).then_inc(s_nin, 1)
            pe_eng.wait_ge(s_vb, 1)
            pe_eng.wait_ge(s_ce, MH)
            VBf = VB.rearrange("p g v -> p (g v)")
            for n in range(11):
                if n >= 2:
                    pe_eng.wait_ge(s_cue, n - 1)
                c0, c1 = n * 387, min(32 * 129, (n + 1) * 387)
                mm(PB[6 + n % 2][:, 0:c1 - c0], kws, VBf[:, c0:c1]).then_inc(s_cup, 1)
            rest_tensor(pe_eng)

        @block.scalar
        def _(act):
            sc = nc.scalar

            act.wait_ge(s_st, 32 + 16 * KC)
            act.wait_ge(s_pad, 1)
            for n, (g, kind, a, what, off) in enumerate(units):
                act.wait_ge(s_zps, n + 1)
                bank = PB[n % 4]
                if kind == "qk":
                    if what == "prompt":
                        last = sc.activation(zpad[:, a, 3:3 + SEQ], bank[:, :], ACT.Copy)
                    else:
                        last = sc.activation(zspad[:, a, :, 3:7],
                                             bank[:, 0:NS].rearrange("p (b t) -> p b t", b=DB), ACT.Copy)
                elif kind == "if":
                    s0, s1 = (0, SEQ) if what == "prompt" else (SEQ, T)
                    dst = (r_ig, r_f)[a]
                    last = sc.activation(dst[:, s0:s1], bank[0:MH, 0:s1 - s0], ACT.Identity,
                                         bias=b_if[:, a:a + 1])
                elif kind == "v":
                    if a < PT:
                        last = sc.activation(v1[:, a, :, 0:128], bank[:, :].rearrange("p (h v) -> p h v", h=MH),
                                             ACT.Copy)
                    else:
                        for h in range(MH):
                            last = sc.activation(v1s[NS * h:NS * h + NS, 0:128],
                                                 bank[0:NS, h * P:(h + 1) * P], ACT.Copy)
                elif kind == "o":
                    last = sc.activation(zo[0:ROWS[a], a, :], bank[0:ROWS[a], :], ACT.Sigmoid)
                elif kind == "q":
                    last = sc.activation(
                        zq[a][0:ROWS[a], :].rearrange("p (g n d) -> p n g d", g=NG, n=NKV),
                        bank[0:ROWS[a], :].rearrange("p (n g d) -> p n g d", n=NKV, g=NG), ACT.Copy)
                elif kind == "kv":
                    last = sc.activation(zkv[a][0:ROWS[a], 0:512], bank[0:ROWS[a], :], ACT.Copy)
                else:
                    sc.activation(zkv[a][0:ROWS[a], 512:768], bank[0:ROWS[a], 0:256], ACT.Copy)
                    last = sc.activation(gates[0:ROWS[a], a, :], bank[0:ROWS[a], 256:280], ACT.Sigmoid)
                last.then_inc(s_zev, 1)
                if n >= 3 and n % 2 and n // 2 - 1 < KC:
                    c = n // 2 - 1
                    act.wait_ge(s_cv, c + 1)
                    if c >= 2:
                        act.wait_ge(s_qk, c - 1)
                    sc.activation(sg[:, c % 2, :], qkT[:, c, :], ACT.Sigmoid).then_inc(s_sg, 1)
                if n == U_IF + 2:
                    act.wait_ge(s_fabs, 1)
                    sc.activation(r_ex, r_ab, ACT.Exp, scale=-1.0).then_inc(s_act, 1)
                    act.wait_ge(s_act, 1)
                    sc.activation(r_ex, r_ex, ACT.Ln, bias=C("ones", MH)).then_inc(s_fexp, 1)

            for t in range(PT):
                act.wait_ge(s_ktp, t + 1)
                sc.activation(ktok[:, t, :], PB[7][:, :], ACT.Copy).then_inc(s_kte, 1)
            act.wait_ge(s_rows, 1)
            sc.activation(r_ex[:, 0:SEQ], r_m[:, 0:SEQ], ACT.Exp, scale=-1.0)
            sc.activation(SR[:, 2, :], r_m[:, SEQ:T], ACT.Exp, scale=-1.0)
            sc.activation(SR[:, 3:6, :], SR[:, 3:6, :], ACT.Exp).then_inc(s_rexp, 1)
            for n in range(PT * MH):
                L = SEQ - (n % PT) * P
                act.wait_ge(s_wmin, n + 1)
                sc.activation(wt[:, n % 2, 0:L], wt[:, n % 2, 0:L], ACT.Exp).then_inc(s_wexp, 1)
            act.wait_ge(s_wmin, PT * MH)
            sc.activation(wcol[:, 0:16], wcol[:, 0:16], ACT.Exp).then_inc(s_wx, 1)
            for h in range(MH):
                act.wait_ge(s_cp, h + 1)
                sc.activation(Cout[:, h, :], PB[6 + h % 2][:, 0:129], ACT.Copy).then_inc(s_ce, 1)
            act.wait_ge(s_bcs, 1)
            for k in range(2):
                last = sc.activation(BC[:, 2 * k:2 * k + 2, :, :],
                                     PB[k][:, 0:384].rearrange("p (h q s) -> p h q s", h=2, q=6), ACT.Copy)
            last.then_inc(s_bce, 1)
            act.wait_ge(s_sx, 1)
            sc.activation(smt, smt, ACT.Exp).then_inc(s_sxe, 1)
            act.wait_ge(s_ni, 1)
            sc.activation(numT, PB[3][:, 0:128], ACT.Copy).then_inc(s_nie, 1)
            rest_scalar(act)

        @block.vector
        def _(dve):
            ve = nc.vector
            chain = [0]

            def link(ins):
                chain[0] += 1
                ins.then_inc(s_dve, 1)
                dve.wait_ge(s_dve, chain[0])

            settled = {}

            def settle(s):
                settled[s.name] = settled.get(s.name, 0) + 1
                dve.wait_ge(s, settled[s.name])

            ve.memset(v1[:, 0:PT, :, 128:129], 1.0)
            ve.memset(v1s[:, 128:129], 1.0)
            ve.memset(zpad[:, :, 0:3], 0.0).then_inc(s_pad, 1)
            settle(s_pad)
            dve.wait_ge(s_const, 32)
            dve.wait_ge(s_st, 32 + 16 * KC)
            for c in range(KC):
                dve.wait_ge(s_zev, 2 * c + 2)
                d0 = qkT[:, c, 0:SEQ]
                d1 = qkT[:, c, SEQ:T].rearrange("p (b t) -> p b t", b=DB)
                for j in range(4):
                    s0 = zpad[:, c, j:j + SEQ]
                    s1 = zspad[:, c, :, j:j + DT]
                    if j == 0:
                        ve.tensor_scalar(d0, s0, conv_w[:, c, 0:1], conv_b[:, c:c + 1], ALU.mult, ALU.add)
                        link(ve.tensor_scalar(d1, s1, conv_w[:, c, 0:1], conv_b[:, c:c + 1], ALU.mult, ALU.add))
                    else:
                        ve.scalar_tensor_tensor(d0, s0, conv_w[:, c, j:j + 1], d0, ALU.mult, ALU.add)
                        last = ve.scalar_tensor_tensor(d1, s1, conv_w[:, c, j:j + 1], d1, ALU.mult, ALU.add)
                        if j < 3:
                            link(last)
                        else:
                            last.then_inc(s_cv, 1)
                            settle(s_cv)
                if c >= 1:
                    dve.wait_ge(s_sg, c)
                    ve.scalar_tensor_tensor(qkT[:, c - 1, :], qkT[:, c - 1, :], 1.0 if c - 1 < MH else KSCALE,
                                            sg[:, (c - 1) % 2, :], ALU.mult, ALU.mult).then_inc(s_qk, 1)
                    settle(s_qk)
            dve.wait_ge(s_sg, KC)
            ve.scalar_tensor_tensor(qkT[:, KC - 1, :], qkT[:, KC - 1, :], KSCALE, sg[:, (KC - 1) % 2, :],
                                    ALU.mult, ALU.mult).then_inc(s_qk, 1)
            settle(s_qk)
            dve.wait_ge(s_zev, U_IF)
            ve.scalar_tensor_tensor(r_ab, r_f, -1.0, r_f, ALU.mult, ALU.max).then_inc(s_fabs, 1)
            settle(s_fabs)
            dve.wait_ge(s_fexp, 1)
            link(ve.scalar_tensor_tensor(r_b0, r_f, 0.0, r_ex, ALU.min, ALU.subtract))

            def scan(src, other, op):
                d = 1
                while d < SEQ:
                    link(ve.tensor_copy(other[:, 0:d], src[:, 0:d]))
                    ve.tensor_tensor(other[:, d:SEQ], src[:, d:SEQ], src[:, 0:SEQ - d], op)
                    s3 = src[:, SEQ:T].rearrange("p (b t) -> p b t", b=DB)
                    o3 = other[:, SEQ:T].rearrange("p (b t) -> p b t", b=DB)
                    if d < DT:
                        ve.tensor_copy(o3[:, :, 0:d], s3[:, :, 0:d])
                        link(ve.tensor_tensor(o3[:, :, d:DT], s3[:, :, d:DT], s3[:, :, 0:DT - d], op))
                    else:
                        link(ve.tensor_copy(other[:, SEQ:T], src[:, SEQ:T]))
                    src, other = other, src
                    d *= 2
                return src, other

            cum, free = scan(r_b0, r_b1, ALU.add)
            link(ve.tensor_tensor(r_ig, r_ig, cum, ALU.subtract))
            link(ve.tensor_copy(r_f, r_ig))
            mx, _ = scan(r_f, r_ab, ALU.max)
            link(ve.tensor_scalar(mx[:, 0:SEQ], mx[:, 0:SEQ], 0.0, None, ALU.max))
            m03 = m0r.unsqueeze(2).to_broadcast([MH, DB, DT])

            def s3(a):
                return a.rearrange("p (b t) -> p b t", b=DB)

            link(ve.tensor_tensor(s3(mx[:, SEQ:T]), s3(mx[:, SEQ:T]), m03, ALU.max))
            link(ve.tensor_tensor(r_m, mx, cum, ALU.add))
            ve.tensor_copy(m_last, r_m[:, SEQ:T].rearrange("p (b t) -> p b t", b=DB)[:, :, 3])
            link(ve.tensor_scalar(free, mx, -1.0, None, ALU.mult))
            nml = s3(free[:, SEQ:T])[:, :, 3:4].to_broadcast([MH, DB, DT])
            nml_c = small[:, 165:166]
            ve.tensor_copy(SR[:, 0, :], r_ig[:, SEQ:T])
            ve.tensor_copy(SR[:, 1, :], free[:, SEQ:T])
            ve.tensor_tensor(s3(SR[:, 3, :]), s3(free[:, SEQ:T]), m03, ALU.add)
            ve.tensor_tensor(s3(SR[:, 4, :]), s3(r_ig[:, SEQ:T]), nml, ALU.add)
            ve.tensor_tensor(s3(SR[:, 5, :]), nml, m03, ALU.add).then_inc(s_rows, 1)
            settle(s_rows)
            ve.tensor_copy(qcs.rearrange("p (h s) -> p h s", h=MH), qkT[:, 0:MH, SEQ:T])
            link(ve.tensor_copy(kcs.rearrange("p (h s) -> p h s", h=MH), qkT[:, MH:2 * MH, SEQ:T]))
            dve.wait_ge(s_pg, 16)
            ve.tensor_scalar(cidx, pages, 8.0, C("pm8"), ALU.mult, ALU.add).then_inc(s_ci, 1)
            settle(s_ci)
            dve.wait_ge(s_zev, U_KVG)
            cosv = C("cos").rearrange("p (t d) -> p t d", t=TILES)
            sinv = C("sin").rearrange("p (t d) -> p t d", t=TILES)
            for t in range(TILES):
                R = ROWS[t]
                qv = zq[t][0:R, :].rearrange("p (h d) -> p h d", h=NH)
                kv = zkv[t][0:R, :].rearrange("p (b v n d) -> p b v n d", b=3, v=2, n=NKV)[:, :, 0, :, :]
                for x1, x2, shape in ((qv[:, :, 0:32], qv[:, :, 32:64], [R, NH, 32]),
                                      (kv[:, :, :, 0:32], kv[:, :, :, 32:64], [R, 3, NKV, 32])):
                    cs, sn = cosv[0:R, t, :], sinv[0:R, t, :]
                    for _ in shape[1:-1]:
                        cs, sn = cs.unsqueeze(1), sn.unsqueeze(1)
                    cs, sn = cs.to_broadcast(shape), sn.to_broadcast(shape)
                    n = int(np.prod(shape[1:]))

                    def tm(k):
                        a = rtmp[0:R, k, 0:n]
                        return a.rearrange("p (h d) -> p h d", d=32) if len(shape) == 3 else \
                            a.rearrange("p (b n d) -> p b n d", b=3, n=NKV)
                    ve.tensor_tensor(tm(0), x1, cs, ALU.mult)
                    ve.tensor_tensor(tm(1), x2, sn, ALU.mult)
                    ve.tensor_tensor(tm(2), x2, cs, ALU.mult)
                    link(ve.tensor_tensor(tm(3), x1, sn, ALU.mult))
                    ve.tensor_tensor(x1, tm(0), tm(1), ALU.subtract)
                    last = ve.tensor_tensor(x2, tm(2), tm(3), ALU.add)
                    if len(shape) == 3:
                        link(last)
                    else:
                        last.then_inc(s_rope, 1)
                        settle(s_rope)
            dve.wait_ge(s_rope, TILES)

            dve.wait_ge(s_colp, 1)
            ve.tensor_copy(cols, PB[6][:, 0:32].rearrange("p (q t h) -> p q t h", q=2, t=PT)).then_inc(s_cole, 1)
            settle(s_cole)

            NM = PT * MH

            def exponent(n):
                h, t = n // PT, n % PT
                L = SEQ - t * P
                dve.wait_ge(s_bcp, h + 1)
                if t == PT - 1:
                    link(ve.tensor_copy(nml_c, PB[h % 2][:, SEQ - 1:SEQ]))
                    ve.tensor_scalar(wcol[:, 4 * h:4 * h + 4], cols[:, 0, :, h], nml_c, None, ALU.add)
                ve.tensor_scalar(wt[:, n % 2, 0:L], PB[h % 2][:, t * P:SEQ], cols[:, 0, t, h:h + 1], 0.0,
                                 ALU.add, ALU.min).then_inc(s_wmin, 1)
                settle(s_wmin)

            def weighted(n):
                h, t = n // PT, n % PT
                L = SEQ - t * P
                dve.wait_ge(s_wexp, n + 1)
                link(ve.tensor_tensor(wt[:, n % 2, 0:P], wt[:, n % 2, 0:P], C("tri"), ALU.mult))
                dve.wait_ge(s_sp, n + 1)
                if t == 0 and h:
                    dve.wait_ge(s_np, PT * h)
                ve.tensor_tensor(SWb[:, t, t * P:SEQ], PB[2 + n % 2][:, 0:L], wt[:, n % 2, 0:L], ALU.mult)\
                  .then_inc(s_sw, 1)
                settle(s_sw)

            def divide(n):
                h, t = n // PT, n % PT
                bank = PB[4 + n % 2]
                dve.wait_ge(s_np, n + 1)
                d = rs8[:, 2 * (n % 8):2 * (n % 8) + 1]
                link(ve.tensor_copy(d, bank[:, 128:129]))
                link(ve.scalar_tensor_tensor(d, d, -1.0, d, ALU.mult, ALU.max))
                link(ve.tensor_tensor(d, d, cols[:, 1, t, h:h + 1], ALU.max))
                link(ve.reciprocal(d, d))
                ve.scalar_tensor_tensor(mix[t][:, 512 + h * P:512 + (h + 1) * P], bank[:, 0:128], d,
                                        zo[:, t, h * P:(h + 1) * P], ALU.mult, ALU.mult).then_inc(s_nev, 1)
                settle(s_nev)

            dve.wait_ge(s_zev, U_O)
            exponent(0)
            for n in range(NM):
                if n + 1 < NM:
                    exponent(n + 1)
                weighted(n)
                if n % PT == PT - 1:
                    for k in range(n - PT + 1, n + 1):
                        divide(k)
            dve.wait_ge(s_wx, 1)
            dve.wait_ge(s_kte, PT)
            for h in range(MH):
                for t in range(PT):
                    kk = ktok[:, t, h * P:(h + 1) * P]
                    ve.tensor_scalar(kk, kk, wcol[:, 4 * h + t:4 * h + t + 1], None, ALU.mult).then_inc(s_kw, 1)
                    settle(s_kw)
            dve.wait_ge(s_c0, 16)
            ve.tensor_tensor(prod.rearrange("p (g t) -> p g t", t=DT), qcs.rearrange("p (g t) -> p g t", t=DT),
                             C0[:, :, 128:129].to_broadcast([P, 32, DT]), ALU.mult).then_inc(s_prod, 1)
            settle(s_prod)
            dve.wait_ge(s_sps, 1)
            dve.wait_ge(s_bce, 1)
            colv = small[:, 160:164]
            idh = ident.rearrange("p (h s) -> p h s", h=MH)
            for k, q in enumerate((0, 2, 3, 4)):
                link(ve.tensor_tensor(smt.rearrange("p (h s) -> p h s", h=MH), BC[:, :, q, :], idh, ALU.mult))
                link(ve.reduce_sum(colv[:, k:k + 1], smt, axis=AX))
            ve.tensor_scalar(smt.rearrange("p (h s) -> p h s", h=MH), BC[:, :, 1, :], colv[:, 0:1], 0.0,
                             ALU.add, ALU.min).then_inc(s_sx, 1)
            settle(s_sx)
            dve.wait_ge(s_sxe, 1)
            link(ve.tensor_tensor(smt, smt, C("sblk"), ALU.mult))
            ve.tensor_tensor(SWs, PB[2][:, 0:128], smt, ALU.mult).then_inc(s_sws, 1)
            settle(s_sws)
            ve.tensor_tensor(VB, v1s.unsqueeze(1).to_broadcast([P, 32, 129]),
                             C("hb").unsqueeze(2).to_broadcast([P, 32, 129]), ALU.mult).then_inc(s_vb, 1)
            settle(s_vb)
            dve.wait_ge(s_kts, 1)
            ve.tensor_scalar(kws, PB[4][:, 0:128], colv[:, 3:4], None, ALU.mult).then_inc(s_kse, 1)
            settle(s_kse)
            dve.wait_ge(s_nit, 1)
            link(ve.tensor_scalar(h_s, PB[5][:, 0:128], colv[:, 2:3], None, ALU.mult))
            d = small[:, 164:165]
            link(ve.tensor_scalar(d, PB[2][:, 128:129], colv[:, 2:3], None, ALU.mult))
            dve.wait_ge(s_nin, 1)
            link(ve.tensor_tensor(h_s, h_s, PB[4][:, 0:128], ALU.add))
            link(ve.tensor_tensor(d, d, PB[4][:, 128:129], ALU.add))
            link(ve.scalar_tensor_tensor(d, d, -1.0, d, ALU.mult, ALU.max))
            link(ve.tensor_tensor(d, d, colv[:, 1:2], ALU.max))
            link(ve.reciprocal(d, d))
            link(ve.tensor_scalar(h_s, h_s, d, None, ALU.mult))
            for h in range(MH):
                last = ve.tensor_copy(mix[PT][0:NS, 512 + h * P:512 + (h + 1) * P], h_s[NS * h:NS * h + NS, :])
            link(last)
            ve.tensor_tensor(mix[PT][0:NS, 512:1024], mix[PT][0:NS, 512:1024], zo[0:NS, PT, :], ALU.mult)\
              .then_inc(s_omix, 1)
            settle(s_omix)
            wp = BC[:, :, 5, :].rearrange("p h (b t) -> p h b t", b=DB)[:, :, :, 3]
            for h in range(MH):
                cc = C0[:, h * DB:(h + 1) * DB, :]
                last = ve.tensor_tensor(cc, cc, wp[:, h, :].unsqueeze(2).to_broadcast([P, DB, 129]), ALU.mult)
            link(last)
            C0f = C0.rearrange("p g v -> p (g v)")
            for n in range(11):
                dve.wait_ge(s_cup, n + 1)
                c0, c1 = n * 387, min(32 * 129, (n + 1) * 387)
                ve.tensor_tensor(C0f[:, c0:c1], C0f[:, c0:c1], PB[6 + n % 2][:, 0:c1 - c0], ALU.add)\
                  .then_inc(s_cue, 1)
                settle(s_cue)
            rest_vector(dve, link, settle)

        @block.gpsimd
        def _(pool):
            rest_gpsimd(pool)


INS = ["x", "xT", "consts", "par", "b_if", "m0", "stconv", "C0", "w_in", "kcmp", "vcmp", "kslc", "vslc", "kwin",
       "vwin", "pages", "w1", "w2", "w2pad", "w_out", "ln", "w_pq", "subk", "uv"]
OUTS = {
    "y": (T, D), "p_kc": (SEQ, 128), "p_vc": (SEQ, 128), "p_ks": (SEQ, 128), "p_vs": (SEQ, 128),
    "p_kw": (SEQ, 128), "p_vw": (SEQ, 128), "p_C": (P, MH, 129), "p_m": (MH, 1), "p_conv": (1024, 3),
    "s_kc": (NS, 128), "s_vc": (NS, 128), "s_ks": (NS, 128), "s_vs": (NS, 128),
    "s_kw": (DB, WIN, 128), "s_vw": (DB, WIN, 128), "s_C": (P, 32 * 129), "s_m": (MH, DB), "s_conv": (1024, 24),
}


def kernel(**a):
    import concourse.bacc as bacc
    from concourse.bass_utils import run_bass_kernel_spmd

    a = {k: np.asarray(v) for k, v in a.items()}
    f = {}
    f["x"] = np.concatenate([a["x_prompt"].reshape(SEQ, D), a["x_sample"].reshape(NS, D)])
    def chunks(w, n):
        return w.reshape(n, P, -1).transpose(1, 0, 2).reshape(P, -1)

    f["xT"] = chunks(f["x"].T, KC)
    f["consts"] = const_array()
    cols = [a["conv_w"][0].reshape(4, KC, P).transpose(2, 1, 0).reshape(P, -1),
            a["conv_b"][0].reshape(KC, P).T,
            a["b_phi1"][0].reshape(4, P).T,
            a["pe_cmp"][0].reshape(2 * 16, P).T]
    f["par"] = np.concatenate(cols, axis=1)
    f["b_if"] = np.ascontiguousarray(a["b_if"][0].reshape(2, MH).T)
    f["m0"] = np.ascontiguousarray(a["state_m"][0].T)
    f["stconv"] = np.ascontiguousarray(a["state_conv"][0].reshape(DB * 3, 1024).T)
    f["C0"] = np.concatenate([a["state_C"][0].transpose(2, 1, 0, 3),
                              a["state_n"][0].transpose(2, 1, 0)[..., None]], axis=3).reshape(P, 32 * 129)
    f["w_in"] = np.concatenate([chunks(a["w_in"][0][:, c0:c0 + n], KC) for _, c0, n in GROUPS], axis=1)
    for k in ("k_cmp", "v_cmp"):
        f[k.replace("_", "")] = a["cache_" + k].reshape(POOL * 8, 16, NKV, HD).transpose(0, 2, 1, 3)\
            .reshape(POOL * 8, 2048)
    for k in ("k_slc", "v_slc"):
        f[k.replace("_", "")] = a["cache_" + k].reshape(POOL * 8, 2048)
    f["kwin"] = a["cache_k_win"].reshape(DB, WIN, 128)
    f["vwin"] = a["cache_v_win"].reshape(DB, WIN, 128)
    f["pages"] = np.ascontiguousarray(np.repeat(a["page_table"], 8, axis=1).T)
    f["w1"] = np.stack([chunks(w, 16) for w in a["w_phi1"][0]])
    f["w2"] = a["w_phi2"][0]
    pad = np.zeros((2, 256, 128), np.float32)
    pad[0, :, :HD] = a["w_phi2"][0, 0]
    pad[1, :, HD:] = a["w_phi2"][0, 0]
    f["w2pad"] = pad
    f["w_out"] = np.stack([chunks(a["w_out"][0][:, c:c + 512], KC) for c in range(0, D, 512)])
    f["ln"] = np.concatenate([a["ln_g"][0], a["ln_b"][0]])
    f["w_pq"] = np.stack([chunks(a["w_pq"][0][:, c:c + 512], KC) for c in range(0, 2048, 512)])
    f["subk"] = np.ascontiguousarray(a["sub_keys"][0].reshape(16, NK, P).transpose(2, 0, 1))
    f["uv"] = np.concatenate([a["u_tab"][0], a["v_tab"][0]], axis=1)

    nc = bacc.Bacc("TRN2", target_bir_lowering=False, num_devices=1)
    arrays, i, o = {}, {}, {}
    for name in INS:
        x = np.ascontiguousarray(f[name])
        arrays[f"in_{name}"] = x
        i[name] = nc.dram_tensor(f"in_{name}", x.shape, mybir.dt.from_np(x.dtype), kind="ExternalInput").ap()
    for name, shape in OUTS.items():
        o[name] = nc.dram_tensor(f"out_{name}", shape, F32, kind="ExternalOutput").ap()
    program(nc, i, o)
    r = run_bass_kernel_spmd(nc, [arrays], core_ids=[0]).results[0]
    g = {name: np.asarray(r[f"out_{name}"]) for name in OUTS}

    def kv(name, *lead):
        return g[name].reshape(1, *lead, NKV, HD)

    sC = g["s_C"].reshape(P, MH, DB, 129)
    sconv = g["s_conv"].T.reshape(1, DB, 3, 1024)
    return (g["y"][:SEQ].reshape(1, SEQ, D), g["y"][SEQ:].reshape(DB, DT, D),
            *(kv(n, 1, SEQ) for n in ("p_kc", "p_vc", "p_ks", "p_vs", "p_kw", "p_vw")),
            g["p_C"][:, :, :128].transpose(1, 0, 2)[None, None], g["p_C"][:, :, 128].T[None, None],
            g["p_m"].reshape(1, 1, MH), g["p_conv"].T[None, None],
            *(kv(n, DB, DT) for n in ("s_kc", "s_vc", "s_ks", "s_vs")),
            *(kv(n, DB, WIN) for n in ("s_kw", "s_vw")),
            sC[..., :128].transpose(2, 1, 0, 3)[None], sC[..., 128].transpose(2, 1, 0)[None],
            g["s_m"].T[None], sconv)
```
